# Optimizing a Trainium2 kernel written in Bass

```python
import jax, jax.numpy as jnp
from jax import lax
import numpy as np
import math

D_MODEL = 1024
BATCH = 1
SEQ = 512
DEPTH = 2

D_MIX = D_MODEL
HG_HEADS = 4
HG_DK = 128
HG_DV = 128
HG_W = HG_HEADS * HG_DV
HG_CHUNK = 64
NSA_HEADS = 8
NSA_KV_HEADS = 2
NSA_DH = 64
NSA_G = NSA_HEADS // NSA_KV_HEADS
NSA_W = NSA_HEADS * NSA_DH
KV_W = NSA_KV_HEADS * NSA_DH
CMP_BLOCK = 32
CMP_STRIDE = 16
CMP_HIDDEN = 128
SLC_BLOCK = 64
SLC_TOPK = 16
SLC_Q_BLOCK = 64
WINDOW = 512
Q_BLOCK = 128
FORCE_SCORE = 1e4
ROPE_THETA = 500000.0
ROPE_DIM = NSA_DH // 4
PLE_DIM = 256
RMS_EPS = 1e-6
IN_SPLITS = (HG_W,) * 5 + (NSA_W,) + (KV_W,) * 6 + (3 * NSA_HEADS, NSA_W)
IN_COLS = 5 * HG_W + NSA_W + 6 * KV_W + 3 * NSA_HEADS + NSA_W


def rmsnorm(x, g):
    xf = x.astype(jnp.float32)
    var = jnp.mean(xf * xf, axis=-1, keepdims=True)
    return (xf * lax.rsqrt(var + RMS_EPS)).astype(x.dtype) * g

def masked_softmax(s, mask):
    s = jnp.where(mask, s.astype(jnp.float32), -jnp.inf)
    m = jnp.max(s, axis=-1, keepdims=True)
    m = jnp.where(jnp.isfinite(m), m, 0.0)
    e = jnp.where(mask, jnp.exp(s - m), 0.0)
    return e / jnp.maximum(jnp.sum(e, axis=-1, keepdims=True), 1e-30)

def rope_tables(seq):
    pos = jnp.arange(seq, dtype=jnp.float32)
    inv = ROPE_THETA ** (-jnp.arange(0, ROPE_DIM, 2, dtype=jnp.float32) / ROPE_DIM)
    ang = pos[:, None] * inv[None, :]
    return jnp.cos(ang), jnp.sin(ang)

def partial_rope(x, cos, sin):
    half = ROPE_DIM // 2
    x1, x2, xp = x[..., :half], x[..., half:ROPE_DIM], x[..., ROPE_DIM:]
    c = cos.astype(x.dtype)
    s = sin.astype(x.dtype)
    return jnp.concatenate([x1 * c - x2 * s, x1 * s + x2 * c, xp], axis=-1)

def heads(a, n):
    B, T, W = a.shape
    return a.reshape(B, T, n, W // n).transpose(0, 2, 1, 3)

def hgrn2_chunkwise(q, log_f, k, v):
    B, H, T, DK = q.shape
    DV = v.shape[-1]
    C = HG_CHUNK
    N = T // C

    def to_chunks(a):
        return jnp.moveaxis(a.reshape(B, H, N, C, a.shape[-1]), 2, 0)

    causal = jnp.tril(jnp.ones((C, C), dtype=bool))[:, :, None]

    def step(S, inp):
        qi, lfi, ki, vi = inp
        b = jnp.cumsum(lfi.astype(jnp.float32), axis=-2)
        diff = b[..., :, None, :] - b[..., None, :, :]
        decay = jnp.exp(jnp.where(causal, diff, -jnp.inf))
        A = jnp.einsum('bhtd,bhsd,bhtsd->bhts', qi, ki, decay)
        o = jnp.einsum('bhts,bhsv->bhtv', A, vi) + jnp.einsum('bhtd,bhdv->bhtv', qi * jnp.exp(b), S)
        b_last = b[..., -1:, :]
        S_new = jnp.exp(b_last[..., 0, :])[..., None] * S + jnp.einsum(
            'bhsd,bhsv->bhdv', ki * jnp.exp(b_last - b), vi)
        return S_new, o

    S0 = jnp.zeros((B, H, DK, DV), jnp.float32)
    _, o = lax.scan(step, S0, (to_chunks(q), to_chunks(log_f), to_chunks(k), to_chunks(v)))
    return jnp.moveaxis(o, 0, 2).reshape(B, H, T, DV).astype(v.dtype)

def compress(kv, pe, w1, w2):
    B, G, T, dh = kv.shape
    NC = (T - CMP_BLOCK) // CMP_STRIDE + 1
    idx = jnp.arange(NC)[:, None] * CMP_STRIDE + jnp.arange(CMP_BLOCK)[None, :]
    blocks = kv[:, :, idx, :] + pe
    flat = blocks.reshape(B, G, NC, CMP_BLOCK * dh)
    return jax.nn.silu(flat @ w1) @ w2

def window_attn(q, k, v, scale):
    B, KVH, G, T, dh = q.shape
    NB = T // Q_BLOCK
    NW = WINDOW // Q_BLOCK
    pad = ((0, 0), (0, 0), (WINDOW, 0), (0, 0))
    kb = jnp.pad(k, pad).reshape(B, KVH, NB + NW, Q_BLOCK, dh)
    vb = jnp.pad(v, pad).reshape(B, KVH, NB + NW, Q_BLOCK, dh)
    band_k = jnp.concatenate([kb[:, :, i:i + NB] for i in range(NW + 1)], axis=3)
    band_v = jnp.concatenate([vb[:, :, i:i + NB] for i in range(NW + 1)], axis=3)
    qb = q.reshape(B, KVH, G, NB, Q_BLOCK, dh)
    s = jnp.einsum('bgnxqd,bgxkd->bgnxqk', qb, band_k) * scale
    qpos = jnp.arange(NB)[:, None] * Q_BLOCK + jnp.arange(Q_BLOCK)[None, :]
    kpos = jnp.arange(NB)[:, None] * Q_BLOCK - WINDOW + jnp.arange((NW + 1) * Q_BLOCK)[None, :]
    d = qpos[:, :, None] - kpos[:, None, :]
    mask = (d >= 0) & (d < WINDOW) & (kpos[:, None, :] >= 0)
    p = masked_softmax(s, mask)
    o = jnp.einsum('bgnxqk,bgxkd->bgnxqd', p.astype(v.dtype), band_v)
    return o.reshape(B, KVH, G, T, dh)

def selected_attn(q, k, v, sel, scale):
    B, KVH, G, T, dh = q.shape
    K = sel.shape[-1]
    NB = T // SLC_Q_BLOCK
    qb = jnp.moveaxis(q.reshape(B, KVH, G, NB, SLC_Q_BLOCK, dh), 3, 0)
    sb = jnp.moveaxis(sel.reshape(B, KVH, NB, SLC_Q_BLOCK, K), 2, 0)
    t0 = jnp.arange(NB) * SLC_Q_BLOCK
    bi = jnp.arange(B)[:, None, None, None]
    gi = jnp.arange(KVH)[None, :, None, None]

    def one(args):
        qx, sx, s0 = args
        tok = (sx[..., None] * SLC_BLOCK + jnp.arange(SLC_BLOCK)).reshape(B, KVH, SLC_Q_BLOCK, K * SLC_BLOCK)
        kg = k[bi, gi, tok]
        vg = v[bi, gi, tok]
        s = jnp.einsum('bgnqd,bgqkd->bgnqk', qx, kg) * scale
        qpos = s0 + jnp.arange(SLC_Q_BLOCK)
        mask = (tok <= qpos[:, None])[:, :, None]
        p = masked_softmax(s, mask)
        return jnp.einsum('bgnqk,bgqkd->bgnqd', p.astype(vg.dtype), vg)

    o = lax.map(one, (qb, sb, t0))
    return jnp.moveaxis(o, 0, 3).reshape(B, KVH, G, T, dh)

def first_inputs(seed: int = 0) -> dict:
    key = jax.random.key(seed)
    ks = jax.random.split(key, 16)
    n = jax.random.normal
    f32 = jnp.float32
    return {
        "x": n(ks[0], (BATCH, SEQ, D_MODEL), f32),
        "p": n(ks[1], (DEPTH, BATCH, SEQ, PLE_DIM), f32),
        "norm_g": 1.0 + 0.05 * n(ks[2], (DEPTH, D_MODEL), f32),
        "w_in": n(ks[3], (DEPTH, D_MODEL, IN_COLS), f32) * D_MODEL ** -0.5,
        "hgrn_lb": 0.5 * n(ks[4], (DEPTH, HG_HEADS * HG_DK), f32),
        "hgrn_onorm_g": 1.0 + 0.05 * n(ks[5], (DEPTH, HG_DV), f32),
        "nsa_qnorm_g": 1.0 + 0.05 * n(ks[6], (DEPTH, NSA_DH), f32),
        "nsa_knorm_g": 1.0 + 0.05 * n(ks[7], (DEPTH, 3, NSA_DH), f32),
        "cmp_pe": 0.1 * n(ks[8], (DEPTH, 2, CMP_BLOCK, NSA_DH), f32),
        "cmp_w1": n(ks[9], (DEPTH, 2, CMP_BLOCK * NSA_DH, CMP_HIDDEN), f32) * (CMP_BLOCK * NSA_DH) ** -0.5,
        "cmp_w2": n(ks[10], (DEPTH, 2, CMP_HIDDEN, NSA_DH), f32) * CMP_HIDDEN ** -0.5,
        "w_out": n(ks[11], (DEPTH, D_MIX, D_MODEL), f32) * (0.5 * D_MIX ** -0.5),
        "ple_norm_g": 1.0 + 0.05 * n(ks[12], (DEPTH, D_MODEL), f32),
        "w_pg": n(ks[13], (DEPTH, D_MODEL, D_MODEL), f32) * D_MODEL ** -0.5,
        "w_pp": n(ks[14], (DEPTH, PLE_DIM, D_MODEL), f32) * (0.5 * PLE_DIM ** -0.5),
    }

def first_block(x, p, norm_g, w_in, hgrn_lb, hgrn_onorm_g, nsa_qnorm_g, nsa_knorm_g,
              cmp_pe, cmp_w1, cmp_w2, w_out, ple_norm_g, w_pg, w_pp):
    B, T, _ = x.shape
    KVH, G, dh = NSA_KV_HEADS, NSA_G, NSA_DH
    scale = dh ** -0.5
    split_points = np.cumsum(IN_SPLITS)[:-1].tolist()

    cos, sin = rope_tables(T)
    lb_all = jnp.cumsum(jax.nn.softmax(hgrn_lb.astype(jnp.float32), axis=0), axis=0)
    lb_all = lb_all - lb_all[0]

    NC = (T - CMP_BLOCK) // CMP_STRIDE + 1
    NSB = T // SLC_BLOCK
    top_k = min(SLC_TOPK, NSB)
    c_tok = jnp.arange(NC)[:, None] * CMP_STRIDE + jnp.arange(CMP_BLOCK)[None, :]
    overlap = jnp.mean((c_tok[..., None] // SLC_BLOCK == jnp.arange(NSB)).astype(jnp.float32), axis=1)
    c_end = jnp.arange(NC) * CMP_STRIDE + CMP_BLOCK - 1
    cmp_mask = c_end[None, :] <= jnp.arange(T)[:, None]
    cur = (jnp.arange(T) // SLC_BLOCK)[:, None]
    jb = jnp.arange(NSB)[None, :]
    forced = (jb == 0) | (jb == cur) | (jb == cur - 1)
    eligible = jb <= cur

    h = x
    for i in range(DEPTH):
        xn = rmsnorm(h, norm_g[i])
        proj = xn @ w_in[i]
        (hq, hf, hi, hgo, hz, nq, kcm, vcm, ksl, vsl, kwn, vwn, ngate, nz) = jnp.split(proj, split_points, axis=-1)

        lb = lb_all[i].reshape(HG_HEADS, 1, HG_DK)
        fl = heads(hf, HG_HEADS).astype(jnp.float32)
        log_f = jnp.logaddexp(jnp.log(lb), jnp.log1p(-lb) + jax.nn.log_sigmoid(fl))
        k_hg = (1.0 - lb) * jax.nn.sigmoid(-fl)
        o_hg = hgrn2_chunkwise(heads(hq, HG_HEADS), log_f, k_hg, heads(hi, HG_HEADS))
        o_hg = rmsnorm(o_hg, hgrn_onorm_g[i]).transpose(0, 2, 1, 3).reshape(B, T, HG_W)
        y_hg = o_hg * jax.nn.sigmoid(hgo) * jax.nn.silu(hz)

        qn = rmsnorm(heads(nq, NSA_HEADS), nsa_qnorm_g[i])
        q_nope = qn.reshape(B, KVH, G, T, dh)
        q_rope = partial_rope(qn, cos, sin).reshape(B, KVH, G, T, dh)

        kc = rmsnorm(compress(heads(kcm, KVH), cmp_pe[i, 0], cmp_w1[i, 0], cmp_w2[i, 0]), nsa_knorm_g[i, 0])
        vc = compress(heads(vcm, KVH), cmp_pe[i, 1], cmp_w1[i, 1], cmp_w2[i, 1])
        s_cmp = jnp.einsum('bgntd,bgcd->bgntc', q_nope, kc) * scale
        p_cmp = masked_softmax(s_cmp, cmp_mask)
        o_cmp = jnp.einsum('bgntc,bgcd->bgntd', p_cmp.astype(vc.dtype), vc)

        imp = jnp.einsum('bgntc,cj->bgtj', p_cmp, overlap)
        score = jnp.where(forced, FORCE_SCORE, jnp.where(eligible, imp, -1.0))
        _, sel = lax.top_k(score, top_k)
        k_sl = partial_rope(rmsnorm(heads(ksl, KVH), nsa_knorm_g[i, 1]), cos, sin)
        o_slc = selected_attn(q_rope, k_sl, heads(vsl, KVH), sel, scale)

        k_wn = partial_rope(rmsnorm(heads(kwn, KVH), nsa_knorm_g[i, 2]), cos, sin)
        o_win = window_attn(q_rope, k_wn, heads(vwn, KVH), scale)

        gates = jax.nn.sigmoid(ngate).reshape(B, T, 3, KVH, G).transpose(2, 0, 3, 4, 1)[..., None]
        o_nsa = gates[0] * o_cmp + gates[1] * o_slc + gates[2] * o_win
        o_nsa = o_nsa.reshape(B, NSA_HEADS, T, dh).transpose(0, 2, 1, 3).reshape(B, T, NSA_W)
        y_nsa = o_nsa * jax.nn.silu(nz)

        h = h + jnp.concatenate([y_hg, y_nsa], axis=-1) @ w_out[i]

        gate = jax.nn.sigmoid(rmsnorm(h, ple_norm_g[i]) @ w_pg[i])
        h = h + gate * (p[i] @ w_pp[i])
    return h


N_MIXERS = 3
MEM_LEN = 256
DA_HEADS = 8
DA_HEAD_DIM = 64
DA_QBLOCK = 128
ROPE_THETA_2 = 10000.0
POOL_WINDOWS = (2, 4, 8, 16)
POOL_GROUPS = len(POOL_WINDOWS)
POOL_GROUP_DIM = D_MODEL // POOL_GROUPS
RET_HEADS = 4
RET_QK_DIM = D_MODEL // RET_HEADS
RET_V_DIM = 2 * RET_QK_DIM
RET_CHUNK = 128
XA_HEADS = 4
XA_HEAD_DIM = D_MODEL // XA_HEADS
D_FF = 2816
DEEPNORM_ALPHA = (2 * DEPTH) ** 0.25
DEEPNORM_BETA = (8 * DEPTH) ** -0.25
LN_EPS = 1e-5

N_DA = len(range(0, DEPTH, N_MIXERS))
N_POOL = len(range(1, DEPTH, N_MIXERS))
N_RET = len(range(2, DEPTH, N_MIXERS))


def layer_norm(x, g, b):
    xf = x.astype(jnp.float32)
    mu = jnp.mean(xf, axis=-1, keepdims=True)
    var = jnp.mean(jnp.square(xf - mu), axis=-1, keepdims=True)
    y = (xf - mu) * lax.rsqrt(var + LN_EPS) * g.astype(jnp.float32) + b.astype(jnp.float32)
    return y.astype(x.dtype)

def rope(x, cos, sin):
    half = x.shape[-1] // 2
    xf = x.astype(jnp.float32)
    x1, x2 = xf[..., :half], xf[..., half:]
    return jnp.concatenate([x1 * cos - x2 * sin, x2 * cos + x1 * sin], axis=-1).astype(x.dtype)

def swiglu_ffn(x, w_in, w_out):
    h = x @ w_in
    g, u = jnp.split(h, 2, axis=-1)
    return (jax.nn.silu(g) * u) @ w_out

def diff_attention(x, w_qkv, w_o, lam_q, lam_k, subln_g, cos, sin, lam_init):
    B, S, _ = x.shape
    H, dk = DA_HEADS, DA_HEAD_DIM
    q, k, v = jnp.split(x @ w_qkv, 3, axis=-1)
    q = q.reshape(B, S, H, 2, dk)
    k = k.reshape(B, S, H, 2, dk)
    v = v.reshape(B, S, H, 2 * dk)
    c5, s5 = cos[:, :, None, None, :], sin[:, :, None, None, :]
    q = rope(q, c5, s5)
    k = rope(k, c5, s5)
    lq = lam_q.astype(jnp.float32)
    lk = lam_k.astype(jnp.float32)
    lam = jnp.exp(jnp.sum(lq[0] * lk[0])) - jnp.exp(jnp.sum(lq[1] * lk[1])) + lam_init
    scale = dk ** -0.5
    nb = S // DA_QBLOCK
    qb = q.reshape(B, nb, DA_QBLOCK, H, 2, dk).transpose(1, 0, 2, 3, 4, 5)
    kpos = jnp.arange(S)

    def block(args):
        qblk, i = args
        s = jnp.einsum('bqhcd,bkhcd->bhcqk', qblk, k).astype(jnp.float32) * scale
        qpos = i * DA_QBLOCK + jnp.arange(DA_QBLOCK)
        mask = kpos[None, :] <= qpos[:, None]
        s = jnp.where(mask, s, jnp.finfo(jnp.float32).min)
        p = jax.nn.softmax(s, axis=-1)
        a = p[:, :, 0] - lam * p[:, :, 1]
        return jnp.einsum('bhqk,bkhe->bqhe', a.astype(v.dtype), v)

    o = lax.map(block, (qb, jnp.arange(nb)))
    o = o.transpose(1, 0, 2, 3, 4).reshape(B, S, H, 2 * dk).astype(jnp.float32)
    o = o * lax.rsqrt(jnp.mean(jnp.square(o), axis=-1, keepdims=True) + LN_EPS)
    o = o * subln_g.astype(jnp.float32) * (1.0 - lam_init)
    return o.reshape(B, S, H * 2 * dk).astype(x.dtype) @ w_o

def pool_mixer(x, w_grp, b_grp, scale):
    B, S, D = x.shape
    xg = x.reshape(B, S, POOL_GROUPS, POOL_GROUP_DIM).astype(jnp.float32)
    cs = jnp.cumsum(xg, axis=1)
    t = jnp.arange(S)
    pooled = []
    for g, w in enumerate(POOL_WINDOWS):
        c = cs[:, :, g]
        prev = jnp.pad(c, ((0, 0), (w, 0), (0, 0)))[:, :S]
        cnt = jnp.minimum(t + 1, w).astype(jnp.float32)[None, :, None]
        pooled.append((c - prev) / cnt)
    pooled = jnp.stack(pooled, axis=2) - xg
    y = jnp.einsum('bsgc,gcd->bsgd', pooled.astype(x.dtype), w_grp) + b_grp
    return y.reshape(B, S, D) * scale

def retention(x, w_qkvg, w_o, cos, sin):
    B, S, _ = x.shape
    H, dk, dv, C = RET_HEADS, RET_QK_DIM, RET_V_DIM, RET_CHUNK
    proj = x @ w_qkvg
    q, k, v, g = jnp.split(proj, [H * dk, 2 * H * dk, 2 * H * dk + H * dv], axis=-1)
    c4, s4 = cos[:, :, None, :], sin[:, :, None, :]
    q = rope(q.reshape(B, S, H, dk), c4, s4).astype(jnp.float32)
    k = rope(k.reshape(B, S, H, dk), c4, s4).astype(jnp.float32) * (dk ** -0.5)
    v = v.reshape(B, S, H, dv).astype(jnp.float32)
    log_gamma = jnp.log(1.0 - jnp.exp2(-5.0 - jnp.arange(H, dtype=jnp.float32)))
    idx = jnp.arange(C, dtype=jnp.float32)
    rel = idx[:, None] - idx[None, :]
    d_intra = jnp.where(rel[None] >= 0,
                        jnp.exp(jnp.maximum(rel, 0.0)[None] * log_gamma[:, None, None]), 0.0)
    q_decay = jnp.exp((idx[:, None] + 1.0) * log_gamma[None, :])
    k_decay = jnp.exp((C - 1.0 - idx[:, None]) * log_gamma[None, :])
    chunk_decay = jnp.exp(C * log_gamma)
    nc = S // C

    def to_chunks(a):
        return a.reshape(B, nc, C, H, a.shape[-1]).transpose(1, 0, 2, 3, 4)

    def step(R, inp):
        qc, kc, vc = inp
        att = jnp.einsum('bihd,bjhd->bhij', qc, kc) * d_intra[None]
        inner = jnp.einsum('bhij,bjhe->bihe', att, vc)
        cross = jnp.einsum('bihd,bhde->bihe', qc, R) * q_decay[None, :, :, None]
        R = R * chunk_decay[None, :, None, None] + jnp.einsum(
            'bjhd,bjhe->bhde', kc * k_decay[None, :, :, None], vc)
        return R, inner + cross

    R0 = jnp.zeros((B, H, dk, dv), jnp.float32)
    _, o = lax.scan(step, R0, (to_chunks(q), to_chunks(k), to_chunks(v)))
    o = o.transpose(1, 0, 2, 3, 4).reshape(B, S, H, dv)
    mu = jnp.mean(o, axis=-1, keepdims=True)
    var = jnp.mean(jnp.square(o - mu), axis=-1, keepdims=True)
    o = ((o - mu) * lax.rsqrt(var + LN_EPS)).reshape(B, S, H * dv).astype(x.dtype)
    return (jax.nn.silu(g) * o) @ w_o

def memory_cross_attention(x, mem, wq, wkv, wo):
    B, S, _ = x.shape
    M = mem.shape[1]
    q = (x @ wq).reshape(B, S, XA_HEADS, XA_HEAD_DIM)
    k, v = jnp.split(mem @ wkv, 2, axis=-1)
    k = k.reshape(B, M, XA_HEADS, XA_HEAD_DIM)
    v = v.reshape(B, M, XA_HEADS, XA_HEAD_DIM)
    s = jnp.einsum('bshd,bmhd->bhsm', q, k).astype(jnp.float32) * (XA_HEAD_DIM ** -0.5)
    p = jax.nn.softmax(s, axis=-1).astype(v.dtype)
    o = jnp.einsum('bhsm,bmhd->bshd', p, v).reshape(B, S, D_MODEL)
    return o @ wo

def second_inputs(seed: int = 0) -> dict:
    key = jax.random.key(seed)
    ks = jax.random.split(key, 24)
    f32 = jnp.float32
    D, F = D_MODEL, D_FF
    nrm = lambda k, shape, std: jax.random.normal(k, shape, f32) * std
    x = nrm(ks[0], (BATCH, SEQ, D), 1.0)
    mem = nrm(ks[1], (BATCH, MEM_LEN, D), 1.0)
    offset = jax.random.randint(ks[2], (BATCH, 1), 0, 4096, dtype=jnp.int32)
    positions = (jnp.arange(SEQ, dtype=jnp.int32)[None, :] + offset).astype(jnp.int32)
    ffn_w_in = nrm(ks[3], (DEPTH, 2, D, 2 * F), D ** -0.5)
    ffn_w_out = nrm(ks[4], (DEPTH, 2, F, D), F ** -0.5 * DEEPNORM_BETA)
    ln_g = 1.0 + nrm(ks[5], (DEPTH, 4, D), 0.02)
    ln_b = nrm(ks[6], (DEPTH, 4, D), 0.02)
    da_w_qkv = nrm(ks[7], (N_DA, D, 3 * DA_HEADS * 2 * DA_HEAD_DIM), D ** -0.5)
    da_w_o = nrm(ks[8], (N_DA, DA_HEADS * 2 * DA_HEAD_DIM, D),
                 (DA_HEADS * 2 * DA_HEAD_DIM) ** -0.5 * DEEPNORM_BETA)
    da_lam_q = nrm(ks[9], (N_DA, 2, DA_HEAD_DIM), 0.1)
    da_lam_k = nrm(ks[10], (N_DA, 2, DA_HEAD_DIM), 0.1)
    da_subln_g = 1.0 + nrm(ks[11], (N_DA, 2 * DA_HEAD_DIM), 0.02)
    pool_w = nrm(ks[12], (N_POOL, POOL_GROUPS, POOL_GROUP_DIM, POOL_GROUP_DIM),
                 POOL_GROUP_DIM ** -0.5 * DEEPNORM_BETA)
    pool_b = nrm(ks[13], (N_POOL, POOL_GROUPS, POOL_GROUP_DIM), 0.02)
    pool_scale = 1.0 + nrm(ks[14], (N_POOL, D), 0.02)
    ret_w_qkvg = nrm(ks[15], (N_RET, D, 2 * RET_HEADS * RET_QK_DIM + 2 * RET_HEADS * RET_V_DIM),
                     D ** -0.5)
    ret_w_o = nrm(ks[16], (N_RET, RET_HEADS * RET_V_DIM, D),
                  (RET_HEADS * RET_V_DIM) ** -0.5 * DEEPNORM_BETA)
    xa_wq = nrm(ks[17], (DEPTH, D, D), D ** -0.5)
    xa_wkv = nrm(ks[18], (DEPTH, D, 2 * D), D ** -0.5)
    xa_wo = nrm(ks[19], (DEPTH, D, D), D ** -0.5 * DEEPNORM_BETA)
    return {"x": x, "mem": mem, "positions": positions,
            "ffn_w_in": ffn_w_in, "ffn_w_out": ffn_w_out, "ln_g": ln_g, "ln_b": ln_b,
            "da_w_qkv": da_w_qkv, "da_w_o": da_w_o, "da_lam_q": da_lam_q,
            "da_lam_k": da_lam_k, "da_subln_g": da_subln_g,
            "pool_w": pool_w, "pool_b": pool_b, "pool_scale": pool_scale,
            "ret_w_qkvg": ret_w_qkvg, "ret_w_o": ret_w_o,
            "xa_wq": xa_wq, "xa_wkv": xa_wkv, "xa_wo": xa_wo}

def second_block(x, mem, positions, ffn_w_in, ffn_w_out, ln_g, ln_b,
              da_w_qkv, da_w_o, da_lam_q, da_lam_k, da_subln_g,
              pool_w, pool_b, pool_scale, ret_w_qkvg, ret_w_o,
              xa_wq, xa_wkv, xa_wo):
    pos = positions.astype(jnp.float32)[..., None]
    da_inv = 1.0 / (ROPE_THETA_2 ** (jnp.arange(0, DA_HEAD_DIM, 2, dtype=jnp.float32) / DA_HEAD_DIM))
    da_ang = pos * da_inv[None, None, :]
    da_cos, da_sin = jnp.cos(da_ang), jnp.sin(da_ang)
    ret_inv = 1.0 / (ROPE_THETA_2 ** jnp.linspace(0.0, 1.0, RET_QK_DIM // 2, dtype=jnp.float32))
    ret_ang = pos * ret_inv[None, None, :]
    ret_cos, ret_sin = jnp.cos(ret_ang), jnp.sin(ret_ang)
    a = DEEPNORM_ALPHA
    for i in range(DEPTH):
        m, j = i % N_MIXERS, i // N_MIXERS
        x = layer_norm(a * x + 0.5 * swiglu_ffn(x, ffn_w_in[i, 0], ffn_w_out[i, 0]),
                       ln_g[i, 0], ln_b[i, 0])
        if m == 0:
            lam_init = 0.8 - 0.6 * math.exp(-0.3 * i)
            h = diff_attention(x, da_w_qkv[j], da_w_o[j], da_lam_q[j], da_lam_k[j],
                               da_subln_g[j], da_cos, da_sin, lam_init)
        elif m == 1:
            h = pool_mixer(x, pool_w[j], pool_b[j], pool_scale[j])
        else:
            h = retention(x, ret_w_qkvg[j], ret_w_o[j], ret_cos, ret_sin)
        x = layer_norm(a * x + h, ln_g[i, 1], ln_b[i, 1])
        x = layer_norm(a * x + memory_cross_attention(x, mem, xa_wq[i], xa_wkv[i], xa_wo[i]),
                       ln_g[i, 2], ln_b[i, 2])
        x = layer_norm(a * x + 0.5 * swiglu_ffn(x, ffn_w_in[i, 1], ffn_w_out[i, 1]),
                       ln_g[i, 3], ln_b[i, 3])
    return x


def setup_inputs(seed=0):
    out = dict(first_inputs(seed))
    for name, value in second_inputs(seed + 1).items():
        if name != "x":
            out[name + "_2"] = value
    return out


def reference(
    x, p, norm_g, w_in, hgrn_lb, hgrn_onorm_g, nsa_qnorm_g, nsa_knorm_g, cmp_pe, cmp_w1, cmp_w2,
    w_out, ple_norm_g, w_pg, w_pp, mem_2, positions_2, ffn_w_in_2, ffn_w_out_2, ln_g_2, ln_b_2,
    da_w_qkv_2, da_w_o_2, da_lam_q_2, da_lam_k_2, da_subln_g_2, pool_w_2, pool_b_2,
    pool_scale_2, ret_w_qkvg_2, ret_w_o_2, xa_wq_2, xa_wkv_2, xa_wo_2,
):
    x = first_block(
        x, p, norm_g, w_in, hgrn_lb, hgrn_onorm_g, nsa_qnorm_g, nsa_knorm_g, cmp_pe, cmp_w1,
        cmp_w2, w_out, ple_norm_g, w_pg, w_pp,
    )
    return second_block(
        x, mem_2, positions_2, ffn_w_in_2, ffn_w_out_2, ln_g_2, ln_b_2, da_w_qkv_2, da_w_o_2,
        da_lam_q_2, da_lam_k_2, da_subln_g_2, pool_w_2, pool_b_2, pool_scale_2, ret_w_qkvg_2,
        ret_w_o_2, xa_wq_2, xa_wkv_2, xa_wo_2,
    )


_drawn_inputs = setup_inputs


def setup_inputs(seed=0):
    import zlib

    import numpy as np

    out = dict(_drawn_inputs(seed))
    spreads = {}
    factors = {'norm_g': 2.875,
     'hgrn_onorm_g': 6.525,
     'nsa_qnorm_g': 8.0,
     'nsa_knorm_g': 8.0,
     'cmp_pe': 6.379,
     'ple_norm_g': 7.566,
     'da_lam_k_2': 2.735,
     'da_subln_g_2': 23.909,
     'pool_b_2': 4.067,
     'pool_scale_2': 25.389}
    for name, (base, spread) in spreads.items():
        noise = np.random.default_rng([zlib.crc32(name.encode()), seed]).standard_normal(out[name].shape)
        drawn = base * np.exp(spread * noise) if base else spread * noise
        out[name] = __import__('jax').numpy.asarray(drawn.astype(out[name].dtype))
    for name, factor in factors.items():
        out[name] = (out[name] * factor).astype(out[name].dtype)
    return out
```

```python
from contextlib import ExitStack

import numpy as np

import concourse.bass as bass
from concourse import mybir

P = 128
T = 512
TT = T // P
D = 1024
KC = D // P
DEPTH = 2
NF = 22
MEM = 256
MT = MEM // P
NH = 8
NC = 31
NPROJ = 28
HQ, HF, HGO, HZ, NQ, NZ, KCM, VCM, KSL, KWN = 0, 4, 8, 12, 16, 20, 24, 25, 26, 27
KZ = (HF, HZ)
VG = 280
RING = 4
RMS_EPS = 1e-6
LN_EPS = 1e-5
ALPHA = (2 * DEPTH) ** 0.25
LAM_INIT = 0.2
LA = 7
LEVELS = 10
NEG = -1e30
ROUND = 12582912.0
PI = 3.1415925


def columns(sizes):
    at, col = 0, {}
    for name, n in sizes:
        col[name] = at
        at += n
    return col, at


COL1, NPRM1 = columns([("norm_g", DEPTH * KC), ("ple_g", DEPTH * KC), ("onorm", DEPTH), ("qn", DEPTH),
                       ("kn", DEPTH * 3), ("lb", DEPTH * 4), ("pe", DEPTH * 32), ("w2k", DEPTH * 64),
                       ("w2v", DEPTH * 64)])
COL2, NPRM2 = columns([("ln_g", DEPTH * 4 * KC), ("ln_b", DEPTH * 4 * KC), ("subln", 1), ("pool_b", KC),
                       ("pool_s", KC), ("lam_q", 2), ("lam_k", 2), ("inv", 1), ("cnt", 64)])
NPRM = max(NPRM1, NPRM2)
CC, NCONST = columns([("mean", P), ("ident", P), ("block", P), ("e64", 32), ("e128", 32), ("rot", P)])

COUNTS = {
    "sumsq": dict(sq=KC, s2=KC),
    "rms": dict(stat=1, act_stat=1, var=1, v=KC, xh=KC, xl=KC),
    "ln": dict(stat=1, act_stat=2, var=1, v=KC, xh=KC, xl=KC),
    "split": dict(xh=KC, xl=KC),
    "project": dict(slab=36, prod=22, took=16),
    "compress": dict(cmp_p=5, cmp_a=7, cmp_v=10),
    "hgrn": dict(lvl_v=4 * LEVELS, lvl_p=4 * LEVELS, lvl_a=LA + 12, gst=4, gsq=4, gvar=1, gact=1, grs=1,
                 gbc=4, gused=4, hpv=4),
    "nsa_prep": dict(gst=6, gsq=6, gvar=1, gact=1, grs=1, gbc=6, gused=6, rot=6, roped=6),
    "cmp_att": dict(ca_p=4, ca_v=8, ca_a=9, ca_t=4),
    "nsa": dict(qk=64, ex=64, mx=64, pn=64, tr=64, pt=64, pv=16, oe=4),
    "w_out": dict(slab=8, prod=4, took=4, sq=KC // 2, s2=KC),
    "pg": dict(slab=8, prod=4, took=4, r=KC, sq=KC, s2=KC),
    "ffn_in": dict(slab=2 * NF, prod=NF, took=NF, hh=NF, hv=NF, hl=NF),
    "ffn_out": dict(slab=NF, prod=24, took=4, sq=KC // 2, s2=KC),
    "da_project": dict(slab=24, prod=16, took=10),
    "da_prep": dict(dp_v=3, dp_a=3, dp_p=1),
    "da_rope": dict(rot=16, roped=16),
    "da": dict(qk=64, ex=64, mx=64, pn=32, tr=32, pt=32, pv=8, oe=8),
    "da_norm": dict(gst=8, gsq=8, gvar=1, gact=1, grs=1, gbc=8, gused=8),
    "xa_project": dict(slab=24, prod=16, took=10, msplit=2),
    "xa": dict(qk=16, ex=16, mx=16, pn=16, tr=16, pt=16, pv=4, oe=8),
    "pool": dict(pl=KC, plp=4, r=KC, sq=KC, s2=KC, plt=4),
}


def plan():
    order = [("sumsq", 0, 0)]
    for l in range(DEPTH):
        order += [("rms", l, 0), ("project", l, 0), ("compress", l, 0), ("hgrn", l, 0),
                  ("nsa_prep", l, 0), ("cmp_att", l, 0), ("nsa", l, 0), ("split", l, 0), ("w_out", l, 0),
                  ("rms", l, 1), ("pg", l, 0)]
    order += [("split", 0, 1)]
    for l in range(DEPTH):
        order += [("ffn_in", l, 0), ("ffn_out", l, 0), ("ln", l, 0)]
        if l == 0:
            order += [("da_prep", l, 0), ("da_project", l, 0), ("da_rope", l, 0), ("da", l, 0),
                      ("da_norm", l, 0), ("w_out", l, 1)]
        else:
            order += [("pool", l, 0)]
        order += [("ln", l, 1), ("xa_project", l, 0), ("xa", l, 0), ("split", l, 2), ("w_out", l, 2),
                  ("ln", l, 2), ("ffn_in", l, 1), ("ffn_out", l, 1), ("ln", l, 3)]
    keys = {k for c in COUNTS.values() for k in c}
    now, stages = dict.fromkeys(sorted(keys), 0), []
    for kind, layer, which in order:
        add = dict(COUNTS[kind])
        if kind == "ln" and (layer, which) == (1, 3):
            add["xh"] = add["xl"] = 0
        if kind == "da_norm":
            add["xh"] = add["xl"] = KC
        stages.append(dict(kind=kind, layer=layer, which=which, **now))
        for k, n in add.items():
            now[k] = now.get(k, 0) + n
    return stages, now


class Steps:

    def __init__(self, eng, sem):
        self.eng, self.sem, self.n, self.reg = eng, sem, 0, None

    def __call__(self, ins):
        ins.then_inc(self.sem, 1)
        self.n += 1
        self.eng.wait_ge(self.sem, self.n if self.reg is None else self.reg + self.n)

    def loop(self, trips, per):
        start = self.n
        with self.eng.Fori(0, trips) as i:
            if per:
                self.reg = i * per
            yield i
        assert self.n - start == per, self.n - start
        self.reg = None
        self.n = start + per * trips


def flat(ap):
    return ap.rearrange("p o n -> p (o n)")


def program(nc, x_t, slabs, prm1, prm2, consts, rot2, rope, masks, cmp_tab, spread, causal, w1, pp_w, p_t,
            pool_w, mem_t, positions, out):
    f32, f32r, bf16, i32 = mybir.dt.float32, mybir.dt.float32r, mybir.dt.bfloat16, mybir.dt.int32
    A, F, AX = mybir.AluOpType, mybir.ActivationFunctionType, mybir.AxisListType.X
    stages, total = plan()
    n_slabs = total["slab"]
    assert n_slabs == slabs.shape[0] and n_slabs % 4 == 0, (n_slabs, slabs.shape)

    ctx = ExitStack()
    with ctx:
        def keep(name, shape, dt=f32):
            return ctx.enter_context(nc.sbuf_tensor(name, shape, dt))

        def sem(name):
            return ctx.enter_context(nc.semaphore(name))

        h = keep("h", [P, KC, T])
        raw = keep("raw", [P, RING, D])
        wh = keep("wh", [P, RING, D], f32r)
        wl = keep("wl", [P, RING, D], f32r)
        cst = keep("cst", [P, NCONST])
        prm = keep("prm", [P, NPRM])
        ident_b = keep("ident_b", [P, P], bf16)
        causal_b = keep("causal_b", [P, P], bf16)
        sg = keep("sg", [P, 2, T])
        tb = keep("tb", [P, 2, T])
        sq = keep("sq", [P, 2, T])
        s1 = keep("s1", [P, T])
        s2 = keep("s2", [P, T])
        kc = keep("kc", [P, 2, NC])
        vc = keep("vc", [P, 2, 64])
        small = keep("small", [P, 4, 2, 4])
        ksm = keep("ksm", [P, 3, 64])
        lbt = keep("lbt", [P, 4, 4])
        lam = keep("lam", [P, 4])

        def views(specs):
            made = []
            with ExitStack() as scope:
                for name, shape, dt in specs:
                    made.append(scope.enter_context(nc.sbuf_tensor(name, shape, dt)))
            return made

        with nc.sbuf_tensor("x_room", [P, 2 * KC * T], f32):
            pass
        (kk_k, kk_v, w1v, hidk, hidv) = views([("kk_k", [P, 2, T], f32), ("kk_v", [P, 2, T], f32),
                                               ("w1v", [P, 16, P], f32), ("hidk", [P, 64], f32),
                                               ("hidv", [P, 2, 4, 32], f32)])
        (hk, ad, ax) = views([("hk", [P, 4, T], f32), ("ad", [P, 4, T], f32), ("ax", [P, 4, 768], f32)])
        (pa, ptt, pct, cp) = views([("pa", [P, 2, 1280], f32), ("ptt", [P, 2, TT, T], f32),
                                    ("pct", [P, 2, T], f32), ("cp", [P, NH, 32], f32)])
        xh, xl = keep("xh", [P, KC, T], f32r), keep("xl", [P, KC, T], f32r)
        (proj, vt, vgt, rop, msk, cmt, side, spr) = views([
            ("proj", [P, NPROJ, T], f32), ("vt", [P, TT, T], f32), ("vgt", [P, TT, VG], f32),
            ("rop", [P, 2, T], f32), ("msk", [P, 7 + 1, P], i32), ("cmt", [P, 2, TT, 32], f32),
            ("side", [P, 16, P], f32), ("spr", [16, 6 * P], f32)])
        (dq, dk, dkz, dv, drop, dspr) = views([
            ("dq", [P, KC, T], f32), ("dk", [P, KC, T], f32), ("dkz", [P, 2, KC, T], f32), ("dv", [P, TT, D], f32),
            ("drop", [P, 2, T], f32), ("dspr", [16, 8 * P], f32)])
        (dpos,) = views([("dpos", [P, T], i32)])
        dpa, dpt = pa, ptt
        (xq, xk, xv, xm, mh, ml, xpa, xpt) = views([
            ("xq", [P, KC, T], f32), ("xk", [P, KC, MEM], f32), ("xv", [P, MT, D], f32),
            ("xm", [P, KC, MEM], f32), ("mh", [P, KC, MEM], f32r), ("ml", [P, KC, MEM], f32r),
            ("xpa", [P, 2, TT, MEM], f32), ("xpt", [P, 2, MT, T], f32)])
        (pside, pooled) = views([("pside", [P, 16, P], f32), ("pooled", [P, KC, T], f32)])
        hh, hl = keep("hh", [P, NF, T], f32r), keep("hl", [P, NF, T], f32r)
        pin = vt
        tot_a = proj[:, KCM:KCM + 2, :].rearrange("p a t -> p (a t)").rearrange("p (h t) -> p h t", h=4)
        tot_b = sq[:, 0, :].rearrange("p (h t) -> p h t", h=4)

        bank = [ctx.enter_context(nc.psum_tensor(f"bank{i}", [P, T], f32)) for i in range(8)]

        mean_m = cst[:, CC["mean"]:CC["mean"] + P]
        ident = cst[:, CC["ident"]:CC["ident"] + P]
        block_m = cst[:, CC["block"]:CC["block"] + P]
        rot_m = cst[:, CC["rot"]:CC["rot"] + P]

        def group_m(name, j):
            a = CC[name] + 14 - 2 * j
            return cst[:, a:a + 16]

        def par(col, name, i=0, n=1):
            return prm[:, col[name] + i:col[name] + i + n]

        raw_in = [sem(f"raw_in{i}") for i in range(RING)]
        w_high, w_low = sem("w_high"), sem("w_low")
        prod = sem("prod")
        took_a, took_v = sem("took_a"), sem("took_v")
        loaded, params_in, side_in, block2_in, mem_in = (sem(n) for n in ("loaded", "params_in", "side_in",
                                                                          "block2_in", "mem_in"))
        consts_made, final, stored, w1k_in = sem("consts_made"), sem("final"), sem("stored"), sem("w1k_in")
        S = {k: sem("s_" + k) for k in total if k not in ("slab", "prod", "took")}
        act_steps, dve_steps = sem("act_steps"), sem("dve_steps")
        blk = ctx.enter_context(nc.Block())

        @blk.sync
        def _(sp):
            for ap, src in ((h[:], x_t.rearrange("(c p) t -> p c t", p=P)), (prm[:, 0:NPRM1], prm1),
                            (cst[:], consts), (tb[:, 0, 0:P], causal)):
                sp.dma_start(ap, src).then_inc(loaded, 16)
            for n in range(RING):
                sp.dma_start(raw[:, n, :], slabs[n]).then_inc(raw_in[n], 16)
            for ap, src in ((rop[:], rope), (msk[:], masks), (cmt[:], cmp_tab), (spr[:], spread[:, 0:6 * P]),
                            (side[:], w1[0, 0])):
                sp.dma_start(ap, src).then_inc(params_in, 16)
            with sp.Fori(1, n_slabs // RING) as i:
                for n in range(RING):
                    sp.wait_ge(w_low, i * RING + (n - RING + 1))
                    sp.dma_start(raw[:, n, :],
                                 slabs[bass.ds(i * RING + n, 1)].rearrange("o p c -> (o p) c")
                                 ).then_inc(raw_in[n], 16)
            for c in range(KC):
                sp.wait_ge(final, c + 1)
                sp.dma_start(out[c * P:(c + 1) * P, :], h[:, c, :]).then_inc(stored, 16)
            sp.wait_ge(stored, 16 * KC)

        @blk.gpsimd
        def _(pool):
            with pool.Fori(0, n_slabs // RING) as i:
                for n in range(RING):
                    pool.wait_ge(w_high, i * RING + (n + 1))
                    nc.gpsimd.tensor_tensor(wl[:, n, :], raw[:, n, :], wh[:, n, :], A.subtract).then_inc(w_low, 1)

        @blk.tensor
        def _(pe):
            def passes(dst, high_l, low_l, high_r, low_r, first, last):
                nc.tensor.matmul(dst, high_l, high_r, start=first, stop=False)
                nc.tensor.matmul(dst, high_l, low_r, start=False, stop=False)
                return nc.tensor.matmul(dst, low_l, high_r, start=False, stop=last)

            def tile_of(n, j):
                return wh[:, n % RING, j * P:(j + 1) * P], wl[:, n % RING, j * P:(j + 1) * P]

            def pair(slab, kind, act_h, act_l, w, waits, extra=None):
                for k in range(KC):
                    waits(k)
                    for o in range(2):
                        a, b = tile_of(slab + o, k)
                        last = passes(bank[2 * kind + o][:, 0:w], a, b, act_h[:, k, :], act_l[:, k, :],
                                      k == 0, k == KC - 1)
                return last

            def products(st, slab, ticket, step, pairs, split_base, act_h=xh, act_l=xl, w=T):
                pe.wait_ge(took_a, ticket)
                pe.wait_ge(took_v, ticket)
                if split_base is not None:
                    pe.wait_ge(S["xl"], split_base + 1)

                def two(i):
                    for j in range(2):
                        pe.wait_ge(w_low, i * 4 + (slab + 2 * j + 2))
                        if ticket + j > 0:
                            pe.wait_ge(took_a, i * 2 + (ticket + j - 1))
                            pe.wait_ge(took_v, i * 2 + (ticket + j - 1))

                        def waits(k):
                            if split_base is not None and j == 0:
                                pe.wait_ge(S["xl"], split_base + k + 1)
                        pair(slab + 2 * j, j, act_h, act_l, w, waits).then_inc(prod, 1)
                if pairs == 2:
                    two(0)
                else:
                    with pe.Fori(0, pairs // 2) as i:
                        two(i)

            def token_major(slab, ticket, banks, act_h, act_l, tiles, w, split_base):
                pe.wait_ge(took_a, ticket)
                pe.wait_ge(took_v, ticket)
                for s in range(4):
                    pe.wait_ge(w_low, slab + s + 1)
                    for k in range(2):
                        c = 2 * s + k
                        if split_base is not None:
                            pe.wait_ge(S["xl"], split_base + c + 1)
                        n = (slab + s) % RING
                        b_h, b_l = wh[:, n, k * 512:k * 512 + w], wl[:, n, k * 512:k * 512 + w]
                        for t in range(tiles):
                            ts = slice(t * P, (t + 1) * P)
                            last = passes(bank[banks + t][:, 0:w], act_h[:, c, ts], act_l[:, c, ts], b_h, b_l,
                                          c == 0, c == KC - 1)
                    last.then_inc(prod, 1)

            def rms(st):
                pe.wait_ge(S["s2"], st["s2"])
                if st["kind"] == "ln":
                    nc.tensor.matmul(bank[4][:], mean_m, s1[:], start=True, stop=True)
                nc.tensor.matmul(bank[5][:], mean_m, s2[:], start=True, stop=True).then_inc(S["stat"], 1)

            def project(st):
                token_major(st["slab"], st["took"], 4, xh, xl, TT, T, st["xl"] - KC)
                token_major(st["slab"] + 4, st["took"] + 1, 0, xh, xl, TT, VG, None)
                products(st, st["slab"] + 8, st["took"] + 2, st["prod"] + 8, 14, None)

            def compress(st):
                pe.wait_ge(took_a, st["took"])
                pe.wait_ge(took_v, st["took"])
                for b, (w, kk, sems) in enumerate(((side, kk_k, ((params_in, 80),) if st["layer"] == 0 else ((w1k_in, 16),)),
                                                   (w1v, kk_v, ((side_in, 16 * (1 + 3 * st["layer"])),)))):
                    for s, v in sems:
                        pe.wait_ge(s, v)
                    pe.wait_ge(S["cmp_v"], st["cmp_v"] + 4 * b + 4)
                    for i in range(16):
                        nc.tensor.matmul(bank[b][:, 64:65], w[:, i, :],
                                         par(COL1, "pe", (st["layer"] * 2 + b) * 16 + i), start=(i == 0), stop=(i == 15))
                    for i in range(16):
                        last = nc.tensor.matmul(bank[b][:, 0:2 * NC].rearrange("p (g c) -> p g c", g=2), w[:, i, :],
                                                kk[:, :, 2 * i:2 * i + 16 * (NC - 1) + 1:16],
                                                start=(i == 0), stop=(i == 15))
                    last.then_inc(S["cmp_p"], 1)
                pe.wait_ge(S["cmp_a"], st["cmp_a"] + 2)
                for half in (0, 64):
                    last = nc.tensor.matmul(bank[2][half:half + 64, 0:2 * NC], par(COL1, "w2k", 64 * st["layer"], 64),
                                            hidk[:, 0:2 * NC], start=True, stop=True)
                last.then_inc(S["cmp_p"], 1)
                pe.wait_ge(S["cmp_a"], st["cmp_a"] + 5)
                for g in range(2):
                    last = nc.tensor.matmul(bank[3][:, 64 * g:64 * g + 64],
                                            hidv[:, g, :, :].rearrange("p a c -> p (a c)"),
                                            par(COL1, "w2v", 64 * st["layer"], 64), start=True, stop=True)
                last.then_inc(S["cmp_p"], 1)
                pe.wait_ge(S["cmp_a"], st["cmp_a"] + 6)
                nc.tensor.matmul(bank[4][:, 0:2 * NC], block_m, ksm[:, 0, 0:2 * NC], start=True,
                                 stop=True).then_inc(S["cmp_p"], 1)

            def hgrn(st):
                for lv in range(LEVELS):
                    for hd in range(4):
                        pe.wait_ge(S["lvl_v"], st["lvl_v"] + 4 * lv + hd + 1)
                        q, k, b = proj[:, HQ + hd, :], hk[:, hd, :], bank[hd]
                        if lv < LEVELS - 2:
                            for t in range(TT):
                                ts = slice(t * P, (t + 1) * P)
                                last = nc.tensor.matmul(b[:, ts], k[:, ts], q[:, ts], start=True, stop=True)
                        elif lv == LEVELS - 2:
                            for t in range(2):
                                last = nc.tensor.matmul(b[:, t * P:(t + 1) * P], k[:, 2 * t * P:(2 * t + 1) * P],
                                                        q[:, (2 * t + 1) * P:(2 * t + 2) * P], start=True, stop=True)
                        else:
                            pe.wait_ge(S["lvl_a"], st["lvl_a"] + LA + 2 * hd + 2)
                            for t in range(2):
                                last = nc.tensor.matmul(b[:, 256 * t:256 * t + 256], k[:, t * P:(t + 1) * P],
                                                        q[:, 256:512], start=True, stop=True)
                        last.then_inc(S["lvl_p"], 1)
                for hd in range(4):
                    pe.wait_ge(S["lvl_a"], st["lvl_a"] + LA + 8 + hd + 1)
                    o, at = bank[4 + hd], 0
                    for t in range(TT):
                        v = vt[:, t, hd * P:(hd + 1) * P]
                        last = nc.tensor.matmul(o[:, t * P:(t + 1) * P], v, ad[:, hd, t * P:(t + 1) * P],
                                                start=(t == 0), stop=(t == TT - 1))
                        if t < TT - 1:
                            w = T - (t + 1) * P
                            last = nc.tensor.matmul(o[:, (t + 1) * P:T], v, ax[:, hd, at:at + w],
                                                    start=False, stop=False)
                            at += w
                    last.then_inc(S["hpv"], 1)
                group_stats(st, 4, "e128", spr)

            def group_stats(st, n, name, spread_m):
                for j in range(n):
                    pe.wait_ge(S["gsq"], st["gsq"] + j + 1)
                    nc.tensor.matmul(bank[0][0:16, :], group_m(name, j), sq[:, j % 2, :], start=(j == 0),
                                     stop=(j == n - 1)).then_inc(S["gst"], 1)
                pe.wait_ge(S["grs"], st["grs"] + 1)
                for j in range(n):
                    if j >= 2:
                        pe.wait_ge(S["gused"], st["gused"] + j - 1)
                    nc.tensor.matmul(bank[2 + j % 2][:], spread_m[:, j * P:(j + 1) * P], s1[0:16, :],
                                     start=True, stop=True).then_inc(S["gbc"], 1)

            def rotate(st, chunks, sem_name, base, b0):
                for j, ap in enumerate(chunks):
                    if sem_name:
                        pe.wait_ge(S[sem_name], base + j + 1)
                    if j >= 2:
                        pe.wait_ge(S["roped"], st["roped"] + j - 1)
                    nc.tensor.matmul(bank[b0 + j % 2][:], rot_m, ap, start=True, stop=True).then_inc(S["rot"], 1)

            def nsa_prep(st):
                pe.wait_ge(S["gused"], st["gused"])
                group_stats(st, 6, "e64", spr)
                rotate(st, [proj[:, NQ + j, :] for j in range(4)] + [proj[:, KSL, :], proj[:, KWN, :]],
                       "gused", st["gused"], 6)

            def cmp_att(st):
                pe.wait_ge(S["roped"], st["roped"])
                pe.wait_ge(S["cmp_v"], st["cmp_v"])
                for t in range(TT):
                    if t >= 2:
                        pe.wait_ge(S["ca_v"], st["ca_v"] + 2 * (t - 2) + 1)
                    for hd in range(NH):
                        r = slice(64 * (hd % 2), 64 * (hd % 2) + 64)
                        b = bank[4 * (hd % 2) + t % 2]
                        last = nc.tensor.matmul(b[:, 32 * (hd // 2):32 * (hd // 2) + NC],
                                                proj[r, NQ + hd // 2, t * P:(t + 1) * P], kc[r, hd // 4, :],
                                                start=True, stop=True)
                    last.then_inc(S["ca_p"], 1)
                for t in range(TT):
                    pe.wait_ge(S["ca_v"], st["ca_v"] + 2 * t + 2)
                    if t >= 2:
                        pe.wait_ge(S["ca_a"], st["ca_a"] + 2 * t - 1)
                    for g in range(2):
                        last = nc.tensor.transpose(bank[2 + t % 2][:, g * P:(g + 1) * P],
                                                   cp[:, 4 * g:4 * g + 4, :].rearrange("p a c -> p (a c)"), ident)
                    last.then_inc(S["ca_t"], 1)

            def transposes(st, unit, src, dst_tiles, tokens=TT):
                for t in range(TT):
                    g = 4 * unit + t
                    pe.wait_ge(S["pn"], st["pn"] + g + 1)
                    if g >= 2:
                        pe.wait_ge(S["pt"], st["pt"] + g - 1)
                    for k in range(dst_tiles(t)):
                        last = nc.tensor.transpose(bank[4 + t % 2][:, k * P:(k + 1) * P], src(t, k), ident)
                    last.then_inc(S["tr"], 1)

            def scores(st, unit, q, k):
                for t in range(TT):
                    if unit:
                        pe.wait_ge(S["ex"], st["ex"] + 4 * (unit - 1) + t + 1)
                    w = (t + 1) * P
                    nc.tensor.matmul(bank[t][:, 0:w], q[:, t * P:w], k[:, 0:w], start=True, stop=False)
                    nc.tensor.matmul(bank[t][:, t * P:w], ident_b[:], causal_b[:], start=False,
                                     stop=True).then_inc(S["qk"], 1)

            def causal_cols(buf, t, k):
                at = P * (t * (t + 1) // 2)
                return buf[:, at + k * P:at + (k + 1) * P]

            def nsa(st):
                pe.wait_ge(S["ca_a"], st["ca_a"])
                pe.wait_ge(S["ca_v"], st["ca_v"])

                def score_unit(u):
                    hd, br = u // 2, u % 2
                    scores(st, u, proj[:, HQ + hd // 2, :], proj[:, KZ[br] + 2 * (hd // 4) + hd % 2, :])

                score_unit(0)
                for u in range(2 * NH):
                    hd, br = u // 2, u % 2
                    if u + 1 < 2 * NH:
                        score_unit(u + 1)
                    transposes(st, u, lambda t, k: causal_cols(pa[:, u % 2, :], t, k), lambda t: t + 1)
                    o = bank[6 + (hd // 2) % 2][64 * (hd % 2):64 * (hd % 2) + 64, :]
                    if br == 0:
                        if hd % 2 == 0 and hd >= 4:
                            pe.wait_ge(S["oe"], st["oe"] + hd // 2 - 1)
                        r = slice(32 * (hd % 4), 32 * (hd % 4) + 32)
                        nc.tensor.matmul(o, vc[r, hd // 4, :], pct[r, hd // 4, :], start=True, stop=False)
                    pe.wait_ge(S["pt"], st["pt"] + 4 * u + 4)
                    for k in range(TT):
                        col = 128 * br + 64 * (hd // 4)
                        last = nc.tensor.matmul(o[:, k * P:T], vgt[:, k, col:col + 64], ptt[:, u % 2, k, k * P:T],
                                                start=False, stop=(br == 1 and k == TT - 1))
                    last.then_inc(S["pv"], 1)

            def w_out(st):
                products(st, st["slab"], st["took"], st["prod"], 4, st["xl"] - KC)

            def pg(st):
                pe.wait_ge(took_a, st["took"])
                pe.wait_ge(took_v, st["took"])
                pe.wait_ge(side_in, 16 * (3 + 3 * st["layer"]))
                for j in range(4):
                    pe.wait_ge(w_low, st["slab"] + 2 * j + 2)
                    if j >= 2:
                        pe.wait_ge(took_v, st["took"] + j - 1)
                        pe.wait_ge(took_a, st["took"] + j - 1)

                    def waits(k):
                        if j == 0:
                            pe.wait_ge(S["xl"], st["xl"] - KC + k + 1)
                    pair(st["slab"] + 2 * j, j % 2, xh, xl, T, waits)
                    for o in range(2):
                        for k in range(2):
                            last = nc.tensor.matmul(bank[4 + 2 * (j % 2) + o][:], side[:, 2 * (2 * j + o) + k, :],
                                                    pin[:, k, :], start=(k == 0), stop=(k == 1))
                    last.then_inc(prod, 1)

            def ffn_in(st):
                products(st, st["slab"], st["took"], st["prod"], NF, st["xl"] - KC)

            def ffn_out(st):
                pe.wait_ge(took_a, st["took"])
                pe.wait_ge(took_v, st["took"])

                def one(slab, k_h, k_l, first):
                    for o in range(KC):
                        a, b = tile_of(slab, o)
                        last = passes(bank[o][:], a, b, k_h, k_l, first, False)
                    last.then_inc(prod, 1)
                for k in range(4):
                    pe.wait_ge(w_low, st["slab"] + k + 1)
                    pe.wait_ge(S["hl"], st["hl"] - NF + k + 1)
                    one(st["slab"] + k, hh[:, k, :], hl[:, k, :], k == 0)
                with pe.Fori(1, 5) as i:
                    for n in range(4):
                        pe.wait_ge(w_low, i * 4 + (st["slab"] + n + 1))
                        pe.wait_ge(S["hl"], i * 4 + (st["hl"] - NF + n + 1))
                        one(st["slab"] + n, flat(hh[:, bass.ds(i * 4 + n, 1), :]), flat(hl[:, bass.ds(i * 4 + n, 1), :]),
                            False)
                pe.wait_ge(w_low, st["slab"] + NF)
                pe.wait_ge(S["hl"], st["hl"])
                for o in range(KC):
                    for k in (NF - 2, NF - 1):
                        a, b = tile_of(st["slab"] + k, o)
                        last = passes(bank[o][:], a, b, hh[:, k, :], hl[:, k, :], False, k == NF - 1)
                    if o % 2:
                        last.then_inc(prod, 1)

            def da_prep(st):
                pe.wait_ge(S["dp_v"], st["dp_v"] + 1)
                nc.tensor.matmul(bank[4][:, 0:2], mean_m, lam[:, 0:2], start=True, stop=True).then_inc(S["dp_p"], 1)

            def da_project(st):
                products(st, st["slab"], st["took"], st["prod"], 8, st["xl"] - KC)
                for half in range(2):
                    token_major(st["slab"] + 16 + 4 * half, st["took"] + 8 + half, 4 - 4 * half, xh, xl, TT, T, None)

            def da_rope(st):
                pe.wait_ge(took_a, st["took"])
                pe.wait_ge(took_v, st["took"])
                rotate(st, [dq[:, j, :] for j in range(KC)] + [dk[:, j, :] for j in range(KC)], None, 0, 0)

            def da(st):
                pe.wait_ge(S["roped"], st["roped"])

                def score_unit(u):
                    hd, c = u // 2, u % 2
                    scores(st, u, dq[:, hd, :], dkz[:, c, hd, :])
                for hd in range(NH):
                    score_unit(2 * hd)
                    if hd:
                        values(hd - 1, st)
                    score_unit(2 * hd + 1)
                values(NH - 1, st)

            def values(hd, st):
                transposes(st, hd, lambda t, k: causal_cols(dpa[:, 1, :], t, k), lambda t: t + 1)
                pe.wait_ge(S["pt"], st["pt"] + 4 * hd + 4)
                if hd >= 2:
                    pe.wait_ge(S["oe"], st["oe"] + hd - 1)
                for k in range(TT):
                    last = nc.tensor.matmul(bank[6 + hd % 2][:, k * P:T], dv[:, k, hd * P:(hd + 1) * P],
                                            dpt[:, hd % 2, k, k * P:T], start=(k == 0), stop=(k == TT - 1))
                last.then_inc(S["pv"], 1)

            def xa_project(st):
                products(st, st["slab"], st["took"], st["prod"], 4, st["xl"] - KC)
                pe.wait_ge(S["msplit"], st["msplit"] + 2)
                products(st, st["slab"] + 8, st["took"] + 4, st["prod"] + 4, 4, None, mh, ml, MEM)
                for half in range(2):
                    token_major(st["slab"] + 16 + 4 * half, st["took"] + 8 + half, 4 * (1 - half), mh, ml, MT, T, None)

            def xa(st):
                pe.wait_ge(took_a, st["took"])
                pe.wait_ge(took_v, st["took"])

                def score_unit(hd):
                    for t in range(TT):
                        if hd:
                            pe.wait_ge(S["ex"], st["ex"] + 4 * (hd - 1) + t + 1)
                        for k in range(2):
                            last = nc.tensor.matmul(bank[t][:, 0:MEM], xq[:, 2 * hd + k, t * P:(t + 1) * P],
                                                    xk[:, 2 * hd + k, :], start=(k == 0), stop=(k == 1))
                        last.then_inc(S["qk"], 1)
                score_unit(0)
                for hd in range(4):
                    if hd < 3:
                        score_unit(hd + 1)
                    transposes(st, hd, lambda t, k: xpa[:, hd % 2, t, k * P:(k + 1) * P], lambda t: MT)
                    pe.wait_ge(S["pt"], st["pt"] + 4 * hd + 4)
                    if hd:
                        pe.wait_ge(S["oe"], st["oe"] + 2 * hd)
                    for c in range(2):
                        for k in range(MT):
                            last = nc.tensor.matmul(bank[6 + c][:], xv[:, k, hd * 256 + c * P:hd * 256 + (c + 1) * P],
                                                    xpt[:, hd % 2, k, :], start=(k == 0), stop=(k == 1))
                    last.then_inc(S["pv"], 1)

            def pool_mix(st):
                pe.wait_ge(side_in, 16 * 8)
                pe.wait_ge(S["xl"], st["xl"])
                for g in range(4):
                    pe.wait_ge(S["pl"], st["pl"] + 2 * g + 2)
                    if g >= 2:
                        pe.wait_ge(S["plt"], st["plt"] + g - 1)
                    for o in range(2):
                        for k in range(2):
                            last = nc.tensor.matmul(bank[2 * (g % 2) + o][:], pside[:, 4 * g + 2 * o + k, :],
                                                    pooled[:, 2 * g + k, :], start=(k == 0), stop=(k == 1))
                    last.then_inc(S["plp"], 1)

            pe.wait_ge(consts_made, 3)
            does = dict(rms=rms, ln=rms, project=project, compress=compress, hgrn=hgrn, nsa_prep=nsa_prep,
                        cmp_att=cmp_att, nsa=nsa, w_out=w_out, pg=pg, ffn_in=ffn_in, ffn_out=ffn_out,
                        da_prep=da_prep, da_project=da_project, da_rope=da_rope, da=da, xa_project=xa_project,
                        xa=xa, pool=pool_mix,
                        da_norm=lambda st: (pe.wait_ge(S["oe"], st["oe"]), group_stats(st, NH, "e128", dspr)))
            for st in stages:
                if st["kind"] in does:
                    does[st["kind"]](st)

        @blk.scalar
        def _(act):
            step = Steps(act, act_steps)
            copy = nc.scalar.copy

            def high(n, slab=None):
                if isinstance(n, int):
                    if n >= n_slabs:
                        return
                    act.wait_ge(raw_in[n % RING], 16 * (n // RING + 1))
                    slot = n % RING
                else:
                    i, at = n
                    act.wait_ge(raw_in[at % RING], i * 16 + 16 * (at // RING + 1))
                    slot = at % RING
                nc.scalar.copy(wh[:, slot, :], raw[:, slot, :]).then_inc(w_high, 1)

            def squares(st, c):
                act.wait_ge(S["r"], st["r"] + c + 1)
                if c >= 2:
                    act.wait_ge(S["s2"], st["s2"] + c - 1)
                nc.scalar.activation(sq[:, c % 2, :], h[:, c, :], F.Square).then_inc(S["sq"], 1)

            def sumsq(st):
                for c in range(KC):
                    if c >= 2:
                        act.wait_ge(S["s2"], st["s2"] + c - 1)
                    nc.scalar.activation(sq[:, c % 2, :], h[:, c, :], F.Square).then_inc(S["sq"], 1)

            def pair_squares(st, j):
                act.wait_ge(took_v, st["took"] + j + 1)
                for c in (2 * j, 2 * j + 1):
                    if c >= 2:
                        act.wait_ge(S["s2"], st["s2"] + c - 1)
                    nc.scalar.activation(sq[:, c % 2, :], h[:, c, :], F.Square
                                         ).then_inc(took_a if c % 2 else S["sq"], 1)

            def norm(st):
                last_one = st["kind"] == "ln" and (st["layer"], st["which"]) == (1, 3)
                act.wait_ge(S["stat"], st["stat"] + 1)
                if st["kind"] == "ln":
                    nc.scalar.activation(sg[:, 0, :], bank[4][:], F.Square).then_inc(S["act_stat"], 1)
                act.wait_ge(S["var"], st["var"] + 1)
                nc.scalar.activation(sq[:, 1, :], sq[:, 0, :], F.Abs_reciprocal_sqrt).then_inc(S["act_stat"], 1)
                for c in range(KC):
                    act.wait_ge(S["v"], st["v"] + c + 1)
                    v = tb[:, c % 2, :]
                    if st["kind"] == "rms":
                        nc.scalar.copy(xh[:, c, :], v).then_inc(S["xh"], 1)
                    else:
                        b = par(COL2, "ln_b", (st["layer"] * 4 + st["which"]) * KC + c)
                        if last_one:
                            nc.scalar.activation(h[:, c, :], v, F.Identity, bias=b).then_inc(final, 1)
                        else:
                            step(nc.scalar.activation(h[:, c, :], v, F.Identity, bias=b))
                            nc.scalar.copy(xh[:, c, :], h[:, c, :]).then_inc(S["xh"], 1)

            def split_of(st, chunk):
                for c in range(KC):
                    nc.scalar.copy(xh[:, c, :], chunk(c)).then_inc(S["xh"], 1)

            def split(st):
                if st["which"] == 0:
                    act.wait_ge(S["oe"], st["oe"])
                    act.wait_ge(S["pv"], st["pv"])
                    split_of(st, lambda c: proj[:, (HGO if c < 4 else NZ - 4) + c, :])
                elif st["which"] == 1:
                    act.wait_ge(S["r"], st["r"])
                    split_of(st, lambda c: h[:, c, :])
                else:
                    act.wait_ge(S["oe"], st["oe"])
                    split_of(st, lambda c: xq[:, c, :])

            def copy_pairs(st, slab, ticket, step0, pairs, dst, w=T):
                def two(i):
                    for j in range(2):
                        act.wait_ge(prod, i * 2 + (step0 + j + 1))
                        high((i, slab + 2 * j + RING))
                        high((i, slab + 2 * j + RING + 1))
                        nc.scalar.copy(flat(dst[:, bass.ds(i * 4 + 2 * j, 1), :]), bank[2 * j][:, 0:w]
                                       ).then_inc(took_a, 1)
                with act.Fori(0, pairs // 2) as i:
                    two(i)

            def copy_tiles(slab, step0, banks, tiles, dst, w):
                for s in range(4):
                    act.wait_ge(prod, step0 + s + 1)
                    high(slab + s + RING)
                for t in range(0, tiles, 2):
                    last = nc.scalar.copy(dst[:, t, 0:w], bank[banks + t][:, 0:w])
                    if t + 2 < tiles:
                        step(last)
                last.then_inc(took_a, 1)

            def project(st):
                copy_tiles(st["slab"], st["prod"], 4, TT, vt[:], T)
                copy_tiles(st["slab"] + 4, st["prod"] + 4, 0, TT, vgt[:], VG)
                copy_pairs(st, st["slab"] + 8, st["took"] + 2, st["prod"] + 8, 14, proj)
                act.dma_start(w1v[:], w1[st["layer"], 1]).then_inc(side_in, 16)

            def compress(st):
                act.wait_ge(S["cmp_p"], st["cmp_p"] + 1)
                nc.scalar.copy(ksm[:, 1, 0:1], bank[0][:, 64:65]).then_inc(S["cmp_a"], 1)
                act.wait_ge(S["cmp_a"], st["cmp_a"] + 1)
                nc.scalar.activation(hidk[:, 0:2 * NC], bank[0][:, 0:2 * NC], F.Silu, bias=ksm[:, 1, 0:1]
                                     ).then_inc(S["cmp_a"], 1)
                act.wait_ge(S["cmp_p"], st["cmp_p"] + 2)
                nc.scalar.copy(ksm[:, 1, 1:2], bank[1][:, 64:65]).then_inc(S["cmp_a"], 1)
                act.wait_ge(S["cmp_a"], st["cmp_a"] + 3)
                act.wait_ge(S["cmp_v"], st["cmp_v"] + 8)
                for g in range(2):
                    nc.scalar.activation(hidv[:, g, :, 0:NC],
                                         bank[1][:, NC * g:NC * g + NC].rearrange("p (o c) -> p o c", o=1)
                                         .broadcast_to([P, 4, NC]), F.Silu, bias=ksm[:, 1, 1:2]
                                         ).then_inc(S["cmp_a"], 1)
                act.wait_ge(S["cmp_p"], st["cmp_p"] + 3)
                nc.scalar.activation(ksm[:, 0, 0:2 * NC], bank[2][:, 0:2 * NC], F.Square).then_inc(S["cmp_a"], 1)
                act.wait_ge(S["cmp_v"], st["cmp_v"] + 9)
                nc.scalar.activation(ksm[:, 2, 0:2 * NC], ksm[:, 1, 0:2 * NC], F.Abs_reciprocal_sqrt
                                     ).then_inc(S["cmp_a"], 1)

            def group_rstd(st):
                act.wait_ge(S["gvar"], st["gvar"] + 1)
                nc.scalar.activation(sg[0:16, 0, :], s2[0:16, :], F.Abs_reciprocal_sqrt).then_inc(S["gact"], 1)

            def group_squares(st, chunks):
                for j, ap in enumerate(chunks):
                    if j >= 2:
                        act.wait_ge(S["gst"], st["gst"] + j - 1)
                    nc.scalar.activation(sq[:, j % 2, :], ap, F.Square).then_inc(S["gsq"], 1)

            def hgrn(st):
                act.wait_ge(S["cmp_v"], st["cmp_v"])
                nc.scalar.activation(lbt[:, 0, :], lbt[:, 2, :], F.Sigmoid).then_inc(S["lvl_a"], 1)
                nc.scalar.activation(lbt[:, 1, :], lbt[:, 2, :], F.Sigmoid, scale=-1.0).then_inc(S["lvl_a"], 1)
                nc.scalar.activation(hk[:], proj[:, HF:HF + 4, :], F.Sigmoid, scale=-1.0).then_inc(S["lvl_a"], 1)
                nc.scalar.activation(proj[:, HF:HF + 4, :], proj[:, HF:HF + 4, :], F.Sigmoid).then_inc(S["lvl_a"], 1)
                nc.scalar.activation(proj[:, HGO:HGO + 4, :], proj[:, HGO:HGO + 4, :], F.Sigmoid
                                     ).then_inc(S["lvl_a"], 1)
                nc.scalar.activation(proj[:, HZ:HZ + 4, :], proj[:, HZ:HZ + 4, :], F.Silu).then_inc(S["lvl_a"], 1)
                nc.scalar.activation(proj[:, NZ:NZ + 4, :], proj[:, NZ:NZ + 4, :], F.Silu).then_inc(S["lvl_a"], 1)
                act.dma_start(side[:], pp_w[st["layer"]]).then_inc(side_in, 16)
                for hd in range(4):
                    act.wait_ge(S["lvl_p"], st["lvl_p"] + 4 * (LEVELS - 2) + hd + 1)
                    nc.scalar.copy(ax[:, hd, 0:P], bank[hd][:, 0:P]).then_inc(S["lvl_a"], 1)
                    nc.scalar.copy(ax[:, hd, 640:768], bank[hd][:, P:2 * P]).then_inc(S["lvl_a"], 1)
                for hd in range(4):
                    act.wait_ge(S["lvl_p"], st["lvl_p"] + 4 * (LEVELS - 1) + hd + 1)
                    nc.scalar.copy(ax[:, hd, P:640], bank[hd][:]).then_inc(S["lvl_a"], 1)
                for hd in range(4):
                    act.wait_ge(S["hpv"], st["hpv"] + hd + 1)
                    if hd >= 2:
                        act.wait_ge(S["gst"], st["gst"] + hd - 1)
                    nc.scalar.activation(sq[:, hd % 2, :], bank[4 + hd][:], F.Square).then_inc(S["gsq"], 1)
                act.dma_start(pin[:, 0:2, :], p_t[st["layer"]]).then_inc(side_in, 16)
                group_rstd(st)

            def nsa_prep(st):
                act.wait_ge(S["gused"], st["gused"])
                group_squares(st, [proj[:, NQ + j, :] for j in range(4)] + [proj[:, KSL, :], proj[:, KWN, :]])
                group_rstd(st)

            def cmp_att(st):
                nc.scalar.activation(vgt[:, :, 256:280], vgt[:, :, 256:280], F.Sigmoid).then_inc(S["ca_a"], 1)
                for t in range(TT):
                    act.wait_ge(S["ca_v"], st["ca_v"] + 2 * t + 1)
                    nc.scalar.activation(sg[:, 0, 0:256].rearrange("p (h c) -> p h c", h=NH)[:, :, 0:NC],
                                         sg[:, 0, 0:256].rearrange("p (h c) -> p h c", h=NH)[:, :, 0:NC],
                                         F.Exp, scale=0.125).then_inc(S["ca_a"], 1)
                    act.wait_ge(S["ca_t"], st["ca_t"] + t + 1)
                    nc.scalar.copy(pct[:, :, t * P:(t + 1) * P],
                                   bank[2 + t % 2][:, 0:256].rearrange("p (g t) -> p g t", g=2)
                                   ).then_inc(S["ca_a"], 1)

            def exp(st, unit, t, scale, buf, w):
                act.wait_ge(S["mx"], st["mx"] + 4 * unit + t + 1)
                nc.scalar.activation(buf, bank[t][:, 0:w], F.Exp, bias=small[:, 1, unit % 2, t:t + 1],
                                     scale=scale, accum_out=small[:, 2, unit % 2, t:t + 1]).then_inc(S["ex"], 1)

            def transposed(st, unit, t, dst, k):
                act.wait_ge(S["tr"], st["tr"] + 4 * unit + t + 1)
                nc.scalar.copy(dst, bank[4 + t % 2][:, 0:k * P].rearrange("p (k t) -> p k t", k=k)
                               ).then_inc(S["pt"], 1)

            def causal_buf(buf, t):
                at = P * (t * (t + 1) // 2)
                return buf[:, at:at + (t + 1) * P]

            def nsa(st):
                def one(u, t):
                    exp(st, u, t, 0.125, causal_buf(pa[:, u % 2, :], t), (t + 1) * P)
                for t in range(TT):
                    one(0, t)
                for u in range(2 * NH):
                    if 1 <= u < 2 * NH - 1:
                        act.wait_ge(S["tr"], st["tr"] + 4 * (u - 1) + 4)
                    if u >= 2:
                        act.wait_ge(S["pv"], st["pv"] + u - 1)
                    for t in range(TT):
                        if u + 1 < 2 * NH:
                            one(u + 1, t)
                        transposed(st, u, t, ptt[:, u % 2, 0:t + 1, t * P:(t + 1) * P], t + 1)

            def w_out(st):
                for j in range(4):
                    act.wait_ge(prod, st["prod"] + j + 1)
                    high(st["slab"] + 2 * j + RING)
                    high(st["slab"] + 2 * j + RING + 1)
                    pair_squares(st, j)

            def pg(st):
                for j in range(4):
                    act.wait_ge(prod, st["prod"] + j + 1)
                    high(st["slab"] + 2 * j + RING)
                    high(st["slab"] + 2 * j + RING + 1)
                    if j:
                        act.wait_ge(took_v, st["took"] + j)
                    step(nc.scalar.activation(sg[:, 0, :], bank[2 * (j % 2)][:], F.Sigmoid))
                    nc.scalar.activation(sg[:, 1, :], bank[2 * (j % 2) + 1][:], F.Sigmoid).then_inc(took_a, 1)
                    squares(st, 2 * j)
                    squares(st, 2 * j + 1)
                if st["layer"] == 0:
                    act.dma_start(side[:], w1[1, 0]).then_inc(w1k_in, 16)
                else:
                    act.dma_start(prm[:, 0:NPRM2], prm2).then_inc(side_in, 16)

            def ffn_in(st):
                def two(i):
                    for j in range(2):
                        act.wait_ge(prod, i * 2 + (st["prod"] + j + 1))
                        nc.scalar.activation(sg[:, j, :], bank[2 * j][:], F.Silu).then_inc(took_a, 1)
                        high((i, st["slab"] + 2 * j + RING))
                        high((i, st["slab"] + 2 * j + RING + 1))
                        act.wait_ge(took_v, i * 2 + (st["took"] + j + 1))
                        nc.scalar.copy(flat(hh[:, bass.ds(i * 2 + j, 1), :]), tb[:, j, :]).then_inc(S["hh"], 1)
                with act.Fori(0, NF // 2) as i:
                    two(i)

            def ffn_out(st):
                with act.Fori(0, 4) as i:
                    for n in range(4):
                        act.wait_ge(prod, i * 4 + (st["prod"] + n + 1))
                        high((i, st["slab"] + n + RING))
                for k in range(16, 20):
                    act.wait_ge(prod, st["prod"] + k + 1)
                    high(st["slab"] + k + RING)
                for j in range(4):
                    act.wait_ge(prod, st["prod"] + 20 + j + 1)
                    pair_squares(st, j)
                high(st["slab"] + NF - 2 + RING)
                high(st["slab"] + NF - 1 + RING)

            def da_prep(st):
                act.dma_start(dspr[:], spread).then_inc(block2_in, 16)
                act.dma_start(rot_m, rot2).then_inc(block2_in, 16)
                act.dma_start(dpos[:], positions.broadcast_to([P, T])).then_inc(block2_in, 16)
                act.wait_ge(S["dp_v"], st["dp_v"] + 2)
                nc.scalar.activation(drop[:, 1, :], tb[:, 0, :], F.Sin).then_inc(S["dp_a"], 1)
                act.wait_ge(S["dp_v"], st["dp_v"] + 3)
                nc.scalar.activation(drop[:, 0, :], tb[:, 1, :], F.Sin).then_inc(S["dp_a"], 1)
                act.wait_ge(S["dp_p"], st["dp_p"] + 1)
                nc.scalar.activation(lam[:, 0:2], bank[4][:, 0:2], F.Exp, scale=float(D)).then_inc(S["dp_a"], 1)

            def da_project(st):
                copy_pairs(st, st["slab"], st["took"], st["prod"], 4, dq)
                copy_pairs(st, st["slab"] + 8, st["took"] + 4, st["prod"] + 4, 4, dk)
                for half in range(2):
                    copy_tiles(st["slab"] + 16 + 4 * half, st["prod"] + 8 + 4 * half, 4 - 4 * half, TT,
                               dv[:, :, 512 * half:512 * half + 512], T)

            def da(st):
                def one(u, t):
                    exp(st, u, t, 0.125, causal_buf(dpa[:, u % 2, :], t), (t + 1) * P)

                def turn(hd, t):
                    transposed(st, hd, t, dpt[:, hd % 2, 0:t + 1, t * P:(t + 1) * P], t + 1)
                for hd in range(NH):
                    if hd:
                        act.wait_ge(S["pn"], st["pn"] + 4 * hd)
                    if hd >= 3:
                        act.wait_ge(S["pv"], st["pv"] + hd - 2)
                    for t in range(TT):
                        one(2 * hd, t)
                        if hd:
                            turn(hd - 1, t)
                    for t in range(TT):
                        one(2 * hd + 1, t)
                for t in range(TT):
                    turn(NH - 1, t)

            def da_norm(st):
                act.wait_ge(S["oe"], st["oe"])
                group_squares(st, [dq[:, j, :] for j in range(NH)])
                group_rstd(st)
                for c in range(KC):
                    act.wait_ge(S["gused"], st["gused"] + c + 1)
                    nc.scalar.copy(xh[:, c, :], dq[:, c, :]).then_inc(S["xh"], 1)

            def xa_project(st):
                act.wait_ge(mem_in, 16 * (st["layer"] + 1))
                nc.scalar.copy(mh[:], xm[:]).then_inc(S["msplit"], 1)
                copy_pairs(st, st["slab"], st["took"], st["prod"], 4, xq)
                copy_pairs(st, st["slab"] + 8, st["took"] + 4, st["prod"] + 4, 4, xk, MEM)
                for half in range(2):
                    copy_tiles(st["slab"] + 16 + 4 * half, st["prod"] + 8 + 4 * half, 4 * (1 - half), MT,
                               xv[:, :, 512 * half:512 * half + 512], T)

            def xa(st):
                def one(u, t):
                    exp(st, u, t, 1.0 / 16, xpa[:, u % 2, t, :], MEM)
                for t in range(TT):
                    one(0, t)
                for u in range(4):
                    if 1 <= u < 3:
                        act.wait_ge(S["tr"], st["tr"] + 4 * (u - 1) + 4)
                    if u >= 2:
                        act.wait_ge(S["pv"], st["pv"] + u - 1)
                    for t in range(TT):
                        if u + 1 < 4:
                            one(u + 1, t)
                        transposed(st, u, t, xpt[:, u % 2, :, t * P:(t + 1) * P], MT)

            def pool_mix(st):
                act.dma_start(pside[:], pool_w).then_inc(side_in, 16)
                for c in range(KC):
                    squares(st, c)

            act.wait_ge(loaded, 16 * 4)
            for n in range(RING):
                high(n)
            act.wait_ge(consts_made, 3)
            does = dict(sumsq=sumsq, rms=norm, ln=norm, split=split, project=project, compress=compress, hgrn=hgrn,
                        nsa_prep=nsa_prep, cmp_att=cmp_att, nsa=nsa, w_out=w_out, pg=pg, ffn_in=ffn_in,
                        ffn_out=ffn_out, da_prep=da_prep, da_project=da_project, da=da, da_norm=da_norm,
                        xa_project=xa_project, xa=xa, pool=pool_mix)
            for st in stages:
                if st["kind"] in does:
                    if st["kind"] == "ln" and st["which"] == 1:
                        act.wait_ge(S["s2"], st["s2"])
                        act.dma_start(xm[:], mem_t).then_inc(mem_in, 16)
                    does[st["kind"]](st)

        @blk.vector
        def _(dve):
            step = Steps(dve, dve_steps)
            V = nc.vector

            def cat(ap, n):
                return ap.rearrange("p (m o) -> p m o", o=1).broadcast_to([P, ap.shape[1], n])

            def newton(y, var, tmp, dst):
                step(V.scalar_tensor_tensor(out=tmp, in0=y, scalar=-0.5, in1=y, op0=A.mult, op1=A.mult))
                step(V.tensor_tensor(tmp, tmp, var, A.mult))
                return V.scalar_tensor_tensor(out=dst, in0=tmp, scalar=1.5, in1=y, op0=A.add, op1=A.mult)

            def clear_sums(ln):
                step(V.memset(s2[:], 0.0))
                if ln:
                    step(V.memset(s1[:], 0.0))

            def add_squares(st, c, sem_, value):
                dve.wait_ge(sem_, value)
                V.tensor_tensor(s2[:], s2[:], sq[:, c % 2, :], A.add).then_inc(S["s2"], 1)
                dve.wait_ge(S["s2"], st["s2"] + c + 1)

            def sumsq(st):
                clear_sums(False)
                for c in range(KC):
                    add_squares(st, c, S["sq"], st["sq"] + c + 1)

            def lower(st, c, src):
                dve.wait_ge(S["xh"], st["xh"] + c + 1)
                V.tensor_tensor(xl[:, c, :], src, xh[:, c, :], A.subtract).then_inc(S["xl"], 1)
                dve.wait_ge(S["xl"], st["xl"] + c + 1)

            def norm(st):
                ln = st["kind"] == "ln"
                last_one = ln and (st["layer"], st["which"]) == (1, 3)
                var, y = sq[:, 0, :], sq[:, 1, :]
                dve.wait_ge(S["stat"], st["stat"] + 1)
                if ln:
                    if (st["layer"], st["which"]) == (0, 0):
                        dve.wait_ge(side_in, 16 * 7)
                    eps = LN_EPS * (4 if st["which"] in (0, 3) else 1)
                    dve.wait_ge(S["act_stat"], st["act_stat"] + 1)
                    step(V.tensor_tensor(var, bank[5][:], sg[:, 0, :], A.subtract))
                    V.tensor_scalar(var, var, 0.0, eps, A.max, A.add).then_inc(S["var"], 1)
                    step(V.tensor_copy(s1[:], bank[4][:]))
                    dve.wait_ge(S["act_stat"], st["act_stat"] + 2)
                else:
                    V.tensor_scalar(var, bank[5][:], RMS_EPS, None, A.add).then_inc(S["var"], 1)
                    dve.wait_ge(S["act_stat"], st["act_stat"] + 1)
                dve.wait_ge(S["var"], st["var"] + 1)
                step(newton(y, var, sg[:, 1, :], s2[:]))
                for c in range(KC):
                    if ln:
                        g = par(COL2, "ln_g", (st["layer"] * 4 + st["which"]) * KC + c)
                        step(V.tensor_tensor(sg[:, c % 2, :], h[:, c, :], s1[:], A.subtract))
                        if last_one and c >= 2:
                            dve.wait_ge(final, c - 1)
                        src = sg[:, c % 2, :]
                    else:
                        g = par(COL1, "norm_g" if st["which"] == 0 else "ple_g", st["layer"] * KC + c)
                        src = h[:, c, :]
                    V.scalar_tensor_tensor(out=tb[:, c % 2, :], in0=src, scalar=g, in1=s2[:], op0=A.mult,
                                           op1=A.mult).then_inc(S["v"], 1)
                    if c and not last_one:
                        lower(st, c - 1, h[:, c - 1, :] if ln else tb[:, (c - 1) % 2, :])
                if not last_one:
                    lower(st, KC - 1, h[:, KC - 1, :] if ln else tb[:, (KC - 1) % 2, :])

            def split(st):
                for c in range(KC):
                    lower(st, c, (proj[:, (HGO if c < 4 else NZ - 4) + c, :], h[:, c, :], xq[:, c, :])[st["which"]])

            def copy_pairs(step0, pairs, dst, w=T):
                with dve.Fori(0, pairs // 2) as i:
                    for j in range(2):
                        dve.wait_ge(prod, i * 2 + (step0 + j + 1))
                        V.tensor_copy(flat(dst[:, bass.ds(i * 4 + 2 * j + 1, 1), :]), bank[2 * j + 1][:, 0:w]
                                      ).then_inc(took_v, 1)

            def copy_tiles(step0, banks, tiles, dst, w):
                dve.wait_ge(prod, step0 + 4)
                for t in range(1, tiles, 2):
                    last = V.tensor_copy(dst[:, t, 0:w], bank[banks + t][:, 0:w])
                    if t + 2 < tiles:
                        step(last)
                last.then_inc(took_v, 1)

            def project(st):
                copy_tiles(st["prod"], 4, TT, vt[:], T)
                copy_tiles(st["prod"] + 4, 0, TT, vgt[:], VG)
                copy_pairs(st["prod"] + 8, 14, proj)

            def compress(st):
                dve.wait_ge(took_a, st["took"])
                dve.wait_ge(took_v, st["took"])
                step(V.memset(hidv[:], 0.0))
                for chunk, kk in ((KCM, kk_k), (VCM, kk_v)):
                    for g in range(2):
                        src = proj[64 * g:64 * g + 64, chunk, :]
                        V.tensor_copy(kk[0:64, g, :], src).then_inc(S["cmp_v"], 1)
                        V.tensor_copy(kk[64:P, g, 0:T - 1], src[:, 1:T]).then_inc(S["cmp_v"], 1)
                n = 2 * NC
                dve.wait_ge(S["cmp_p"], st["cmp_p"] + 4)
                step(V.tensor_copy(vc[:].rearrange("p g d -> p (g d)"), bank[3][:, 0:P]))
                dve.wait_ge(S["cmp_p"], st["cmp_p"] + 5)
                V.tensor_scalar(ksm[:, 1, 0:n], bank[4][:, 0:n], RMS_EPS, None, A.add).then_inc(S["cmp_v"], 1)
                dve.wait_ge(S["cmp_v"], st["cmp_v"] + 9)
                dve.wait_ge(S["cmp_a"], st["cmp_a"] + 7)
                step(newton(ksm[:, 2, 0:n], ksm[:, 1, 0:n], ksm[:, 0, 0:n], ksm[:, 0, 0:n]))
                V.scalar_tensor_tensor(out=kc[:].rearrange("p g c -> p (g c)"), in0=bank[2][:, 0:n],
                                       scalar=par(COL1, "kn", st["layer"] * 3), in1=ksm[:, 0, 0:n], op0=A.mult,
                                       op1=A.mult).then_inc(S["cmp_v"], 1)

            def group_rstd(st, n, eps):
                dve.wait_ge(S["gst"], st["gst"] + n)
                V.tensor_scalar(s2[0:16, :], bank[0][0:16, :], eps, None, A.add).then_inc(S["gvar"], 1)
                dve.wait_ge(S["gvar"], st["gvar"] + 1)
                dve.wait_ge(S["gact"], st["gact"] + 1)
                newton(sg[0:16, 0, :], s2[0:16, :], sg[0:16, 1, :], s1[0:16, :]).then_inc(S["grs"], 1)

            def hgrn(st):
                dve.wait_ge(S["lvl_a"], st["lvl_a"] + LA)
                for lv in range(LEVELS):
                    for hd in range(4):
                        q, k, f = proj[:, HQ + hd, :], hk[:, hd, :], proj[:, HF + hd, :]
                        if lv == 0:
                            if st["layer"]:
                                step(V.tensor_scalar(f, f, lbt[:, 1, hd:hd + 1], lbt[:, 0, hd:hd + 1], A.mult, A.add))
                                step(V.tensor_scalar(k, k, lbt[:, 1, hd:hd + 1], None, A.mult))
                            V.memset(ad[:, hd, :], 0.0).then_inc(S["lvl_v"], 1)
                            continue
                        dve.wait_ge(S["lvl_v"], st["lvl_v"] + 4 * (lv - 1) + hd + 1)
                        dve.wait_ge(S["lvl_p"], st["lvl_p"] + 4 * (lv - 1) + hd + 1)
                        if lv - 1 < LEVELS - 2:
                            step(V.copy_predicated(ad[:, hd, :].rearrange("p (t s) -> p t s", t=TT),
                                                   msk[:, lv - 1, :].rearrange("p (o s) -> p o s", o=1)
                                                   .broadcast_to([P, TT, P]),
                                                   bank[hd][:].rearrange("p (t s) -> p t s", t=TT)))
                        if lv == 1:
                            V.tensor_tensor(q, q, f, A.mult).then_inc(S["lvl_v"], 1)
                            continue
                        m = 2 ** (lv - 2)
                        nb = T // (2 * m)
                        tot = f if m == 1 else (tot_a if lv % 2 else tot_b)[:, hd, 0:2 * nb]
                        new = (tot_b if lv % 2 else tot_a)[:, hd, 0:nb]
                        even, odd = tot[:, 0:2 * nb:2], tot[:, 1:2 * nb:2]
                        qv = q.rearrange("p (b two m) -> p b two m", two=2, m=m)[:, :, 1, :]
                        kv = k.rearrange("p (b two m) -> p b two m", two=2, m=m)[:, :, 0, :]
                        step(V.tensor_tensor(qv, qv, cat(even, m), A.mult))
                        if lv < LEVELS - 1:
                            step(V.tensor_tensor(new, even, odd, A.mult))
                        V.tensor_tensor(kv, kv, cat(odd, m), A.mult).then_inc(S["lvl_v"], 1)
                group_rstd(st, 4, RMS_EPS)
                for hd in range(4):
                    dve.wait_ge(S["gbc"], st["gbc"] + hd + 1)
                    y = tb[:, hd % 2, :]
                    step(V.scalar_tensor_tensor(out=y, in0=bank[4 + hd][:], scalar=par(COL1, "onorm", st["layer"]),
                                                in1=proj[:, HGO + hd, :], op0=A.mult, op1=A.mult))
                    step(V.tensor_tensor(y, y, bank[2 + hd % 2][:], A.mult))
                    V.tensor_tensor(proj[:, HGO + hd, :], y, proj[:, HZ + hd, :], A.mult).then_inc(S["gused"], 1)

            def rope(st, j, x, table, outs):
                step(V.tensor_tensor(tb[:, 0, :], x, table[:, 0, :], A.mult))
                dve.wait_ge(S["rot"], st["rot"] + j + 1)
                return outs

            def nsa_prep(st):
                dve.wait_ge(S["gused"], st["gused"])
                group_rstd(st, 6, RMS_EPS)
                chunks = [NQ + j for j in range(4)] + [KSL, KWN]
                for j, c in enumerate(chunks):
                    dve.wait_ge(S["gbc"], st["gbc"] + j + 1)
                    g = par(COL1, "qn", st["layer"]) if j < 4 else par(COL1, "kn", st["layer"] * 3 + j - 3)
                    V.scalar_tensor_tensor(out=proj[:, c, :], in0=proj[:, c, :], scalar=g, in1=bank[2 + j % 2][:],
                                           op0=A.mult, op1=A.mult).then_inc(S["gused"], 1)
                dve.wait_ge(S["gused"], st["gused"] + 6)
                for z in KZ:
                    for half in range(2):
                        step(V.memset(proj[64 - 64 * half:P - 64 * half, z + half:z + 4:2, :], 0.0))
                for j, c in enumerate(chunks):
                    step(V.tensor_tensor(tb[:, 0, :], proj[:, c, :], rop[:, 0, :], A.mult))
                    dve.wait_ge(S["rot"], st["rot"] + j + 1)
                    step(V.tensor_tensor(tb[:, 1, :], bank[6 + j % 2][:], rop[:, 1, :], A.mult))
                    if j < 4:
                        V.tensor_tensor(proj[:, HQ + j, :], tb[:, 0, :], tb[:, 1, :], A.add).then_inc(S["roped"], 1)
                        dve.wait_ge(S["roped"], st["roped"] + j + 1)
                        continue
                    for g in range(2):
                        src = slice(64 * g, 64 * g + 64)
                        for half in range(2):
                            last = V.tensor_tensor(proj[64 * half:64 * half + 64, KZ[j - 4] + 2 * g + half, :],
                                                   tb[src, 0, :], tb[src, 1, :], A.add)
                            if g + half < 2:
                                step(last)
                    last.then_inc(S["roped"], 1)
                    dve.wait_ge(S["roped"], st["roped"] + j + 1)

            def cmp_att(st):
                s = sg[:, 0, 0:256].rearrange("p (h c) -> p h c", h=NH)[:, :, 0:NC]
                mx, den = ksm[:, 0, 0:NH], ksm[:, 0, 8:8 + NH]

                def heads(ap):
                    return ap.rearrange("p (o c) -> p o c", o=1).broadcast_to([P, NH, NC])
                step(V.memset(cp[:], 0.0))
                for t in range(TT):
                    dve.wait_ge(S["ca_p"], st["ca_p"] + t + 1)
                    for o in range(2):
                        step(V.tensor_tensor(s[:, o:NH:2, :],
                                             bank[4 * o + t % 2][:, 0:P].rearrange("p (h c) -> p h c", h=4)[:, :, 0:NC],
                                             heads(cmt[:, 1, t, 0:NC])[:, 0:4, :], A.add))
                    step(V.tensor_reduce(mx, s, AX, A.max))
                    V.tensor_tensor(s, s, cat(mx, NC), A.subtract).then_inc(S["ca_v"], 1)
                    dve.wait_ge(S["ca_a"], st["ca_a"] + 2 * t + 2)
                    step(V.tensor_tensor(s, s, heads(cmt[:, 0, t, 0:NC]), A.mult))
                    step(V.tensor_reduce(den, s, AX, A.add))
                    step(V.tensor_scalar(den, den, 1e-30, None, A.max))
                    step(V.reciprocal(den, den))
                    step(V.tensor_tensor(den, den, vgt[:, t, 256:264], A.mult))
                    if t:
                        dve.wait_ge(S["ca_t"], st["ca_t"] + t)
                    V.tensor_tensor(cp[:, :, 0:NC], s, cat(den, NC), A.mult).then_inc(S["ca_v"], 1)
                    dve.wait_ge(S["ca_v"], st["ca_v"] + 2 * t + 2)

            def maxima(st, u, scale, w):
                for t in range(TT):
                    dve.wait_ge(S["qk"], st["qk"] + 4 * u + t + 1)
                    step(V.tensor_reduce(small[:, 0, u % 2, t:t + 1], bank[t][:, 0:w(t)], AX, A.max))
                    V.tensor_scalar(small[:, 1, u % 2, t:t + 1], small[:, 0, u % 2, t:t + 1], -scale, None, A.mult
                                    ).then_inc(S["mx"], 1)

            def causal_buf(buf, t):
                at = P * (t * (t + 1) // 2)
                return buf[:, at:at + (t + 1) * P]

            def nsa(st):
                def out_pair(j):
                    dve.wait_ge(S["pv"], st["pv"] + 4 * j + 4)
                    V.tensor_tensor(proj[:, NZ + j, :], bank[6 + j % 2][:], proj[:, NZ + j, :], A.mult
                                    ).then_inc(S["oe"], 1)
                for u in range(2 * NH):
                    hd, br = u // 2, u % 2
                    maxima(st, u, 0.125, lambda t: (t + 1) * P)
                    dve.wait_ge(S["ex"], st["ex"] + 4 * u + 4)
                    rw = small[:, 3, u % 2, :]
                    step(V.reciprocal(rw, small[:, 2, u % 2, :]))
                    step(V.tensor_tensor(rw, rw, vgt[:, :, 264 + 8 * br + hd:265 + 8 * br + hd]
                                         .rearrange("p t o -> p (t o)"), A.mult))
                    for t in range(TT):
                        b = causal_buf(pa[:, u % 2, :], t)
                        V.tensor_scalar(b, b, rw[:, t:t + 1], None, A.mult).then_inc(S["pn"], 1)
                    if u >= 5 and (u - 5) % 4 == 0:
                        out_pair((u - 5) // 4)
                out_pair(3)

            def residual(st, j, a, banks, ln):
                for o in range(2):
                    c = 2 * j + o
                    ins = V.scalar_tensor_tensor(out=h[:, c, :], in0=h[:, c, :], scalar=a, in1=bank[banks + o][:],
                                                 op0=A.mult, op1=A.add)
                    if o:
                        ins.then_inc(took_v, 1)
                        dve.wait_ge(took_v, st["took"] + j + 1)
                    else:
                        step(ins)
                if ln:
                    for o in range(2):
                        step(V.tensor_tensor(s1[:], s1[:], h[:, 2 * j + o, :], A.add))
                add_squares(st, 2 * j, S["sq"], st["sq"] + j + 1)
                add_squares(st, 2 * j + 1, took_a, st["took"] + j + 1)

            def w_out(st):
                ln = st["which"] > 0
                clear_sums(ln)
                for j in range(4):
                    dve.wait_ge(prod, st["prod"] + j + 1)
                    residual(st, j, ALPHA if ln else 1.0, 2 * (j % 2), ln)

            def ffn_out(st):
                clear_sums(True)
                for j in range(4):
                    dve.wait_ge(prod, st["prod"] + 20 + j + 1)
                    residual(st, j, 2 * ALPHA, 2 * j, True)

            def pg(st):
                clear_sums(False)
                for j in range(4):
                    dve.wait_ge(took_a, st["took"] + j + 1)
                    step(V.tensor_tensor(tb[:, 0, :], sg[:, 0, :], bank[4 + 2 * (j % 2)][:], A.mult))
                    V.tensor_tensor(tb[:, 1, :], sg[:, 1, :], bank[5 + 2 * (j % 2)][:], A.mult).then_inc(took_v, 1)
                    dve.wait_ge(took_v, st["took"] + j + 1)
                    for o in range(2):
                        c = 2 * j + o
                        V.tensor_tensor(h[:, c, :], h[:, c, :], tb[:, o, :], A.add).then_inc(S["r"], 1)
                    for o in range(2):
                        add_squares(st, 2 * j + o, S["sq"], st["sq"] + 2 * j + o + 1)

            def ffn_in(st):
                with dve.Fori(0, NF // 2) as i:
                    for j in range(2):
                        dve.wait_ge(took_a, i * 2 + (st["took"] + j + 1))
                        V.tensor_tensor(tb[:, j, :], sg[:, j, :], bank[2 * j + 1][:], A.mult).then_inc(took_v, 1)
                        dve.wait_ge(S["hh"], i * 2 + (st["hh"] + j + 1))
                        V.tensor_tensor(flat(hl[:, bass.ds(i * 2 + j, 1), :]), tb[:, j, :],
                                        flat(hh[:, bass.ds(i * 2 + j, 1), :]), A.subtract).then_inc(S["hl"], 1)

            def da_prep(st):
                V.tensor_tensor(lam[:, 0:2], par(COL2, "lam_q", 0, 2), par(COL2, "lam_k", 0, 2), A.mult
                                ).then_inc(S["dp_v"], 1)
                step(V.tensor_scalar(par(COL2, "subln"), par(COL2, "subln"), 1.0 - LAM_INIT, None, A.mult))
                dve.wait_ge(block2_in, 16 * 3)
                ang, k, r = sg[:, 0, :], sg[:, 1, :], tb[:, 0, :]
                step(V.tensor_copy(ang, dpos[:]))
                step(V.tensor_scalar(ang, ang, par(COL2, "inv"), None, A.mult))
                step(V.tensor_scalar(k, ang, float(1 / (2 * np.pi)), None, A.mult))
                step(V.tensor_scalar(k, k, ROUND, None, A.add))
                step(V.tensor_scalar(k, k, ROUND, None, A.subtract))
                parts = (6.28125, 0.0019340515136718750, 2 * np.pi - 6.28125 - 0.0019340515136718750)
                src = ang
                for p in parts:
                    step(V.scalar_tensor_tensor(out=r, in0=k, scalar=-float(p), in1=src, op0=A.mult, op1=A.add))
                    src = r
                r2 = tb[:, 1, :]
                step(V.tensor_scalar(r2, r, float(np.pi / 2), None, A.add))
                step(V.tensor_scalar(k, r2, float(np.pi), None, A.is_gt))
                step(V.scalar_tensor_tensor(out=r2, in0=k, scalar=-float(2 * np.pi), in1=r2, op0=A.mult, op1=A.add))
                V.tensor_scalar(r, r, PI, -PI, A.min, A.max).then_inc(S["dp_v"], 1)
                V.tensor_scalar(r2, r2, PI, -PI, A.min, A.max).then_inc(S["dp_v"], 1)
                dve.wait_ge(S["dp_a"], st["dp_a"] + 3)
                step(V.tensor_tensor(lam[:, 2:3], lam[:, 1:2], lam[:, 0:1], A.subtract))
                step(V.tensor_scalar(lam[:, 2:3], lam[:, 2:3], LAM_INIT, None, A.subtract))

            def da_project(st):
                copy_pairs(st["prod"], 4, dq)
                copy_pairs(st["prod"] + 4, 4, dk)
                for half in range(2):
                    copy_tiles(st["prod"] + 8 + 4 * half, 4 - 4 * half, TT, dv[:, :, 512 * half:512 * half + 512], T)

            def da_rope(st):
                dve.wait_ge(took_a, st["took"])
                dve.wait_ge(took_v, st["took"])
                step(V.memset(dkz[64:P, 0, :, :], 0.0))
                step(V.memset(dkz[0:64, 1, :, :], 0.0))
                for j in range(2 * KC):
                    x = (dq if j < KC else dk)[:, j % KC, :]
                    step(V.tensor_tensor(tb[:, 0, :], x, drop[:, 0, :], A.mult))
                    dve.wait_ge(S["rot"], st["rot"] + j + 1)
                    step(V.tensor_tensor(tb[:, 1, :], bank[j % 2][:], drop[:, 1, :], A.mult))
                    if j < KC:
                        V.tensor_tensor(x, tb[:, 0, :], tb[:, 1, :], A.add).then_inc(S["roped"], 1)
                    else:
                        step(V.tensor_tensor(dkz[0:64, 0, j - KC, :], tb[0:64, 0, :], tb[0:64, 1, :], A.add))
                        V.tensor_tensor(dkz[64:P, 1, j - KC, :], tb[64:P, 0, :], tb[64:P, 1, :], A.add
                                        ).then_inc(S["roped"], 1)
                    dve.wait_ge(S["roped"], st["roped"] + j + 1)

            def da(st):
                def out_head(hd):
                    dve.wait_ge(S["pv"], st["pv"] + hd + 1)
                    V.tensor_copy(dq[:, hd, :], bank[6 + hd % 2][:]).then_inc(S["oe"], 1)
                for hd in range(NH):
                    maxima(st, 2 * hd, 0.125, lambda t: (t + 1) * P)
                    dve.wait_ge(S["ex"], st["ex"] + 8 * hd + 4)
                    step(V.reciprocal(small[:, 3, 0, :], small[:, 2, 0, :]))
                    for t in range(TT):
                        p0 = causal_buf(dpa[:, 0, :], t)
                        step(V.tensor_scalar(p0, p0, small[:, 3, 0, t:t + 1], None, A.mult))
                    maxima(st, 2 * hd + 1, 0.125, lambda t: (t + 1) * P)
                    if hd:
                        out_head(hd - 1)
                    dve.wait_ge(S["ex"], st["ex"] + 8 * hd + 8)
                    step(V.reciprocal(small[:, 3, 1, :], small[:, 2, 1, :]))
                    step(V.tensor_scalar(small[:, 3, 1, :], small[:, 3, 1, :], lam[:, 2:3], None, A.mult))
                    for t in range(TT):
                        p0, p1 = causal_buf(dpa[:, 0, :], t), causal_buf(dpa[:, 1, :], t)
                        V.scalar_tensor_tensor(out=p1, in0=p1, scalar=small[:, 3, 1, t:t + 1], in1=p0, op0=A.mult,
                                               op1=A.add).then_inc(S["pn"], 1)
                out_head(NH - 1)

            def da_norm(st):
                dve.wait_ge(S["oe"], st["oe"])
                group_rstd(st, NH, LN_EPS)
                for j in range(NH):
                    dve.wait_ge(S["gbc"], st["gbc"] + j + 1)
                    V.scalar_tensor_tensor(out=dq[:, j, :], in0=dq[:, j, :], scalar=par(COL2, "subln"),
                                           in1=bank[2 + j % 2][:], op0=A.mult, op1=A.mult).then_inc(S["gused"], 1)
                    if j:
                        lower(st, j - 1, dq[:, j - 1, :])
                lower(st, NH - 1, dq[:, NH - 1, :])

            def xa_project(st):
                dve.wait_ge(S["msplit"], st["msplit"] + 1)
                V.tensor_tensor(ml[:], xm[:], mh[:], A.subtract).then_inc(S["msplit"], 1)
                copy_pairs(st["prod"], 4, xq)
                copy_pairs(st["prod"] + 4, 4, xk, MEM)
                for half in range(2):
                    copy_tiles(st["prod"] + 8 + 4 * half, 4 * (1 - half), MT, xv[:, :, 512 * half:512 * half + 512], T)

            def xa(st):
                def out_head(hd):
                    dve.wait_ge(S["pv"], st["pv"] + hd + 1)
                    for c in range(2):
                        V.tensor_copy(xq[:, 2 * hd + c, :], bank[6 + c][:]).then_inc(S["oe"], 1)
                for u in range(4):
                    maxima(st, u, 1.0 / 16, lambda t: MEM)
                    dve.wait_ge(S["ex"], st["ex"] + 4 * u + 4)
                    rw = small[:, 3, u % 2, :]
                    step(V.reciprocal(rw, small[:, 2, u % 2, :]))
                    for t in range(TT):
                        b = xpa[:, u % 2, t, :]
                        V.tensor_scalar(b, b, rw[:, t:t + 1], None, A.mult).then_inc(S["pn"], 1)
                    if u:
                        out_head(u - 1)
                out_head(3)

            def pool_mix(st):
                clear_sums(True)
                for c in range(KC):
                    g = c // 2
                    src, x = h[:, c, :], h[:, c, :]
                    for k in range(g + 1):
                        s = 2 ** k
                        dst = tb[:, k % 2, :]
                        step(V.tensor_tensor(dst[:, s:T], src[:, s:T], src[:, 0:T - s], A.add))
                        step(V.tensor_copy(dst[:, 0:s], src[:, 0:s]))
                        src = dst
                    step(V.scalar_tensor_tensor(out=pooled[:, c, :], in0=src, scalar=1.0 / 2 ** (g + 1), in1=x,
                                                op0=A.mult, op1=A.subtract))
                    step(V.tensor_tensor(sg[:, 0, 0:16], src[:, 0:16], par(COL2, "cnt", 16 * g, 16), A.mult))
                    V.tensor_tensor(pooled[:, c, 0:16], sg[:, 0, 0:16], x[:, 0:16], A.subtract).then_inc(S["pl"], 1)
                dve.wait_ge(S["pl"], st["pl"] + KC)
                for g in range(4):
                    dve.wait_ge(S["plp"], st["plp"] + g + 1)
                    for o in range(2):
                        c = 2 * g + o
                        ins = V.tensor_scalar(tb[:, o, :], bank[2 * (g % 2) + o][:], par(COL2, "pool_b", c),
                                              par(COL2, "pool_s", c), A.add, A.mult)
                        if o:
                            ins.then_inc(S["plt"], 1)
                            dve.wait_ge(S["plt"], st["plt"] + g + 1)
                        else:
                            step(ins)
                    for o in range(2):
                        c = 2 * g + o
                        V.scalar_tensor_tensor(out=h[:, c, :], in0=h[:, c, :], scalar=ALPHA, in1=tb[:, o, :],
                                               op0=A.mult, op1=A.add).then_inc(S["r"], 1)
                        dve.wait_ge(S["r"], st["r"] + c + 1)
                        step(V.tensor_tensor(s1[:], s1[:], h[:, c, :], A.add))
                    for o in range(2):
                        add_squares(st, 2 * g + o, S["sq"], st["sq"] + 2 * g + o + 1)

            dve.wait_ge(loaded, 16 * 4)
            V.tensor_copy(causal_b[:], tb[:, 0, 0:P]).then_inc(consts_made, 1)
            V.tensor_copy(ident_b[:], ident).then_inc(consts_made, 1)
            V.tensor_tensor(lbt[:, 2, :], par(COL1, "lb", 4, 4), par(COL1, "lb", 0, 4), A.subtract
                            ).then_inc(consts_made, 1)
            does = dict(sumsq=sumsq, rms=norm, ln=norm, split=split, project=project, compress=compress, hgrn=hgrn,
                        nsa_prep=nsa_prep, cmp_att=cmp_att, nsa=nsa, w_out=w_out, pg=pg, ffn_in=ffn_in,
                        ffn_out=ffn_out, da_prep=da_prep, da_project=da_project, da_rope=da_rope, da=da,
                        da_norm=da_norm, xa_project=xa_project, xa=xa, pool=pool_mix)
            for st in stages:
                if st["kind"] in does:
                    does[st["kind"]](st)


def shape_constants():
    eye = np.eye(P, dtype=np.float32)
    group = np.arange(P) // 64
    e64, e128 = np.zeros((P, 32), np.float32), np.zeros((P, 32), np.float32)
    e64[:, 14], e64[:, 15] = (group == 0) / 64, (group == 1) / 64
    e128[:, 14:16] = 1 / 128
    block = (group[:, None] == group[None, :]).astype(np.float32) / 64

    def rotation(half, width):
        r = np.zeros((P, P), np.float32)
        for m in range(P):
            d = m % 64
            if d < half:
                r[m + half, m] = -1
            elif d < width:
                r[m - half, m] = 1
        return r
    consts = np.concatenate([np.full((P, P), 1 / D, np.float32), eye, block, e64, e128, rotation(8, 16)], 1)
    inv = np.float32(500000.0) ** (-np.arange(0, 16, 2, dtype=np.float32) / np.float32(16))
    ang = np.arange(T, dtype=np.float32)[None, :] * inv[:, None].astype(np.float32)
    rope = np.zeros((P, 2, T), np.float32)
    rope[:, 0] = 1
    for m in range(P):
        if m % 64 < 16:
            rope[m, 0], rope[m, 1] = np.cos(ang[m % 8]), np.sin(ang[m % 8])
    s, t = np.arange(P)[:, None], np.arange(P)[None, :]
    masks = [s == t] + [(s // (2 * m) == t // (2 * m)) & (s % (2 * m) < m) & (t % (2 * m) >= m)
                        for m in (1, 2, 4, 8, 16, 32, 64)]
    masks = np.stack(masks, 1).astype(np.int32)
    tok = np.arange(TT)[None, :, None] * P + np.arange(P)[:, None, None]
    seen = (np.arange(32)[None, None, :] * 16 + 31 <= tok)
    cmp_tab = np.stack([seen.astype(np.float32), np.where(seen, 0, NEG).astype(np.float32)], 1)
    spread = np.zeros((16, 8, P), np.float32)
    for j in range(8):
        spread[2 * j, j, 0:64] = 1
        spread[2 * j + 1, j, 64:P] = 1
    causal = np.where(t <= s, 0, NEG).astype(np.float32)
    inv2 = (1.0 / (np.float32(10000.0) ** (np.arange(0, 64, 2, dtype=np.float32) / np.float32(64)))).astype(np.float32)
    cnt = np.stack([1.0 / np.minimum(np.arange(16) + 1, 2 ** (g + 1)) for g in range(4)]).astype(np.float32)
    return dict(consts=consts, rope=rope, masks=masks, cmp_tab=cmp_tab, spread=spread.reshape(16, 8 * P),
                causal=causal, rot2=rotation(32, 64), inv=inv2[np.arange(P) % 32][:, None],
                cnt=np.tile(cnt.reshape(1, 64), (P, 1)))


def weight_slabs(w_in, w_out, w_pg, ffn_w_in, ffn_w_out, da_w_qkv, da_w_o, xa_wq, xa_wkv, xa_wo):
    slabs = []

    def chunk(w, c0):
        slabs.append(w[:, c0:c0 + P].reshape(KC, P, P).transpose(1, 0, 2).reshape(P, D))

    def tokens(w):
        for q in range(4):
            slabs.append(w[256 * q:256 * q + 256].reshape(2, P, 512).transpose(1, 0, 2).reshape(P, D))

    def ffn(l, i):
        for f in range(NF):
            chunk(ffn_w_in[l, i], f * P)
            chunk(ffn_w_in[l, i], NF * P + f * P)
        for f in range(NF):
            slabs.append(ffn_w_out[l, i, f * P:(f + 1) * P])

    for l in range(DEPTH):
        w = w_in[l]
        tokens(w[:, 1024:1536])
        tokens(np.concatenate([w[:, 3456:3584], w[:, 3712:3840], w[:, 3840:3864],
                               np.zeros((D, 512 - VG), w.dtype)], 1))
        starts = [0, 512, 1536, 2048, 2560, 3864]
        for s in starts:
            for c in range(4):
                chunk(w, s + c * P)
        for s in (3072, 3200, 3328, 3584):
            chunk(w, s)
        for c in range(KC):
            chunk(w_out[l], c * P)
        for c in range(KC):
            chunk(w_pg[l], c * P)
    for l in range(DEPTH):
        ffn(l, 0)
        if l == 0:
            for c in range(2 * KC):
                chunk(da_w_qkv[0], c * P)
            for half in range(2):
                tokens(da_w_qkv[0][:, 2 * D + 512 * half:2 * D + 512 * half + 512])
            for c in range(KC):
                chunk(da_w_o[0], c * P)
        for c in range(KC):
            chunk(xa_wq[l], c * P)
        for c in range(KC):
            chunk(xa_wkv[l], c * P)
        for half in range(2):
            tokens(xa_wkv[l][:, D + 512 * half:D + 512 * half + 512])
        for c in range(KC):
            chunk(xa_wo[l], c * P)
        ffn(l, 1)
    return np.ascontiguousarray(np.stack(slabs))


def by_chunk(v):
    return np.ascontiguousarray(v.reshape(-1, P).T)


def kernel(x, p, norm_g, w_in, hgrn_lb, hgrn_onorm_g, nsa_qnorm_g, nsa_knorm_g, cmp_pe, cmp_w1, cmp_w2,
           w_out, ple_norm_g, w_pg, w_pp, mem_2, positions_2, ffn_w_in_2, ffn_w_out_2, ln_g_2, ln_b_2,
           da_w_qkv_2, da_w_o_2, da_lam_q_2, da_lam_k_2, da_subln_g_2, pool_w_2, pool_b_2, pool_scale_2,
           ret_w_qkvg_2, ret_w_o_2, xa_wq_2, xa_wkv_2, xa_wo_2):
    import concourse.bacc as bacc
    from concourse.bass_utils import run_bass_kernel_spmd

    (x, p, norm_g, w_in, hgrn_lb, hgrn_onorm_g, nsa_qnorm_g, nsa_knorm_g, cmp_pe, cmp_w1, cmp_w2, w_out, ple_norm_g,
     w_pg, w_pp, mem_2, positions_2, ffn_w_in_2, ffn_w_out_2, ln_g_2, ln_b_2, da_w_qkv_2, da_w_o_2, da_lam_q_2,
     da_lam_k_2, da_subln_g_2, pool_w_2, pool_b_2, pool_scale_2, xa_wq_2, xa_wkv_2, xa_wo_2) = (
        np.asarray(a) for a in (
            x, p, norm_g, w_in, hgrn_lb, hgrn_onorm_g, nsa_qnorm_g, nsa_knorm_g, cmp_pe, cmp_w1, cmp_w2, w_out,
            ple_norm_g, w_pg, w_pp, mem_2, positions_2, ffn_w_in_2, ffn_w_out_2, ln_g_2, ln_b_2, da_w_qkv_2, da_w_o_2,
            da_lam_q_2, da_lam_k_2, da_subln_g_2, pool_w_2, pool_b_2, pool_scale_2, xa_wq_2, xa_wkv_2, xa_wo_2))
    const = shape_constants()

    def twice(v):
        return np.concatenate([v.T, v.T], 0)

    def padded(v):
        return np.concatenate([v.T, np.zeros((64, v.shape[0]), v.dtype)], 0)
    prm1 = np.concatenate([
        by_chunk(norm_g), by_chunk(ple_norm_g), by_chunk(hgrn_onorm_g), twice(nsa_qnorm_g),
        twice(nsa_knorm_g.reshape(-1, 64)), by_chunk(hgrn_lb), by_chunk(cmp_pe),
        cmp_w2[:, 0].transpose(1, 0, 2).reshape(P, -1), cmp_w2[:, 1].transpose(1, 0, 2).reshape(P, -1)], 1)
    prm2 = np.concatenate([
        by_chunk(ln_g_2), by_chunk(ln_b_2), by_chunk(da_subln_g_2), by_chunk(pool_b_2), by_chunk(pool_scale_2),
        padded(da_lam_q_2[0]), padded(da_lam_k_2[0]), const["inv"], const["cnt"]], 1)
    arrays = dict(
        x_t=x[0].T,
        slabs=weight_slabs(w_in, w_out, w_pg, ffn_w_in_2, ffn_w_out_2, da_w_qkv_2, da_w_o_2, xa_wq_2, xa_wkv_2,
                           xa_wo_2),
        prm1=prm1, prm2=prm2, consts=const["consts"], rot2=const["rot2"], rope=const["rope"],
        masks=const["masks"], cmp_tab=const["cmp_tab"], spread=const["spread"], causal=const["causal"],
        w1=cmp_w1.reshape(DEPTH, 2, 16, P, P).transpose(0, 1, 3, 2, 4),
        pp_w=w_pp.reshape(DEPTH, 2, P, KC, P).transpose(0, 2, 3, 1, 4).reshape(DEPTH, P, 16, P),
        p_t=p[:, 0].reshape(DEPTH, T, 2, P).transpose(0, 3, 2, 1),
        pool_w=pool_w_2[0].reshape(4, 2, P, 2, P).transpose(2, 0, 3, 1, 4).reshape(P, 16, P),
        mem_t=mem_2[0].reshape(MEM, KC, P).transpose(2, 1, 0),
        positions=positions_2)
    arrays = {"in_" + k: np.ascontiguousarray(v) for k, v in arrays.items()}
    nc = bacc.Bacc("TRN2", target_bir_lowering=False, num_devices=1)
    args = {k[3:]: nc.dram_tensor(k, a.shape, mybir.dt.from_np(a.dtype), kind="ExternalInput").ap()
            for k, a in arrays.items()}
    out = nc.dram_tensor("out", (D, T), mybir.dt.float32, kind="ExternalOutput").ap()
    program(nc, out=out, **args)
    r = run_bass_kernel_spmd(nc, [arrays], core_ids=[0])
    return np.ascontiguousarray(r.results[0]["out"].T)[None]
```

```python
from contextlib import ExitStack

import numpy as np

import concourse.bass as bass
from concourse import mybir

P = 128
T = 512
TT = T // P
D = 1024
KC = D // P
DEPTH = 2
NF = 22
MEM = 256
MT = MEM // P
NH = 8
NC = 31
NPROJ = 28
HQ, HF, HGO, HZ, NQ, NZ, KCM, VCM, KSL, KWN = 0, 4, 8, 12, 16, 20, 24, 25, 26, 27
KZ = (HF, HZ)
VG = 280
RING = 4
TAIL = 3
RMS_EPS = 1e-6
LN_EPS = 1e-5
ALPHA = (2 * DEPTH) ** 0.25
LAM_INIT = 0.2
LA = 7
LEVELS = 10
NEG = -1e30
ROUND = 12582912.0
PI = 3.1415925


def columns(sizes):
    at, col = 0, {}
    for name, n in sizes:
        col[name] = at
        at += n
    return col, at


COL1, NPRM1 = columns([("norm_g", DEPTH * KC), ("ple_g", DEPTH * KC), ("onorm", DEPTH), ("qn", DEPTH),
                       ("kn", DEPTH * 3), ("lb", DEPTH * 4), ("pe", DEPTH * 32), ("w2k", DEPTH * 64),
                       ("w2v", DEPTH * 64)])
COL2, NPRM2 = columns([("ln_g", DEPTH * 4 * KC), ("ln_b", DEPTH * 4 * KC), ("subln", 1), ("pool_b", KC),
                       ("pool_s", KC), ("lam_q", 2), ("lam_k", 2), ("inv", 1), ("cnt", 64)])
NPRM = max(NPRM1, NPRM2)
CC, NCONST = columns([("mean", P), ("ident", P), ("block", P), ("e64", 32), ("e128", 32), ("rot", P)])

COUNTS = {
    "sumsq": dict(sq=KC, s2=KC - 2),
    "rms": dict(stat=1, act_stat=1, var=1, v=KC, xh=KC, xl=KC),
    "ln": dict(stat=2, act_stat=2, var=1, v=KC, xh=KC, xl=KC),
    "split": dict(xh=KC, xl=KC),
    "project": dict(slab=36, prod=22, took=16),
    "compress": dict(cmp_p=5, cmp_a=9, cmp_v=8),
    "hgrn": dict(lvl_k=4 * (LEVELS - 2), lvl_v=4 * LEVELS, lvl_p=4 * LEVELS, lvl_a=LA + 12, gst=4, gsq=4, gvar=1, gact=1, grs=1,
                 gbc=4, gused=4, hpv=4),
    "nsa_prep": dict(gst=6, gsq=6, gvar=1, gact=1, grs=1, gbc=6, gused=6, rot=6, roped=6, xcos=6,
                     zeroed=4, ca_p=1, ca_v=2, ca_a=2),
    "cmp_att": dict(ca_a=2, ca_t=1),
    "nsa": dict(qk=64, ex=64, mx=64, pn=64, tr=64, pt=64, pv=16, oe=4),
    "w_out": dict(slab=8, prod=4, took=4, r=KC // 2, sq=KC // 2, s2=KC - 2),
    "pg": dict(slab=8, prod=4, took=4, r=KC, sq=KC, s2=KC - 2),
    "ffn_in": dict(slab=2 * NF, prod=NF, took=NF, hh=NF, hv=NF, hl=NF),
    "ffn_out": dict(slab=NF, prod=NF - TAIL + 4, took=4, r=KC // 2, sq=KC // 2, s2=KC - 2),
    "da_project": dict(slab=24, prod=16, took=10, zeroed=2),
    "da_prep": dict(dp_v=3, dp_a=3, dp_p=1),
    "da_rope": dict(rot=16, roped=16, xcos=16),
    "da": dict(qk=64, ex=64, mx=64, pn=32, tr=32, pt=32, pv=8, oe=8),
    "da_norm": dict(gst=8, gsq=8, gvar=1, gact=1, grs=1, gbc=8, gused=8),
    "xa_project": dict(slab=24, prod=16, took=10, msplit=2),
    "xa": dict(qk=16, ex=16, mx=16, pn=16, tr=16, pt=16, pv=4, oe=8),
    "xa_rest": dict(slab=12, prod=8, took=5),
    "pool": dict(slab=12, prod=8, took=5, msplit=2, pl=KC, plp=4, r=KC, sq=KC, s2=KC - 2, plt=4),
}


def plan():
    order = [("sumsq", 0, 0)]
    for l in range(DEPTH):
        order += [("rms", l, 0), ("project", l, 0), ("compress", l, 0), ("hgrn", l, 0),
                  ("nsa_prep", l, 0), ("cmp_att", l, 0), ("nsa", l, 0), ("split", l, 0), ("w_out", l, 0),
                  ("rms", l, 1), ("pg", l, 0)]
    order += [("split", 0, 1)]
    for l in range(DEPTH):
        order += [("ffn_in", l, 0), ("ffn_out", l, 0), ("ln", l, 0)]
        if l == 0:
            order += [("da_prep", l, 0), ("da_project", l, 0), ("da_rope", l, 0), ("da", l, 0),
                      ("da_norm", l, 0), ("w_out", l, 1)]
        else:
            order += [("pool", l, 0)]
        order += [("ln", l, 1), ("xa_rest" if l else "xa_project", l, 0), ("xa", l, 0), ("split", l, 2), ("w_out", l, 2),
                  ("ln", l, 2), ("ffn_in", l, 1), ("ffn_out", l, 1), ("ln", l, 3)]
    keys = {k for c in COUNTS.values() for k in c} | {"hn"}
    now, stages = dict.fromkeys(sorted(keys), 0), []
    for kind, layer, which in order:
        add = dict(COUNTS[kind])
        if kind == "ln" and (layer, which) == (1, 3):
            add["xh"] = add["xl"] = 0
        if kind == "ln" and (layer, which) == (1, 0):
            add["xh"] = add["xl"] = 0
            add["hn"] = KC
        if kind == "da_norm":
            add["xh"] = add["xl"] = KC
        before = stages[-1]["kind"] if stages else None
        stages.append(dict(kind=kind, layer=layer, which=which, before=before, pooled=before == "pool",
                           own_sq=before in ("sumsq", "pg", "pool"), **now))
        for k, n in add.items():
            now[k] = now.get(k, 0) + n
    return stages, now


class Steps:

    def __init__(self, eng, sem):
        self.eng, self.sem, self.n, self.reg = eng, sem, 0, None

    def __call__(self, ins):
        ins.then_inc(self.sem, 1)
        self.n += 1
        self.eng.wait_ge(self.sem, self.n if self.reg is None else self.reg + self.n)

    def loop(self, trips, per):
        start = self.n
        with self.eng.Fori(0, trips) as i:
            if per:
                self.reg = i * per
            yield i
        assert self.n - start == per, self.n - start
        self.reg = None
        self.n = start + per * trips


def flat(ap):
    return ap.rearrange("p o n -> p (o n)")


def program(nc, x_t, slabs, prm1, prm2, consts, rot2, rope, masks, cmp_tab, spread, causal, w1, pp_w, p_t,
            pool_w, mem_t, positions, out):
    f32, f32r, bf16, i32 = mybir.dt.float32, mybir.dt.float32r, mybir.dt.bfloat16, mybir.dt.int32
    A, F, AX = mybir.AluOpType, mybir.ActivationFunctionType, mybir.AxisListType.X
    stages, total = plan()
    n_slabs = total["slab"]
    assert n_slabs == slabs.shape[0] and n_slabs % 4 == 0, (n_slabs, slabs.shape)

    ctx = ExitStack()
    with ctx:
        def keep(name, shape, dt=f32):
            return ctx.enter_context(nc.sbuf_tensor(name, shape, dt))

        def sem(name):
            return ctx.enter_context(nc.semaphore(name))

        h = keep("h", [P, KC, T])
        raw = keep("raw", [P, RING, D])
        wh = keep("wh", [P, RING, D], f32r)
        wl = keep("wl", [P, RING, D], f32r)
        cst = keep("cst", [P, NCONST])
        prm = keep("prm", [P, NPRM])
        ident_b = keep("ident_b", [P, P], bf16)
        causal_b = keep("causal_b", [P, P], bf16)
        sg = keep("sg", [P, 2, T])
        with nc.sbuf_tensor("w1v", [P, 16, P], f32) as w1v:
            pass
        tb = keep("tb", [P, 2, T])
        sq = keep("sq", [P, 2, T])
        s1 = keep("s1", [P, T])
        s2 = keep("s2", [P, T])
        kc = keep("kc", [P, 2, 32])
        vc = keep("vc", [P, 2, 64])
        small = keep("small", [P, 4, 2, 4])
        ksm = keep("ksm", [P, 3, 64])
        lbt = keep("lbt", [P, 4, 4])
        lam = keep("lam", [P, 4])

        def views(specs):
            made = []
            with ExitStack() as scope:
                for name, shape, dt in specs:
                    made.append(scope.enter_context(nc.sbuf_tensor(name, shape, dt)))
            return made

        with nc.sbuf_tensor("x_room", [P, 2 * KC * T], f32):
            pass
        (kk_k, kk_v, blocks_k, blocks_v, _, hidk, hidv) = views([
            ("kk_k", [P, 2, T], f32), ("kk_v", [P, 2, T], f32), ("blocks_k", [P, 16, 2 * NC], f32),
            ("blocks_v", [P, 16, 2 * NC], f32), ("gap", [P, 12 * T + 1024 - 4 * T - 64 * NC], f32),
            ("hidk", [P, 64], f32),
                                               ("hidv", [P, 2, 4, 32], f32)])
        (hk, ad, ax) = views([("hk", [P, 4, T], f32), ("ad", [P, 4, T], f32), ("ax", [P, 4, 768], f32)])
        (pa, ptt, pct) = views([("pa", [P, 2, 1280], f32), ("ptt", [P, 2, TT, T], f32),
                                    ("pct", [P, 2, T], f32)])
        (dpa, dpt) = views([("dpa", [P, 3, 1280], f32), ("dpt", [P, 2, TT, T], f32)])
        xh, xl = keep("xh", [P, KC, T], f32r), keep("xl", [P, KC, T], f32r)
        (proj, vt, vgt, rop, msk, cmt, side, spr) = views([
            ("proj", [P, NPROJ, T], f32), ("vt", [P, TT, T], f32), ("vgt", [P, TT, VG], f32),
            ("rop", [P, 2, T], f32), ("msk", [P, 7 + 1, P], i32), ("cmt", [P, 2, TT, 32], f32),
            ("side", [P, 16, P], f32), ("spr", [16, 6 * P], f32)])
        (dq, dk, dkz, dv, drop, dspr) = views([
            ("dq", [P, KC, T], f32), ("dk", [P, KC, T], f32), ("dkz", [P, 2, KC, T], f32), ("dv", [P, TT, D], f32),
            ("drop", [P, 2, T], f32), ("dspr", [16, 8 * P], f32)])
        (dpos,) = views([("dpos", [P, T], i32)])
        (xq, xk, xv, xm, mh, ml, xpa, xpt) = views([
            ("xq", [P, KC, T], f32), ("xk", [P, KC, MEM], f32), ("xv", [P, MT, D], f32),
            ("xm", [P, KC, MEM], f32), ("mh", [P, KC, MEM], f32r), ("ml", [P, KC, MEM], f32r),
            ("xpa", [P, 2, TT, MEM], f32), ("xpt", [P, 2, MT, T], f32)])
        (pooled, _, pside) = views([("pooled", [P, KC, T], f32), ("memory_room", [P, 5 * KC * MEM], f32),
                                    ("pside", [P, 16, P], f32)])
        hh, hl = keep("hh", [P, NF, T], f32r), keep("hl", [P, NF, T], f32r)
        pin = vt
        tot_a = proj[:, KCM:KCM + 2, :].rearrange("p a t -> p (a t)").rearrange("p (h t) -> p h t", h=4)
        tot_b = sq[:, 0, :].rearrange("p (h t) -> p h t", h=4)

        bank = [ctx.enter_context(nc.psum_tensor(f"bank{i}", [P, T], f32)) for i in range(8)]

        mean_m = cst[:, CC["mean"]:CC["mean"] + P]
        ident = cst[:, CC["ident"]:CC["ident"] + P]
        block_m = cst[:, CC["block"]:CC["block"] + P]
        rot_m = cst[:, CC["rot"]:CC["rot"] + P]

        def group_m(name, j):
            a = CC[name] + 14 - 2 * j
            return cst[:, a:a + 16]

        def par(col, name, i=0, n=1):
            return prm[:, col[name] + i:col[name] + i + n]

        def cat(ap, n):
            return ap.rearrange("p (m o) -> p m o", o=1).broadcast_to([P, ap.shape[1], n])

        def level(lv, hd):
            m = 2 ** (lv - 2)
            nb = T // (2 * m)
            tot = proj[:, HF + hd, :] if m == 1 else (tot_a if lv % 2 else tot_b)[:, hd, 0:2 * nb]
            q = proj[:, HQ + hd, :].rearrange("p (b two m) -> p b two m", two=2, m=m)[:, :, 1, :]
            k = hk[:, hd, :].rearrange("p (b two m) -> p b two m", two=2, m=m)[:, :, 0, :]
            return tot, tot[:, 0:2 * nb:2], tot[:, 1:2 * nb:2], q, k

        raw_in = [sem(f"raw_in{i}") for i in range(RING)]
        w_high, w_low = sem("w_high"), sem("w_low")
        prod = sem("prod")
        took_a, took_v = sem("took_a"), sem("took_v")
        loaded, params_in, side_in, block2_in, mem_in = (sem(n) for n in ("loaded", "params_in", "side_in",
                                                                          "block2_in", "mem_in"))
        consts_made, final, stored, w1k_in = sem("consts_made"), sem("final"), sem("stored"), sem("w1k_in")
        S = {k: sem("s_" + k) for k in total if k not in ("slab", "prod", "took")}
        act_steps, dve_steps = sem("act_steps"), sem("dve_steps")
        blk = ctx.enter_context(nc.Block())

        @blk.sync
        def _(sp):
            for ap, src in ((h[:], x_t.rearrange("(c p) t -> p c t", p=P)), (prm[:, 0:NPRM1], prm1),
                            (cst[:], consts), (tb[:, 0, 0:P], causal)):
                sp.dma_start(ap, src).then_inc(loaded, 16)
            for n in range(RING):
                sp.dma_start(raw[:, n, :], slabs[n]).then_inc(raw_in[n], 16)
            for ap, src in ((rop[:], rope), (msk[:], masks), (cmt[:], cmp_tab), (spr[:], spread[:, 0:6 * P]),
                            (side[:], w1[0, 0])):
                sp.dma_start(ap, src).then_inc(params_in, 16)
            with sp.Fori(1, n_slabs // RING) as i:
                for n in range(RING):
                    sp.wait_ge(w_low, i * RING + (n - RING + 1))
                    sp.dma_start(raw[:, n, :],
                                 slabs[bass.ds(i * RING + n, 1)].rearrange("o p c -> (o p) c")
                                 ).then_inc(raw_in[n], 16)
            for c in range(KC):
                sp.wait_ge(final, c + 1)
                sp.dma_start(out[c * P:(c + 1) * P, :], h[:, c, :]).then_inc(stored, 16)
            sp.wait_ge(stored, 16 * KC)

        @blk.gpsimd
        def _(pool):
            def low(n, i=None):
                pool.wait_ge(w_high, n + 1 if i is None else i * RING + (n + 1))
                nc.gpsimd.tensor_tensor(wl[:, n % RING, :], raw[:, n % RING, :], wh[:, n % RING, :], A.subtract
                                        ).then_inc(w_low, 1)

            def lows(first, count):
                with pool.Fori(0, count // RING) as i:
                    for n in range(RING):
                        low(first + n, i)
                for n in range(count // RING * RING, count):
                    low(first + n)

            def norm(st):
                for c in range(KC):
                    pool.wait_ge(S["xh"], st["xh"] + c + 1)
                    nc.gpsimd.tensor_tensor(xl[:, c, :], h[:, c, :] if st["kind"] == "ln" else tb[:, c % 2, :],
                                            xh[:, c, :], A.subtract).then_inc(S["xl"], 1)

            def cosines(st, n, ready, x, table):
                for j in range(n):
                    if ready:
                        pool.wait_ge(S[ready], st[ready] + j + 1)
                    if j >= 2:
                        pool.wait_ge(S["roped"], st["roped"] + j - 1)
                    nc.gpsimd.tensor_tensor(sq[:, j % 2, :], x(j), table[:, 0, :], A.mult).then_inc(S["xcos"], 1)

            def hgrn(st):
                for lv in range(2, LEVELS):
                    for hd in range(4):
                        pool.wait_ge(S["lvl_v"], st["lvl_v"] + 4 * (lv - 1) + hd + 1)
                        pool.wait_ge(S["lvl_p"], st["lvl_p"] + 4 * (lv - 1) + hd + 1)
                        tot, even, odd, q, k = level(lv, hd)
                        nc.gpsimd.tensor_tensor(k, k, cat(odd, k.shape[2]), A.mult).then_inc(S["lvl_k"], 1)

            def nsa_prep(st):
                pool.wait_ge(S["gused"], st["gused"])
                pool.wait_ge(S["lvl_k"], st["lvl_k"])
                for n in range(4):
                    half, z = n // 2, KZ[n % 2]
                    nc.gpsimd.memset(proj[64 - 64 * half:P - 64 * half, z + half:z + 4:2, :], 0.0
                                     ).then_inc(S["zeroed"], 1)
                    pool.wait_ge(S["zeroed"], st["zeroed"] + n + 1)
                cosines(st, 6, "gused", lambda j: proj[:, (NQ, NQ + 1, NQ + 2, NQ + 3, KSL, KWN)[j], :], rop)

            def da_rope(st):
                pool.wait_ge(took_a, st["took"])
                pool.wait_ge(took_v, st["took"])
                cosines(st, 2 * KC, None, lambda j: (dq if j < KC else dk)[:, j % KC, :], drop)

            lows(0, RING)
            for st, after in zip(stages, stages[1:] + [total]):
                if st["kind"] in ("rms", "ln") and after["xh"] > st["xh"]:
                    norm(st)
                elif st["kind"] == "hgrn":
                    hgrn(st)
                elif st["kind"] == "nsa_prep":
                    nsa_prep(st)
                elif st["kind"] == "da_rope":
                    da_rope(st)
                elif st["kind"] == "da_project":
                    lows(st["slab"] + RING, after["slab"] - st["slab"] - RING)
                    pool.wait_ge(w_low, after["slab"])
                    for half in range(2):
                        nc.gpsimd.memset(dkz[64 - 64 * half:P - 64 * half, half, :, :], 0.0).then_inc(S["zeroed"], 1)
                        pool.wait_ge(S["zeroed"], st["zeroed"] + half + 1)
                    lows(after["slab"], RING)
                elif after["slab"] > st["slab"]:
                    if st["kind"] == "pool":
                        pool.wait_ge(S["msplit"], st["msplit"] + 1)
                        nc.gpsimd.tensor_tensor(ml[:], xm[:], mh[:], A.subtract).then_inc(S["msplit"], 1)
                    lows(st["slab"] + RING, min(after["slab"] + RING, n_slabs) - st["slab"] - RING)

        @blk.tensor
        def _(pe):
            def passes(dst, high_l, low_l, high_r, low_r, first, last):
                nc.tensor.matmul(dst, high_l, high_r, start=first, stop=False)
                nc.tensor.matmul(dst, high_l, low_r, start=False, stop=False)
                return nc.tensor.matmul(dst, low_l, high_r, start=False, stop=last)

            def tile_of(n, j):
                return wh[:, n % RING, j * P:(j + 1) * P], wl[:, n % RING, j * P:(j + 1) * P]

            def pair(slab, kind, act_h, act_l, w, waits):
                for k in range(KC):
                    waits(k)
                    for o in range(2):
                        a, b = tile_of(slab + o, k)
                        last = passes(bank[2 * kind + o][:, 0:w], a, b, act_h[:, k, :], act_l[:, k, :],
                                      k == 0, k == KC - 1)
                return last

            def products(st, slab, ticket, step, pairs, split_base, act_h=xh, act_l=xl, w=T):
                pe.wait_ge(took_a, ticket)
                pe.wait_ge(took_v, ticket)
                if split_base is not None:
                    pe.wait_ge(S["xl"], split_base + 1)

                def two(i):
                    for j in range(2):
                        pe.wait_ge(w_low, i * 4 + (slab + 2 * j + 2))
                        if ticket + j > 0:
                            pe.wait_ge(took_a, i * 2 + (ticket + j - 1))
                            pe.wait_ge(took_v, i * 2 + (ticket + j - 1))

                        def waits(k):
                            if split_base is not None and j == 0:
                                pe.wait_ge(S["xl"], split_base + k + 1)
                        pair(slab + 2 * j, j, act_h, act_l, w, waits).then_inc(prod, 1)
                if pairs == 2:
                    two(0)
                else:
                    with pe.Fori(0, pairs // 2) as i:
                        two(i)

            def token_major(slab, ticket, banks, act_h, act_l, tiles, w, split_base):
                pe.wait_ge(took_a, ticket)
                pe.wait_ge(took_v, ticket)
                for s in range(4):
                    pe.wait_ge(w_low, slab + s + 1)
                    for k in range(2):
                        c = 2 * s + k
                        if split_base is not None:
                            pe.wait_ge(S["xl"], split_base + c + 1)
                        n = (slab + s) % RING
                        b_h, b_l = wh[:, n, k * 512:k * 512 + w], wl[:, n, k * 512:k * 512 + w]
                        for t in range(tiles):
                            ts = slice(t * P, (t + 1) * P)
                            last = passes(bank[banks + t][:, 0:w], act_h[:, c, ts], act_l[:, c, ts], b_h, b_l,
                                          c == 0, c == KC - 1)
                    last.then_inc(prod, 1)

            def rms(st):
                if st["pooled"]:
                    pe.wait_ge(took_a, st["took"])
                    pe.wait_ge(took_v, st["took"])
                pe.wait_ge(S["s2"], st["s2"])
                if st["kind"] == "ln":
                    nc.tensor.matmul(bank[4][:], mean_m, s1[:], start=True, stop=False)
                nc.tensor.matmul(bank[5][:], mean_m, s2[:], start=True, stop=False)
                if st["kind"] == "ln":
                    for c in (KC - 2, KC - 1):
                        pe.wait_ge(S["r"], st["r"] - (1 if st["pooled"] and c == KC - 2 else 0))
                        if c == KC - 1:
                            pe.wait_ge(took_v, st["took"])
                        last = nc.tensor.matmul(bank[4][:], mean_m, h[:, c, :], start=False, stop=(c == KC - 1))
                    last.then_inc(S["stat"], 1)
                for o in range(2):
                    pe.wait_ge(S["sq"], st["sq"] - (1 if st["own_sq"] and o == 0 else 0))
                    if o and st["took"]:
                        pe.wait_ge(took_a, st["took"])
                    last = nc.tensor.matmul(bank[5][:], mean_m, sq[:, o, :], start=False, stop=(o == 1))
                last.then_inc(S["stat"], 1)

            def project(st):
                token_major(st["slab"], st["took"], 4, xh, xl, TT, T, st["xl"] - KC)
                token_major(st["slab"] + 4, st["took"] + 1, 0, xh, xl, TT, VG, None)
                products(st, st["slab"] + 8, st["took"] + 2, st["prod"] + 8, 14, None)

            def compress(st):
                pe.wait_ge(took_a, st["took"])
                pe.wait_ge(took_v, st["took"])
                for b, (w, x, weights) in enumerate((
                        (side, blocks_k, (params_in, 80) if st["layer"] == 0 else (w1k_in, 16)),
                        (w1v, blocks_v, (side_in, 16 * (1 + 3 * st["layer"]))))):
                    pe.wait_ge(*weights)
                    pe.wait_ge(S["cmp_v"], st["cmp_v"] + 5 + b)
                    for i in range(16):
                        last = nc.tensor.matmul(bank[4 + b][:, 0:2 * NC], w[:, i, :], x[:, i, :],
                                                start=(i == 0), stop=(i == 15))
                    last.then_inc(S["cmp_p"], 1)

            def compressed(st, part):
                done = st["cmp_a"] - COUNTS["compress"]["cmp_a"]
                if part == 0:
                    pe.wait_ge(S["cmp_a"], done + 5)
                    for half in (0, 64):
                        last = nc.tensor.matmul(bank[6][half:half + 64, 0:2 * NC], par(COL1, "w2k", 64 * st["layer"], 64),
                                                hidk[:, 0:2 * NC], start=True, stop=True)
                    last.then_inc(S["cmp_p"], 1)
                    pe.wait_ge(S["cmp_a"], done + 7)
                    for g in range(2):
                        last = nc.tensor.matmul(bank[7][:, 64 * g:64 * g + 64],
                                                hidv[:, g, :, :].rearrange("p a c -> p (a c)"),
                                                par(COL1, "w2v", 64 * st["layer"], 64), start=True, stop=True)
                    last.then_inc(S["cmp_p"], 1)
                else:
                    pe.wait_ge(S["cmp_a"], done + 8)
                    nc.tensor.matmul(bank[4][:, 0:2 * NC], block_m, ksm[:, 0, 0:2 * NC], start=True,
                                     stop=True).then_inc(S["cmp_p"], 1)

            def hgrn(st):
                for lv in range(LEVELS):
                    if lv in (3, 5):
                        compressed(st, lv // 4)
                    for hd in range(4):
                        pe.wait_ge(S["lvl_v"], st["lvl_v"] + 4 * lv + hd + 1)
                        if lv >= 2:
                            pe.wait_ge(S["lvl_k"], st["lvl_k"] + 4 * (lv - 2) + hd + 1)
                        q, k, b = proj[:, HQ + hd, :], hk[:, hd, :], bank[hd]
                        if lv < LEVELS - 2:
                            for t in range(TT):
                                ts = slice(t * P, (t + 1) * P)
                                last = nc.tensor.matmul(b[:, ts], k[:, ts], q[:, ts], start=True, stop=True)
                        elif lv == LEVELS - 2:
                            for t in range(2):
                                last = nc.tensor.matmul(b[:, t * P:(t + 1) * P], k[:, 2 * t * P:(2 * t + 1) * P],
                                                        q[:, (2 * t + 1) * P:(2 * t + 2) * P], start=True, stop=True)
                        else:
                            pe.wait_ge(S["lvl_a"], st["lvl_a"] + LA + 2 * hd + 2)
                            for t in range(2):
                                last = nc.tensor.matmul(b[:, 256 * t:256 * t + 256], k[:, t * P:(t + 1) * P],
                                                        q[:, 256:512], start=True, stop=True)
                        last.then_inc(S["lvl_p"], 1)
                pe.wait_ge(S["cmp_v"], st["cmp_v"])
                for hd in range(4):
                    pe.wait_ge(S["lvl_a"], st["lvl_a"] + LA + 8 + hd + 1)
                    o, at = bank[4 + hd], 0
                    for t in range(TT):
                        v = vt[:, t, hd * P:(hd + 1) * P]
                        last = nc.tensor.matmul(o[:, t * P:(t + 1) * P], v, ad[:, hd, t * P:(t + 1) * P],
                                                start=(t == 0), stop=(t == TT - 1))
                        if t < TT - 1:
                            w = T - (t + 1) * P
                            last = nc.tensor.matmul(o[:, (t + 1) * P:T], v, ax[:, hd, at:at + w],
                                                    start=False, stop=False)
                            at += w
                    last.then_inc(S["hpv"], 1)
                group_stats(st, 4, "e128", spr)

            def group_stats(st, n, name, spread_m):
                for j in range(n):
                    pe.wait_ge(S["gsq"], st["gsq"] + j + 1)
                    nc.tensor.matmul(bank[0][0:16, :], group_m(name, j), sq[:, j % 2, :], start=(j == 0),
                                     stop=(j == n - 1)).then_inc(S["gst"], 1)
                pe.wait_ge(S["grs"], st["grs"] + 1)
                for j in range(n):
                    if j >= 2:
                        pe.wait_ge(S["gused"], st["gused"] + j - 1)
                    nc.tensor.matmul(bank[2 + j % 2][:], spread_m[:, j * P:(j + 1) * P], s1[0:16, :],
                                     start=True, stop=True).then_inc(S["gbc"], 1)

            def rotate(st, chunks):
                for j, ap in enumerate(chunks):
                    if j >= 2:
                        pe.wait_ge(S["roped"], st["roped"] + j - 1)
                    nc.tensor.matmul(bank[j % 2][:], rot_m, ap, start=True, stop=True).then_inc(S["rot"], 1)

            def nsa_prep(st):
                pe.wait_ge(S["gused"], st["gused"])
                group_stats(st, 6, "e64", spr)
                chunks = [proj[:, NQ + j, :] for j in range(4)] + [proj[:, KSL, :], proj[:, KWN, :]]

                def turn(j):
                    pe.wait_ge(S["gused"], st["gused"] + j + 1)
                    if j >= 2:
                        pe.wait_ge(S["roped"], st["roped"] + j - 1)
                    nc.tensor.matmul(bank[6 + j % 2][:], rot_m, chunks[j], start=True, stop=True).then_inc(S["rot"], 1)
                for j in range(2):
                    turn(j)
                pe.wait_ge(S["gused"], st["gused"] + 4)
                pe.wait_ge(S["cmp_v"], st["cmp_v"])
                for t in range(TT):
                    for hd in range(NH):
                        r = slice(64 * (hd % 2), 64 * (hd % 2) + 64)
                        c = t * P + 32 * (hd // 2)
                        last = nc.tensor.matmul(bank[4 + hd % 2][:, c:c + 32],
                                                proj[r, NQ + hd // 2, t * P:(t + 1) * P], kc[r, hd // 4, :],
                                                start=True, stop=True)
                last.then_inc(S["ca_p"], 1)
                for j in range(2, 6):
                    turn(j)

            def cmp_att(st):
                pe.wait_ge(S["ca_v"], st["ca_v"])
                for g in range(2):
                    for t in range(TT):
                        last = nc.tensor.transpose(bank[4 + g][:, t * P:(t + 1) * P],
                                                   sg[:, t // 2, (t % 2) * 256 + g * P:(t % 2) * 256 + (g + 1) * P], ident)
                last.then_inc(S["ca_t"], 1)

            def transposes(st, unit, src, dst_tiles, tiles):
                for t in tiles:
                    g = 4 * unit + t
                    pe.wait_ge(S["pn"], st["pn"] + g + 1)
                    if g >= 2:
                        pe.wait_ge(S["pt"], st["pt"] + g - 1)
                    for k in range(dst_tiles(t)):
                        last = nc.tensor.transpose(bank[4 + t % 2][:, k * P:(k + 1) * P], src(t, k), ident)
                    last.then_inc(S["tr"], 1)

            def scores(st, unit, q, k):
                for t in range(TT):
                    if unit:
                        pe.wait_ge(S["ex"], st["ex"] + 4 * (unit - 1) + t + 1)
                    w = (t + 1) * P
                    nc.tensor.matmul(bank[t][:, 0:w], q[:, t * P:w], k[:, 0:w], start=True, stop=False)
                    nc.tensor.matmul(bank[t][:, t * P:w], ident_b[:], causal_b[:], start=False,
                                     stop=True).then_inc(S["qk"], 1)

            def causal_cols(buf, t, k):
                at = P * (t * (t + 1) // 2)
                return buf[:, at + k * P:at + (k + 1) * P]

            def nsa(st):
                pe.wait_ge(S["roped"], st["roped"])

                def score_unit(u):
                    hd, br = u // 2, u % 2
                    scores(st, u, proj[:, HQ + hd // 2, :], proj[:, KZ[br] + 2 * (hd // 4) + hd % 2, :])

                def values_unit(u):
                    hd, br = u // 2, u % 2
                    o = bank[6 + (hd // 2) % 2][64 * (hd % 2):64 * (hd % 2) + 64, :]
                    if br == 0:
                        if hd % 2 == 0 and hd >= 4:
                            pe.wait_ge(S["oe"], st["oe"] + hd // 2 - 1)
                        r = slice(32 * (hd % 4), 32 * (hd % 4) + 32)
                        nc.tensor.matmul(o, vc[r, hd // 4, :], pct[r, hd // 4, :], start=True, stop=False)
                    pe.wait_ge(S["pt"], st["pt"] + 4 * u + 4)
                    for k in range(TT):
                        col = 128 * br + 64 * (hd // 4)
                        last = nc.tensor.matmul(o[:, k * P:T], vgt[:, k, col:col + 64], ptt[:, u % 2, k, k * P:T],
                                                start=False, stop=(br == 1 and k == TT - 1))
                    last.then_inc(S["pv"], 1)

                score_unit(0)
                for u in range(2 * NH):
                    if u + 1 < 2 * NH:
                        score_unit(u + 1)
                    if u == 0:
                        pe.wait_ge(S["ca_a"], st["ca_a"])
                    for tiles in ((0, 1), (2, 3)):
                        transposes(st, u, lambda t, k: causal_cols(pa[:, u % 2, :], t, k), lambda t: t + 1, tiles)
                        if u and tiles[0] == 0:
                            values_unit(u - 1)
                values_unit(2 * NH - 1)

            def w_out(st):
                products(st, st["slab"], st["took"], st["prod"], 4, st["xl"] - KC)

            def pg(st):
                pe.wait_ge(took_a, st["took"])
                pe.wait_ge(took_v, st["took"])
                pe.wait_ge(side_in, 16 * (3 + 3 * st["layer"]))

                def embed(j, o):
                    for k in range(2):
                        last = nc.tensor.matmul(bank[4 + 2 * (j % 2) + o][:], side[:, 2 * (2 * j + o) + k, :],
                                                pin[:, k, :], start=(k == 0), stop=(k == 1))
                    return last
                for j, o in ((1, 0), (1, 1), (0, 0), (0, 1)):
                    if (j, o) == (0, 1):
                        pe.wait_ge(S["var"], st["var"])
                    last = embed(j, o)
                for j in range(4):
                    pe.wait_ge(w_low, st["slab"] + 2 * j + 2)
                    if j >= 2:
                        pe.wait_ge(took_v, st["took"] + j - 1)
                        pe.wait_ge(took_a, st["took"] + j - 1)

                    def waits(k):
                        if j == 0:
                            pe.wait_ge(S["xl"], st["xl"] - KC + k + 1)
                    last = pair(st["slab"] + 2 * j, j % 2, xh, xl, T, waits)
                    if j >= 2:
                        for o in range(2):
                            last = embed(j, o)
                    last.then_inc(prod, 1)

            def ffn_in(st):
                products(st, st["slab"], st["took"], st["prod"], NF, st["xl"] - KC)

            def ffn_out(st):
                pe.wait_ge(took_a, st["took"])
                pe.wait_ge(took_v, st["took"])

                def one(slab, k_h, k_l, first):
                    for o in range(KC):
                        a, b = tile_of(slab, o)
                        last = passes(bank[o][:], a, b, k_h, k_l, first, False)
                    last.then_inc(prod, 1)
                for k in range(TAIL):
                    pe.wait_ge(w_low, st["slab"] + k + 1)
                    pe.wait_ge(S["hl"], st["hl"] - NF + k + 1)
                    one(st["slab"] + k, hh[:, k, :], hl[:, k, :], k == 0)
                with pe.Fori(0, (NF - 2 * TAIL) // 4) as i:
                    for n in range(TAIL, TAIL + 4):
                        pe.wait_ge(w_low, i * 4 + (st["slab"] + n + 1))
                        pe.wait_ge(S["hl"], i * 4 + (st["hl"] - NF + n + 1))
                        one(st["slab"] + n, flat(hh[:, bass.ds(i * 4 + n, 1), :]), flat(hl[:, bass.ds(i * 4 + n, 1), :]),
                            False)
                pe.wait_ge(w_low, st["slab"] + NF)
                pe.wait_ge(S["hl"], st["hl"])
                for o in range(KC):
                    for k in range(NF - TAIL, NF):
                        a, b = tile_of(st["slab"] + k, o)
                        last = passes(bank[o][:], a, b, hh[:, k, :], hl[:, k, :], False, k == NF - 1)
                    if o % 2:
                        last.then_inc(prod, 1)

            def da_project(st):
                products(st, st["slab"], st["took"], st["prod"], 8, st["xl"] - KC)
                for half in range(2):
                    token_major(st["slab"] + 16 + 4 * half, st["took"] + 8 + half, 4 - 4 * half, xh, xl, TT, T, None)

            def da_rope(st):
                pe.wait_ge(took_a, st["took"])
                pe.wait_ge(took_v, st["took"])
                pe.wait_ge(S["dp_v"], st["dp_v"])
                nc.tensor.matmul(bank[4][:, 0:2], mean_m, lam[:, 0:2], start=True, stop=True).then_inc(S["dp_p"], 1)
                rotate(st, [dq[:, j, :] for j in range(KC)] + [dk[:, j, :] for j in range(KC)])

            def da(st):
                pe.wait_ge(S["roped"], st["roped"])

                def score_unit(u):
                    hd, c = u // 2, u % 2
                    scores(st, u, dq[:, hd, :], dkz[:, c, hd, :])
                def turn(hd, tiles):
                    transposes(st, hd, lambda t, k: causal_cols(dpa[:, 1, :], t, k), lambda t: t + 1, tiles)
                for hd in range(NH):
                    score_unit(2 * hd)
                    if hd:
                        turn(hd - 1, (0, 1))
                        if hd >= 2:
                            values(hd - 2, st)
                        turn(hd - 1, (2, 3))
                    score_unit(2 * hd + 1)
                turn(NH - 1, (0, 1))
                values(NH - 2, st)
                turn(NH - 1, (2, 3))
                values(NH - 1, st)

            def values(hd, st):
                pe.wait_ge(S["pt"], st["pt"] + 4 * hd + 4)
                if hd >= 2:
                    pe.wait_ge(S["oe"], st["oe"] + hd - 1)
                for k in range(TT):
                    last = nc.tensor.matmul(bank[6 + hd % 2][:, k * P:T], dv[:, k, hd * P:(hd + 1) * P],
                                            dpt[:, hd % 2, k, k * P:T], start=(k == 0), stop=(k == TT - 1))
                last.then_inc(S["pv"], 1)

            def xa_project(st):
                products(st, st["slab"], st["took"], st["prod"], 4, st["xl"] - KC)
                pe.wait_ge(S["msplit"], st["msplit"] + 2)
                products(st, st["slab"] + 8, st["took"] + 4, st["prod"] + 4, 4, None, mh, ml, MEM)
                for half in range(2):
                    token_major(st["slab"] + 16 + 4 * half, st["took"] + 8 + half, 4 * (1 - half), mh, ml, MT, T, None)

            def xa(st):
                pe.wait_ge(took_a, st["took"])
                pe.wait_ge(took_v, st["took"])

                def score_unit(hd):
                    for t in range(TT):
                        if hd:
                            pe.wait_ge(S["ex"], st["ex"] + 4 * (hd - 1) + t + 1)
                        for k in range(2):
                            last = nc.tensor.matmul(bank[t][:, 0:MEM], xq[:, 2 * hd + k, t * P:(t + 1) * P],
                                                    xk[:, 2 * hd + k, :], start=(k == 0), stop=(k == 1))
                        last.then_inc(S["qk"], 1)
                def values_of(hd):
                    pe.wait_ge(S["pt"], st["pt"] + 4 * hd + 4)
                    if hd:
                        pe.wait_ge(S["oe"], st["oe"] + 2 * hd)
                    for c in range(2):
                        for k in range(MT):
                            last = nc.tensor.matmul(bank[6 + c][:], xv[:, k, hd * 256 + c * P:hd * 256 + (c + 1) * P],
                                                    xpt[:, hd % 2, k, :], start=(k == 0), stop=(k == 1))
                    last.then_inc(S["pv"], 1)

                score_unit(0)
                for hd in range(4):
                    if hd < 3:
                        score_unit(hd + 1)
                    for tiles in ((0, 1), (2, 3)):
                        transposes(st, hd, lambda t, k: xpa[:, hd % 2, t, k * P:(k + 1) * P], lambda t: MT, tiles)
                        if hd and tiles[0] == 0:
                            values_of(hd - 1)
                values_of(3)

            def pool_mix(st):
                pe.wait_ge(S["msplit"], st["msplit"] + 2)
                products(st, st["slab"], st["took"], st["prod"], 4, None, mh, ml, MEM)
                pe.wait_ge(side_in, 16 * 8)
                for g in range(4):
                    if g == 2:
                        pe.wait_ge(took_a, st["took"] + 4)
                        pe.wait_ge(took_v, st["took"] + 4)
                    pe.wait_ge(S["pl"], st["pl"] + 2 * g + 2)
                    for o in range(2):
                        for k in range(2):
                            last = nc.tensor.matmul(bank[(4 + 2 * g + o) % 8][:], pside[:, 4 * g + 2 * o + k, :],
                                                    pooled[:, 2 * g + k, :], start=(k == 0), stop=(k == 1))
                    last.then_inc(S["plp"], 1)
                pe.wait_ge(S["plt"], st["plt"] + 1)
                token_major(st["slab"] + 8, st["took"] + 4, 4, mh, ml, MT, T, None)

            def xa_rest(st):
                products(st, st["slab"], st["took"], st["prod"], 4, st["xl"] - KC)
                token_major(st["slab"] + 8, st["took"] + 4, 4, mh, ml, MT, T, None)

            pe.wait_ge(consts_made, 3)
            does = dict(rms=rms, ln=rms, project=project, compress=compress, hgrn=hgrn, nsa_prep=nsa_prep,
                        cmp_att=cmp_att, nsa=nsa, w_out=w_out, pg=pg, ffn_in=ffn_in, ffn_out=ffn_out,
                        da_project=da_project, da_rope=da_rope, da=da, xa_project=xa_project,
                        xa=xa, pool=pool_mix, xa_rest=xa_rest,
                        da_norm=lambda st: (pe.wait_ge(S["oe"], st["oe"]), group_stats(st, NH, "e128", dspr)))
            for st in stages:
                if st["kind"] in does:
                    does[st["kind"]](st)

        @blk.scalar
        def _(act):
            step = Steps(act, act_steps)
            table = nc.scalar.preload_act_table

            def high(n, slab=None):
                if isinstance(n, int):
                    if n >= n_slabs:
                        return
                    act.wait_ge(raw_in[n % RING], 16 * (n // RING + 1))
                    slot = n % RING
                else:
                    i, at = n
                    act.wait_ge(raw_in[at % RING], i * 16 + 16 * (at // RING + 1))
                    slot = at % RING
                nc.scalar.copy(wh[:, slot, :], raw[:, slot, :]).then_inc(w_high, 1)

            def squares(st, c):
                act.wait_ge(S["r"], st["r"] + c + 1)
                if c >= 2:
                    act.wait_ge(S["s2"], st["s2"] + c - 1)
                nc.scalar.activation(sq[:, c % 2, :], h[:, c, :], F.Square).then_inc(S["sq"], 1)

            def sumsq(st):
                for c in range(KC):
                    if c >= 2:
                        act.wait_ge(S["s2"], st["s2"] + c - 1)
                    nc.scalar.activation(sq[:, c % 2, :], h[:, c, :], F.Square).then_inc(S["sq"], 1)

            def pair_squares(st, j):
                for c in (2 * j, 2 * j + 1):
                    if c % 2:
                        act.wait_ge(took_v, st["took"] + j + 1)
                    else:
                        act.wait_ge(S["r"], st["r"] + j + 1)
                    if c >= 2:
                        act.wait_ge(S["s2"], st["s2"] + c - 1)
                    nc.scalar.activation(sq[:, c % 2, :], h[:, c, :], F.Square
                                         ).then_inc(took_a if c % 2 else S["sq"], 1)

            def norm(st):
                last_one = st["kind"] == "ln" and (st["layer"], st["which"]) == (1, 3)
                table(F.Abs_reciprocal_sqrt)
                act.wait_ge(S["stat"], st["stat"] + 1)
                if st["kind"] == "ln":
                    nc.scalar.activation(sg[:, 0, :], bank[4][:], F.Square).then_inc(S["act_stat"], 1)
                if st["before"] == "ffn_out":
                    for k in range(1, TAIL):
                        high(st["slab"] - TAIL + k + RING)
                act.wait_ge(S["var"], st["var"] + 1)
                nc.scalar.activation(sq[:, 1, :], sq[:, 0, :], F.Abs_reciprocal_sqrt).then_inc(S["act_stat"], 1)
                if st["kind"] == "ln" and (st["layer"], st["which"]) == (1, 0):
                    act.wait_ge(mem_in, 16 * 2)
                    nc.scalar.copy(mh[:], xm[:]).then_inc(S["msplit"], 1)
                for c in range(KC):
                    act.wait_ge(S["v"], st["v"] + c + 1)
                    v = tb[:, c % 2, :]
                    if st["kind"] == "rms":
                        nc.scalar.copy(xh[:, c, :], v).then_inc(S["xh"], 1)
                    else:
                        b = par(COL2, "ln_b", (st["layer"] * 4 + st["which"]) * KC + c)
                        if last_one:
                            nc.scalar.activation(h[:, c, :], v, F.Identity, bias=b).then_inc(final, 1)
                        elif (st["layer"], st["which"]) == (1, 0):
                            nc.scalar.activation(h[:, c, :], v, F.Identity, bias=b).then_inc(S["hn"], 1)
                        else:
                            nc.scalar.activation(h[:, c, :], v, F.Identity, bias=b)
                            nc.scalar.activation(xh[:, c, :], v, F.Identity, bias=b).then_inc(S["xh"], 1)

            def split_of(st, chunk):
                for c in range(KC):
                    nc.scalar.copy(xh[:, c, :], chunk(c)).then_inc(S["xh"], 1)

            def split(st):
                if st["which"] == 0:
                    act.wait_ge(S["oe"], st["oe"])
                    act.wait_ge(S["pv"], st["pv"])
                    split_of(st, lambda c: proj[:, (HGO if c < 4 else NZ - 4) + c, :])
                elif st["which"] == 1:
                    act.wait_ge(S["r"], st["r"])
                    split_of(st, lambda c: h[:, c, :])
                else:
                    act.wait_ge(S["oe"], st["oe"])
                    split_of(st, lambda c: xq[:, c, :])

            def copy_pairs(st, slab, ticket, step0, pairs, dst, w=T):
                def two(i):
                    for j in range(2):
                        act.wait_ge(prod, i * 2 + (step0 + j + 1))
                        high((i, slab + 2 * j + RING))
                        high((i, slab + 2 * j + RING + 1))
                        nc.scalar.copy(flat(dst[:, bass.ds(i * 4 + 2 * j, 1), :]), bank[2 * j][:, 0:w]
                                       ).then_inc(took_a, 1)
                with act.Fori(0, pairs // 2) as i:
                    two(i)

            def copy_tiles(slab, step0, banks, tiles, dst, w):
                for s in range(4):
                    act.wait_ge(prod, step0 + s + 1)
                    high(slab + s + RING)
                for t in range(0, tiles, 2):
                    last = nc.scalar.copy(dst[:, t, 0:w], bank[banks + t][:, 0:w])
                    if t + 2 < tiles:
                        step(last)
                last.then_inc(took_a, 1)

            def project(st):
                act.wait_ge(S["xl"], st["xl"])
                act.wait_ge(S["v"], st["v"])
                act.dma_start(w1v[:], w1[st["layer"], 1]).then_inc(side_in, 16)
                copy_tiles(st["slab"], st["prod"], 4, TT, vt[:], T)
                copy_tiles(st["slab"] + 4, st["prod"] + 4, 0, TT, vgt[:], VG)
                copy_pairs(st, st["slab"] + 8, st["took"] + 2, st["prod"] + 8, 14, proj)

            def compress(st):
                act.wait_ge(took_a, st["took"])
                act.wait_ge(took_v, st["took"])
                for g in range(2):
                    src = proj[64 * g:64 * g + 64, VCM, :]
                    nc.scalar.copy(kk_v[0:64, g, :], src).then_inc(S["cmp_a"], 1)
                    nc.scalar.copy(kk_v[64:P, g, 0:T - 1], src[:, 1:T]).then_inc(S["cmp_a"], 1)

            def hidden(st):
                done = {k: st[k] - n for k, n in COUNTS["compress"].items()}
                nc.scalar.activation(hidk[:, 0:2 * NC], bank[4][:, 0:2 * NC], F.Silu).then_inc(S["cmp_a"], 1)
                act.wait_ge(S["cmp_v"], done["cmp_v"] + 4)
                for g in range(2):
                    nc.scalar.activation(hidv[:, g, :, 0:NC],
                                         bank[5][:, NC * g:NC * g + NC].rearrange("p (o c) -> p o c", o=1)
                                         .broadcast_to([P, 4, NC]), F.Silu
                                         ).then_inc(S["cmp_a"], 1)
                for chunk in (HZ, NZ):
                    nc.scalar.activation(proj[:, chunk:chunk + 4, :], proj[:, chunk:chunk + 4, :], F.Silu
                                         ).then_inc(S["lvl_a"], 1)
                act.wait_ge(S["cmp_p"], done["cmp_p"] + 3)
                nc.scalar.activation(ksm[:, 0, 0:2 * NC], bank[6][:, 0:2 * NC], F.Square).then_inc(S["cmp_a"], 1)
                table(F.Abs_reciprocal_sqrt)
                act.wait_ge(S["cmp_v"], done["cmp_v"] + 7)
                nc.scalar.activation(ksm[:, 2, 0:2 * NC], ksm[:, 1, 0:2 * NC], F.Abs_reciprocal_sqrt
                                     ).then_inc(S["cmp_a"], 1)

            def group_rstd(st):
                table(F.Abs_reciprocal_sqrt)
                act.wait_ge(S["gvar"], st["gvar"] + 1)
                nc.scalar.activation(sg[0:16, 0, :], s2[0:16, :], F.Abs_reciprocal_sqrt).then_inc(S["gact"], 1)

            def group_squares(st, chunks):
                for j, ap in enumerate(chunks):
                    if j >= 2:
                        act.wait_ge(S["gst"], st["gst"] + j - 1)
                    nc.scalar.activation(sq[:, j % 2, :], ap, F.Square).then_inc(S["gsq"], 1)

            def hgrn(st):
                nc.scalar.activation(lbt[:, 0, :], lbt[:, 2, :], F.Sigmoid).then_inc(S["lvl_a"], 1)
                nc.scalar.activation(lbt[:, 1, :], lbt[:, 2, :], F.Sigmoid, scale=-1.0).then_inc(S["lvl_a"], 1)
                nc.scalar.activation(proj[:, HGO:HGO + 4, :], proj[:, HGO:HGO + 4, :], F.Sigmoid
                                     ).then_inc(S["lvl_a"], 1)
                act.wait_ge(S["cmp_p"], st["cmp_p"] - 3)
                nc.scalar.activation(hk[:], proj[:, HF:HF + 4, :], F.Sigmoid, scale=-1.0).then_inc(S["lvl_a"], 1)
                nc.scalar.activation(proj[:, HF:HF + 4, :], proj[:, HF:HF + 4, :], F.Sigmoid).then_inc(S["lvl_a"], 1)
                hidden(st)
                act.dma_start(side[:], pp_w[st["layer"]]).then_inc(side_in, 16)
                for hd in range(4):
                    act.wait_ge(S["lvl_p"], st["lvl_p"] + 4 * (LEVELS - 2) + hd + 1)
                    nc.scalar.copy(ax[:, hd, 0:P], bank[hd][:, 0:P]).then_inc(S["lvl_a"], 1)
                    nc.scalar.copy(ax[:, hd, 640:768], bank[hd][:, P:2 * P]).then_inc(S["lvl_a"], 1)
                for hd in range(4):
                    act.wait_ge(S["lvl_p"], st["lvl_p"] + 4 * (LEVELS - 1) + hd + 1)
                    nc.scalar.copy(ax[:, hd, P:640], bank[hd][:]).then_inc(S["lvl_a"], 1)
                for hd in range(4):
                    act.wait_ge(S["hpv"], st["hpv"] + hd + 1)
                    if hd >= 2:
                        act.wait_ge(S["gst"], st["gst"] + hd - 1)
                    nc.scalar.activation(sq[:, hd % 2, :], bank[4 + hd][:], F.Square).then_inc(S["gsq"], 1)
                act.dma_start(pin[:, 0:2, :], p_t[st["layer"]]).then_inc(side_in, 16)
                group_rstd(st)

            def nsa_prep(st):
                act.wait_ge(S["gused"], st["gused"])
                group_squares(st, [proj[:, NQ + j, :] for j in range(4)] + [proj[:, KSL, :], proj[:, KWN, :]])
                group_rstd(st)

                nc.scalar.activation(vgt[:, :, 256:280], vgt[:, :, 256:280], F.Sigmoid).then_inc(S["ca_a"], 1)
                table(F.Exp)
                act.wait_ge(S["ca_v"], st["ca_v"] + 1)
                nc.scalar.activation(sg[:], sg[:], F.Exp, scale=0.125).then_inc(S["ca_a"], 1)

            def cmp_att(st):
                act.wait_ge(S["ca_t"], st["ca_t"] + 1)
                for g in range(2):
                    nc.scalar.copy(pct[:, g, :], bank[4 + g][:]).then_inc(S["ca_a"], 1)

            def exp(st, unit, t, scale, buf, w):
                act.wait_ge(S["mx"], st["mx"] + 4 * unit + t + 1)
                nc.scalar.activation(buf, bank[t][:, 0:w], F.Exp, bias=small[:, 1, unit % 2, t:t + 1],
                                     scale=scale, accum_out=small[:, 2, unit % 2, t:t + 1]).then_inc(S["ex"], 1)

            def transposed(st, unit, t, dst, k):
                act.wait_ge(S["tr"], st["tr"] + 4 * unit + t + 1)
                nc.scalar.copy(dst, bank[4 + t % 2][:, 0:k * P].rearrange("p (k t) -> p k t", k=k)
                               ).then_inc(S["pt"], 1)

            def causal_buf(buf, t):
                at = P * (t * (t + 1) // 2)
                return buf[:, at:at + (t + 1) * P]

            def nsa(st):
                table(F.Exp)

                def one(u, t):
                    exp(st, u, t, 0.125, causal_buf(pa[:, u % 2, :], t), (t + 1) * P)
                for t in range(TT):
                    one(0, t)
                for u in range(2 * NH):
                    if 1 <= u < 2 * NH - 1:
                        act.wait_ge(S["tr"], st["tr"] + 4 * (u - 1) + 4)
                    if u >= 2:
                        act.wait_ge(S["pv"], st["pv"] + u - 1)
                    for t in range(TT):
                        if u + 1 < 2 * NH:
                            one(u + 1, t)
                        transposed(st, u, t, ptt[:, u % 2, 0:t + 1, t * P:(t + 1) * P], t + 1)

            def w_out(st):
                for j in range(4):
                    act.wait_ge(prod, st["prod"] + j + 1)
                    high(st["slab"] + 2 * j + RING)
                    high(st["slab"] + 2 * j + RING + 1)
                    pair_squares(st, j)

            def pg(st):
                table(F.Sigmoid)
                for j in range(4):
                    act.wait_ge(prod, st["prod"] + j + 1)
                    high(st["slab"] + 2 * j + RING)
                    high(st["slab"] + 2 * j + RING + 1)
                    if j:
                        act.wait_ge(took_v, st["took"] + j)
                    step(nc.scalar.activation(sg[:, 0, :], bank[2 * (j % 2)][:], F.Sigmoid))
                    nc.scalar.activation(sg[:, 1, :], bank[2 * (j % 2) + 1][:], F.Sigmoid).then_inc(took_a, 1)
                    squares(st, 2 * j)
                    squares(st, 2 * j + 1)
                if st["layer"] == 0:
                    act.dma_start(side[:], w1[1, 0]).then_inc(w1k_in, 16)
                else:
                    act.dma_start(prm[:, 0:NPRM2], prm2).then_inc(side_in, 16)

            def ffn_in(st):
                table(F.Silu)

                def two(i):
                    for j in range(2):
                        act.wait_ge(prod, i * 2 + (st["prod"] + j + 1))
                        nc.scalar.activation(sg[:, j, :], bank[2 * j][:], F.Silu).then_inc(took_a, 1)
                        high((i, st["slab"] + 2 * j + RING))
                        high((i, st["slab"] + 2 * j + RING + 1))
                        act.wait_ge(took_v, i * 2 + (st["took"] + j + 1))
                        nc.scalar.copy(flat(hh[:, bass.ds(i * 2 + j, 1), :]), tb[:, j, :]).then_inc(S["hh"], 1)
                with act.Fori(0, NF // 2) as i:
                    two(i)

            def ffn_out(st):
                with act.Fori(0, (NF - 2 * TAIL) // 4) as i:
                    for n in range(4):
                        act.wait_ge(prod, i * 4 + (st["prod"] + n + 1))
                        high((i, st["slab"] + n + RING))
                for k in range(NF - 2 * TAIL, NF - TAIL):
                    act.wait_ge(prod, st["prod"] + k + 1)
                    high(st["slab"] + k + RING)
                for j in range(4):
                    act.wait_ge(prod, st["prod"] + NF - TAIL + j + 1)
                    pair_squares(st, j)
                high(st["slab"] + NF - TAIL + RING)

            def da_prep(st):
                act.dma_start(dspr[:], spread).then_inc(block2_in, 16)
                act.dma_start(rot_m, rot2).then_inc(block2_in, 16)
                act.dma_start(dpos[:], positions.broadcast_to([P, T])).then_inc(block2_in, 16)
                table(F.Sin)
                act.wait_ge(S["dp_v"], st["dp_v"] + 2)
                nc.scalar.activation(drop[:, 1, :], tb[:, 0, :], F.Sin).then_inc(S["dp_a"], 1)
                act.wait_ge(S["dp_v"], st["dp_v"] + 3)
                nc.scalar.activation(drop[:, 0, :], tb[:, 1, :], F.Sin).then_inc(S["dp_a"], 1)

            def da_project(st):
                copy_pairs(st, st["slab"], st["took"], st["prod"], 4, dq)
                copy_pairs(st, st["slab"] + 8, st["took"] + 4, st["prod"] + 4, 4, dk)
                for half in range(2):
                    copy_tiles(st["slab"] + 16 + 4 * half, st["prod"] + 8 + 4 * half, 4 - 4 * half, TT,
                               dv[:, :, 512 * half:512 * half + 512], T)

            def da(st):
                table(F.Exp)
                act.wait_ge(S["dp_p"], st["dp_p"])
                nc.scalar.activation(lam[:, 0:2], bank[4][:, 0:2], F.Exp, scale=float(D)).then_inc(S["dp_a"], 1)

                def one(u, t):
                    exp(st, u, t, 0.125, causal_buf(dpa[:, 1 if u % 2 else u // 2 % 2 * 2, :], t), (t + 1) * P)

                def out_head(hd):
                    act.wait_ge(S["pv"], st["pv"] + hd + 1)
                    nc.scalar.copy(dq[:, hd, :], bank[6 + hd % 2][:]).then_inc(S["oe"], 1)

                def turn(hd, t):
                    transposed(st, hd, t, dpt[:, hd % 2, 0:t + 1, t * P:(t + 1) * P], t + 1)
                for hd in range(NH):
                    if hd >= 2:
                        act.wait_ge(S["pn"], st["pn"] + 4 * (hd - 1))
                    if hd >= 3:
                        act.wait_ge(S["pv"], st["pv"] + hd - 2)
                    for t in range(TT):
                        one(2 * hd, t)
                        if hd:
                            turn(hd - 1, t)
                    for t in range(TT):
                        one(2 * hd + 1, t)
                    if hd >= 2:
                        out_head(hd - 2)
                for t in range(TT):
                    turn(NH - 1, t)
                out_head(NH - 2)
                out_head(NH - 1)

            def da_norm(st):
                act.wait_ge(S["oe"], st["oe"])
                group_squares(st, [dq[:, j, :] for j in range(NH)])
                group_rstd(st)
                for c in range(KC):
                    act.wait_ge(S["gused"], st["gused"] + c + 1)
                    nc.scalar.copy(xh[:, c, :], dq[:, c, :]).then_inc(S["xh"], 1)

            def xa_project(st):
                act.wait_ge(mem_in, 16 * (st["layer"] + 1))
                nc.scalar.copy(mh[:], xm[:]).then_inc(S["msplit"], 1)
                copy_pairs(st, st["slab"], st["took"], st["prod"], 4, xq)
                copy_pairs(st, st["slab"] + 8, st["took"] + 4, st["prod"] + 4, 4, xk, MEM)
                for half in range(2):
                    copy_tiles(st["slab"] + 16 + 4 * half, st["prod"] + 8 + 4 * half, 4 * (1 - half), MT,
                               xv[:, :, 512 * half:512 * half + 512], T)

            def xa(st):
                table(F.Exp)

                def one(u, t):
                    exp(st, u, t, 1.0 / 16, xpa[:, u % 2, t, :], MEM)
                for t in range(TT):
                    one(0, t)
                for u in range(4):
                    if 1 <= u < 3:
                        act.wait_ge(S["tr"], st["tr"] + 4 * (u - 1) + 4)
                    if u >= 2:
                        act.wait_ge(S["pv"], st["pv"] + u - 1)
                    for t in range(TT):
                        if u + 1 < 4:
                            one(u + 1, t)
                        transposed(st, u, t, xpt[:, u % 2, :, t * P:(t + 1) * P], MT)

            def pool_mix(st):
                with act.Fori(0, 2) as i:
                    for j in range(2):
                        act.wait_ge(prod, i * 2 + (st["prod"] + j + 1))
                        high((i, st["slab"] + 2 * j + RING))
                        high((i, st["slab"] + 2 * j + RING + 1))
                        for o in range(2):
                            nc.scalar.copy(flat(xk[:, bass.ds(i * 4 + 2 * j + o, 1), :]), bank[2 * j + o][:, 0:MEM]
                                           ).then_inc(took_v if o else took_a, 1)
                for c in range(KC - 2):
                    squares(st, c)
                for n in range(4):
                    act.wait_ge(prod, st["prod"] + 4 + n + 1)
                    high(st["slab"] + 8 + n + RING)
                for t in range(MT):
                    nc.scalar.copy(xv[:, t, 0:T], bank[4 + t][:]).then_inc(took_v if t else took_a, 1)
                for c in range(KC - 2, KC):
                    squares(st, c)

            def xa_rest(st):
                copy_pairs(st, st["slab"], st["took"], st["prod"], 4, xq)
                copy_tiles(st["slab"] + 8, st["prod"] + 4, 4, MT, xv[:, :, T:2 * T], T)

            act.wait_ge(loaded, 16 * 4)
            for n in range(RING):
                high(n)
            act.wait_ge(consts_made, 3)
            does = dict(sumsq=sumsq, rms=norm, ln=norm, split=split, project=project, compress=compress, hgrn=hgrn,
                        nsa_prep=nsa_prep, cmp_att=cmp_att, nsa=nsa, w_out=w_out, pg=pg, ffn_in=ffn_in,
                        ffn_out=ffn_out, da_prep=da_prep, da_project=da_project, da=da, da_norm=da_norm,
                        xa_project=xa_project, xa=xa, pool=pool_mix, xa_rest=xa_rest)
            for st in stages:
                if st["kind"] in does:
                    if st["kind"] == "ln" and (st["layer"], st["which"]) == (1, 0):
                        act.dma_start(xm[:], mem_t).then_inc(mem_in, 16)
                        act.dma_start(pside[:], pool_w).then_inc(side_in, 16)
                    if st["kind"] == "ln" and (st["layer"], st["which"]) == (0, 1):
                        act.wait_ge(S["s2"], st["s2"])
                        act.dma_start(xm[:], mem_t).then_inc(mem_in, 16)
                    does[st["kind"]](st)

        @blk.vector
        def _(dve):
            step = Steps(dve, dve_steps)
            V = nc.vector

            def newton(y, var, tmp, dst):
                step(V.scalar_tensor_tensor(out=tmp, in0=y, scalar=-0.5, in1=y, op0=A.mult, op1=A.mult))
                step(V.tensor_tensor(tmp, tmp, var, A.mult))
                return V.scalar_tensor_tensor(out=dst, in0=tmp, scalar=1.5, in1=y, op0=A.add, op1=A.mult)

            def clear_sums(ln):
                step(V.memset(s2[:], 0.0))
                if ln:
                    step(V.memset(s1[:], 0.0))

            def add_squares(st, c, sem_, value):
                dve.wait_ge(sem_, value)
                if c < KC - 2:
                    V.tensor_tensor(s2[:], s2[:], sq[:, c % 2, :], A.add).then_inc(S["s2"], 1)
                    dve.wait_ge(S["s2"], st["s2"] + c + 1)

            def sumsq(st):
                clear_sums(False)
                for c in range(KC):
                    add_squares(st, c, S["sq"], st["sq"] + c + 1)

            def lower(st, c, src):
                dve.wait_ge(S["xh"], st["xh"] + c + 1)
                V.tensor_tensor(xl[:, c, :], src, xh[:, c, :], A.subtract).then_inc(S["xl"], 1)
                dve.wait_ge(S["xl"], st["xl"] + c + 1)

            def norm(st):
                ln = st["kind"] == "ln"
                last_one = ln and (st["layer"], st["which"]) == (1, 3)
                unsplit = ln and (st["layer"], st["which"]) == (1, 0)
                var, y = sq[:, 0, :], sq[:, 1, :]
                if ln:
                    if (st["layer"], st["which"]) == (0, 0):
                        dve.wait_ge(side_in, 16 * 7)
                    eps = LN_EPS * (4 if st["which"] in (0, 3) else 1)
                    dve.wait_ge(S["act_stat"], st["act_stat"] + 1)
                    step(V.tensor_copy(s1[:], bank[4][:]))
                    dve.wait_ge(S["stat"], st["stat"] + 2)
                    step(V.tensor_tensor(var, bank[5][:], sg[:, 0, :], A.subtract))
                    V.tensor_scalar(var, var, 0.0, eps, A.max, A.add).then_inc(S["var"], 1)
                    step(V.tensor_tensor(sg[:, 0, :], h[:, 0, :], s1[:], A.subtract))
                    dve.wait_ge(S["act_stat"], st["act_stat"] + 2)
                else:
                    dve.wait_ge(S["stat"], st["stat"] + 1)
                    V.tensor_scalar(var, bank[5][:], RMS_EPS, None, A.add).then_inc(S["var"], 1)
                    dve.wait_ge(S["act_stat"], st["act_stat"] + 1)
                dve.wait_ge(S["var"], st["var"] + 1)
                step(newton(y, var, sg[:, 1, :], s2[:]))
                for c in range(KC):
                    if ln:
                        g = par(COL2, "ln_g", (st["layer"] * 4 + st["which"]) * KC + c)
                        if c:
                            step(V.tensor_tensor(sg[:, c % 2, :], h[:, c, :], s1[:], A.subtract))
                        if c >= 2:
                            dve.wait_ge(*((final, c - 1) if last_one else (S["hn"], st["hn"] + c - 1) if unsplit
                                          else (S["xh"], st["xh"] + c - 1)))
                        src = sg[:, c % 2, :]
                    else:
                        g = par(COL1, "norm_g" if st["which"] == 0 else "ple_g", st["layer"] * KC + c)
                        src = h[:, c, :]
                        if c >= 2:
                            dve.wait_ge(S["xl"], st["xl"] + c - 1)
                    V.scalar_tensor_tensor(out=tb[:, c % 2, :], in0=src, scalar=g, in1=s2[:], op0=A.mult,
                                           op1=A.mult).then_inc(S["v"], 1)
                dve.wait_ge(S["v"], st["v"] + KC)
                if unsplit:
                    dve.wait_ge(S["hn"], st["hn"] + KC)
                elif not last_one:
                    dve.wait_ge(S["xl"], st["xl"] + KC)

            def split(st):
                for c in range(KC):
                    lower(st, c, (proj[:, (HGO if c < 4 else NZ - 4) + c, :], h[:, c, :], xq[:, c, :])[st["which"]])

            def copy_pairs(step0, pairs, dst, w=T):
                with dve.Fori(0, pairs // 2) as i:
                    for j in range(2):
                        dve.wait_ge(prod, i * 2 + (step0 + j + 1))
                        V.tensor_copy(flat(dst[:, bass.ds(i * 4 + 2 * j + 1, 1), :]), bank[2 * j + 1][:, 0:w]
                                      ).then_inc(took_v, 1)

            def copy_tiles(step0, banks, tiles, dst, w):
                dve.wait_ge(prod, step0 + 4)
                for t in range(1, tiles, 2):
                    last = V.tensor_copy(dst[:, t, 0:w], bank[banks + t][:, 0:w])
                    if t + 2 < tiles:
                        step(last)
                last.then_inc(took_v, 1)

            def project(st):
                copy_tiles(st["prod"], 4, TT, vt[:], T)
                copy_tiles(st["prod"] + 4, 0, TT, vgt[:], VG)
                copy_pairs(st["prod"] + 8, 14, proj)

            def compress(st):
                dve.wait_ge(took_a, st["took"])
                dve.wait_ge(took_v, st["took"])
                step(V.memset(hidv[:], 0.0))
                step(V.memset(kc[:], 0.0))
                for g in range(2):
                    src = proj[64 * g:64 * g + 64, KCM, :]
                    V.tensor_copy(kk_k[0:64, g, :], src).then_inc(S["cmp_v"], 1)
                    V.tensor_copy(kk_k[64:P, g, 0:T - 1], src[:, 1:T]).then_inc(S["cmp_v"], 1)
                for b, (kk, x) in enumerate(((kk_k, blocks_k), (kk_v, blocks_v))):
                    if b:
                        dve.wait_ge(S["cmp_a"], st["cmp_a"] + 4)
                    else:
                        dve.wait_ge(S["cmp_v"], st["cmp_v"] + 4)
                    for half in range(2):
                        i0 = 8 * half
                        tok = kk.rearrange("p g (c i r) -> p i g c r", i=8, r=2)[:, :, :, half:half + NC, 0]
                        pe_col = par(COL1, "pe", (st["layer"] * 2 + b) * 16 + i0, 8).rearrange(
                            "p (i a o) -> p i a o", a=1, o=1).broadcast_to([P, 8, 2, NC])
                        ins = V.tensor_tensor(x[:, i0:i0 + 8, :].rearrange("p i (g c) -> p i g c", g=2), tok, pe_col,
                                              A.add)
                        if half:
                            ins.then_inc(S["cmp_v"], 1)
                        else:
                            step(ins)

            def compressed(st, part):
                done = {k: st[k] - n for k, n in COUNTS["compress"].items()}
                n = 2 * NC
                if part == 0:
                    dve.wait_ge(S["cmp_p"], done["cmp_p"] + 4)
                    step(V.tensor_copy(vc[:].rearrange("p g d -> p (g d)"), bank[7][:, 0:P]))
                elif part == 1:
                    dve.wait_ge(S["cmp_p"], done["cmp_p"] + 5)
                    V.tensor_scalar(ksm[:, 1, 0:n], bank[4][:, 0:n], RMS_EPS, None, A.add).then_inc(S["cmp_v"], 1)
                else:
                    dve.wait_ge(S["cmp_v"], done["cmp_v"] + 7)
                    dve.wait_ge(S["cmp_a"], done["cmp_a"] + 9)
                    step(newton(ksm[:, 2, 0:n], ksm[:, 1, 0:n], ksm[:, 0, 0:n], ksm[:, 0, 0:n]))
                    V.scalar_tensor_tensor(out=kc[:, :, 0:NC], in0=bank[6][:, 0:n].rearrange("p (g c) -> p g c", g=2),
                                           scalar=par(COL1, "kn", st["layer"] * 3),
                                           in1=ksm[:, 0, 0:n].rearrange("p (g c) -> p g c", g=2), op0=A.mult,
                                           op1=A.mult).then_inc(S["cmp_v"], 1)

            def group_rstd(st, n, eps):
                dve.wait_ge(S["gst"], st["gst"] + n)
                V.tensor_scalar(s2[0:16, :], bank[0][0:16, :], eps, None, A.add).then_inc(S["gvar"], 1)
                dve.wait_ge(S["gvar"], st["gvar"] + 1)
                dve.wait_ge(S["gact"], st["gact"] + 1)
                newton(sg[0:16, 0, :], s2[0:16, :], sg[0:16, 1, :], s1[0:16, :]).then_inc(S["grs"], 1)

            def hgrn(st):
                dve.wait_ge(S["lvl_a"], st["lvl_a"] + LA - 2)
                for lv in range(LEVELS):
                    if lv in (4, 6, 7):
                        compressed(st, (4, 6, 7).index(lv))
                    for hd in range(4):
                        q, k, f = proj[:, HQ + hd, :], hk[:, hd, :], proj[:, HF + hd, :]
                        if lv == 0:
                            if st["layer"]:
                                step(V.tensor_scalar(f, f, lbt[:, 1, hd:hd + 1], lbt[:, 0, hd:hd + 1], A.mult, A.add))
                                step(V.tensor_scalar(k, k, lbt[:, 1, hd:hd + 1], None, A.mult))
                            V.memset(ad[:, hd, :], 0.0).then_inc(S["lvl_v"], 1)
                            continue
                        dve.wait_ge(S["lvl_v"], st["lvl_v"] + 4 * (lv - 1) + hd + 1)
                        dve.wait_ge(S["lvl_p"], st["lvl_p"] + 4 * (lv - 1) + hd + 1)
                        if lv - 1 < LEVELS - 2:
                            V.copy_predicated(ad[:, hd, :].rearrange("p (t s) -> p t s", t=TT),
                                                   msk[:, lv - 1, :].rearrange("p (o s) -> p o s", o=1)
                                                   .broadcast_to([P, TT, P]),
                                                   bank[hd][:].rearrange("p (t s) -> p t s", t=TT))
                        if lv == 1:
                            V.tensor_tensor(q, q, f, A.mult).then_inc(S["lvl_v"], 1)
                            continue
                        tot, even, odd, qv, kv = level(lv, hd)
                        last = V.tensor_tensor(qv, qv, cat(even, qv.shape[2]), A.mult)
                        if lv < LEVELS - 1:
                            if lv > 2:
                                dve.wait_ge(S["lvl_k"], st["lvl_k"] + 4 * (lv - 3) + hd + 1)
                            new = (tot_b if lv % 2 else tot_a)[:, hd, 0:even.shape[1]]
                            last = V.tensor_tensor(new, even, odd, A.mult)
                        last.then_inc(S["lvl_v"], 1)
                dve.wait_ge(S["lvl_a"], st["lvl_a"] + LA)
                group_rstd(st, 4, RMS_EPS)
                for hd in range(4):
                    dve.wait_ge(S["gbc"], st["gbc"] + hd + 1)
                    y = tb[:, hd % 2, :]
                    step(V.scalar_tensor_tensor(out=y, in0=bank[4 + hd][:], scalar=par(COL1, "onorm", st["layer"]),
                                                in1=proj[:, HGO + hd, :], op0=A.mult, op1=A.mult))
                    step(V.tensor_tensor(y, y, bank[2 + hd % 2][:], A.mult))
                    V.tensor_tensor(proj[:, HGO + hd, :], y, proj[:, HZ + hd, :], A.mult).then_inc(S["gused"], 1)

            def nsa_prep(st):
                dve.wait_ge(S["gused"], st["gused"])
                group_rstd(st, 6, RMS_EPS)
                chunks = [NQ + j for j in range(4)] + [KSL, KWN]
                for j, c in enumerate(chunks):
                    dve.wait_ge(S["gbc"], st["gbc"] + j + 1)
                    g = par(COL1, "qn", st["layer"]) if j < 4 else par(COL1, "kn", st["layer"] * 3 + j - 3)
                    V.scalar_tensor_tensor(out=proj[:, c, :], in0=proj[:, c, :], scalar=g, in1=bank[2 + j % 2][:],
                                           op0=A.mult, op1=A.mult).then_inc(S["gused"], 1)
                dve.wait_ge(S["gused"], st["gused"] + 6)
                s = sg[:].rearrange("p a (t h c) -> p (a t) h c", t=2, h=NH)
                flat_s = sg[:].rearrange("p a (t c) -> p (a t) c", c=32)
                mx, den = ksm[:, 0, 0:TT * NH], ksm[:, 1, 0:TT * NH]

                def seen(i, n=NH):
                    return cmt[:, i, :, :].rearrange("p t (o c) -> p t o c", o=1).broadcast_to([P, TT, n, 32])

                def turn(j):
                    dve.wait_ge(S["rot"], st["rot"] + j + 1)
                    m, x = tb[:, j % 2, :], sq[:, j % 2, :]
                    step(V.tensor_tensor(m, bank[6 + j % 2][:], rop[:, 1, :], A.mult))
                    dve.wait_ge(S["xcos"], st["xcos"] + j + 1)
                    if j < 4:
                        V.tensor_tensor(proj[:, HQ + j, :], x, m, A.add).then_inc(S["roped"], 1)
                        return
                    dve.wait_ge(S["zeroed"], st["zeroed"] + 4)
                    for g in range(2):
                        src = slice(64 * g, 64 * g + 64)
                        for half in range(2):
                            last = V.tensor_tensor(proj[64 * half:64 * half + 64, KZ[j - 4] + 2 * g + half, :],
                                                   x[src, :], m[src, :], A.add)
                            if g + half < 2:
                                step(last)
                    last.then_inc(S["roped"], 1)

                turn(0)
                turn(1)
                dve.wait_ge(S["ca_p"], st["ca_p"] + 1)
                for o in range(2):
                    step(V.tensor_tensor(s[:, :, o:NH:2, :], bank[4 + o][:].rearrange("p (t h c) -> p t h c", t=TT, h=4),
                                         seen(1, 4), A.add))
                step(V.tensor_reduce(mx, flat_s, AX, A.max))
                V.tensor_tensor(flat_s, flat_s, cat(mx, 32), A.subtract).then_inc(S["ca_v"], 1)
                turn(2)
                turn(3)
                dve.wait_ge(S["ca_a"], st["ca_a"] + 2)
                step(V.tensor_tensor(s, s, seen(0), A.mult))
                step(V.tensor_reduce(den, flat_s, AX, A.add))
                step(V.tensor_scalar(den, den, 1e-30, None, A.max))
                step(V.reciprocal(den, den))
                step(V.tensor_tensor(den.rearrange("p (t h) -> p t h", t=TT), den.rearrange("p (t h) -> p t h", t=TT),
                                     vgt[:, :, 256:264], A.mult))
                V.tensor_tensor(flat_s, flat_s, cat(den, 32), A.mult).then_inc(S["ca_v"], 1)
                turn(4)
                turn(5)
                dve.wait_ge(S["roped"], st["roped"] + 6)

            def maxima(st, u, scale, w, tiles=range(TT)):
                for t in tiles:
                    dve.wait_ge(S["qk"], st["qk"] + 4 * u + t + 1)
                    step(V.tensor_reduce(small[:, 0, u % 2, t:t + 1], bank[t][:, 0:w(t)], AX, A.max))
                    V.tensor_scalar(small[:, 1, u % 2, t:t + 1], small[:, 0, u % 2, t:t + 1], -scale, None, A.mult
                                    ).then_inc(S["mx"], 1)

            def causal_buf(buf, t):
                at = P * (t * (t + 1) // 2)
                return buf[:, at:at + (t + 1) * P]

            def nsa(st):
                def out_pair(j):
                    dve.wait_ge(S["pv"], st["pv"] + 4 * j + 4)
                    V.tensor_tensor(proj[:, NZ + j, :], bank[6 + j % 2][:], proj[:, NZ + j, :], A.mult
                                    ).then_inc(S["oe"], 1)
                def some_maxima(u, tiles):
                    if u < 2 * NH:
                        maxima(st, u, 0.125, lambda t: (t + 1) * P, tiles)

                some_maxima(0, range(TT))
                for u in range(2 * NH):
                    hd, br = u // 2, u % 2
                    some_maxima(u + 1, range(2))
                    dve.wait_ge(S["ex"], st["ex"] + 4 * u + 4)
                    rw = small[:, 3, u % 2, :]
                    step(V.reciprocal(rw, small[:, 2, u % 2, :]))
                    step(V.tensor_tensor(rw, rw, vgt[:, :, 264 + 8 * br + hd:265 + 8 * br + hd]
                                         .rearrange("p t o -> p (t o)"), A.mult))
                    for t in range(TT):
                        b = causal_buf(pa[:, u % 2, :], t)
                        V.tensor_scalar(b, b, rw[:, t:t + 1], None, A.mult).then_inc(S["pn"], 1)
                    some_maxima(u + 1, range(2, TT))
                    if u >= 6 and (u - 6) % 4 == 0:
                        out_pair((u - 6) // 4)
                out_pair(3)

            def residual(st, j, a, banks, ln):
                for o in range(2):
                    c = 2 * j + o
                    ins = V.scalar_tensor_tensor(out=h[:, c, :], in0=h[:, c, :], scalar=a, in1=bank[banks + o][:],
                                                 op0=A.mult, op1=A.add)
                    if o:
                        ins.then_inc(took_v, 1)
                        dve.wait_ge(took_v, st["took"] + j + 1)
                    else:
                        ins.then_inc(S["r"], 1)
                        dve.wait_ge(S["r"], st["r"] + j + 1)
                if j == 3:
                    return
                if ln:
                    for o in range(2):
                        step(V.tensor_tensor(s1[:], s1[:], h[:, 2 * j + o, :], A.add))
                add_squares(st, 2 * j, S["sq"], st["sq"] + j + 1)
                add_squares(st, 2 * j + 1, took_a, st["took"] + j + 1)

            def w_out(st):
                ln = st["which"] > 0
                clear_sums(ln)
                for j in range(4):
                    dve.wait_ge(prod, st["prod"] + j + 1)
                    residual(st, j, ALPHA if ln else 1.0, 2 * (j % 2), ln)

            def ffn_out(st):
                clear_sums(True)
                for j in range(4):
                    dve.wait_ge(prod, st["prod"] + NF - TAIL + j + 1)
                    residual(st, j, 2 * ALPHA, 2 * j, True)

            def pg(st):
                clear_sums(False)
                for j in range(4):
                    dve.wait_ge(took_a, st["took"] + j + 1)
                    step(V.tensor_tensor(tb[:, 0, :], sg[:, 0, :], bank[4 + 2 * (j % 2)][:], A.mult))
                    V.tensor_tensor(tb[:, 1, :], sg[:, 1, :], bank[5 + 2 * (j % 2)][:], A.mult).then_inc(took_v, 1)
                    dve.wait_ge(took_v, st["took"] + j + 1)
                    for o in range(2):
                        c = 2 * j + o
                        V.tensor_tensor(h[:, c, :], h[:, c, :], tb[:, o, :], A.add).then_inc(S["r"], 1)
                    for o in range(2):
                        add_squares(st, 2 * j + o, S["sq"], st["sq"] + 2 * j + o + 1)

            def ffn_in(st):
                with dve.Fori(0, NF // 2) as i:
                    for j in range(2):
                        dve.wait_ge(took_a, i * 2 + (st["took"] + j + 1))
                        V.tensor_tensor(tb[:, j, :], sg[:, j, :], bank[2 * j + 1][:], A.mult).then_inc(took_v, 1)
                        dve.wait_ge(S["hh"], i * 2 + (st["hh"] + j + 1))
                        V.tensor_tensor(flat(hl[:, bass.ds(i * 2 + j, 1), :]), tb[:, j, :],
                                        flat(hh[:, bass.ds(i * 2 + j, 1), :]), A.subtract).then_inc(S["hl"], 1)

            def da_prep(st):
                V.tensor_tensor(lam[:, 0:2], par(COL2, "lam_q", 0, 2), par(COL2, "lam_k", 0, 2), A.mult
                                ).then_inc(S["dp_v"], 1)
                step(V.tensor_scalar(par(COL2, "subln"), par(COL2, "subln"), 1.0 - LAM_INIT, None, A.mult))
                dve.wait_ge(block2_in, 16 * 3)
                ang, k, r = sg[:, 0, :], sg[:, 1, :], tb[:, 0, :]
                step(V.tensor_copy(ang, dpos[:]))
                step(V.tensor_scalar(ang, ang, par(COL2, "inv"), None, A.mult))
                step(V.tensor_scalar(k, ang, float(1 / (2 * np.pi)), None, A.mult))
                step(V.tensor_scalar(k, k, ROUND, None, A.add))
                step(V.tensor_scalar(k, k, ROUND, None, A.subtract))
                parts = (6.28125, 0.0019340515136718750, 2 * np.pi - 6.28125 - 0.0019340515136718750)
                src = ang
                for p in parts:
                    step(V.scalar_tensor_tensor(out=r, in0=k, scalar=-float(p), in1=src, op0=A.mult, op1=A.add))
                    src = r
                r2 = tb[:, 1, :]
                step(V.tensor_scalar(r2, r, float(np.pi / 2), None, A.add))
                step(V.tensor_scalar(k, r2, float(np.pi), None, A.is_gt))
                step(V.scalar_tensor_tensor(out=r2, in0=k, scalar=-float(2 * np.pi), in1=r2, op0=A.mult, op1=A.add))
                V.tensor_scalar(r, r, PI, -PI, A.min, A.max).then_inc(S["dp_v"], 1)
                V.tensor_scalar(r2, r2, PI, -PI, A.min, A.max).then_inc(S["dp_v"], 1)
                dve.wait_ge(S["dp_a"], st["dp_a"] + 2)

            def da_project(st):
                copy_pairs(st["prod"], 4, dq)
                copy_pairs(st["prod"] + 4, 4, dk)
                for half in range(2):
                    copy_tiles(st["prod"] + 8 + 4 * half, 4 - 4 * half, TT, dv[:, :, 512 * half:512 * half + 512], T)

            def da_rope(st):
                dve.wait_ge(took_a, st["took"])
                dve.wait_ge(took_v, st["took"])
                dve.wait_ge(S["zeroed"], st["zeroed"])
                for j in range(2 * KC):
                    dve.wait_ge(S["rot"], st["rot"] + j + 1)
                    m, x = tb[:, j % 2, :], sq[:, j % 2, :]
                    step(V.tensor_tensor(m, bank[j % 2][:], drop[:, 1, :], A.mult))
                    dve.wait_ge(S["xcos"], st["xcos"] + j + 1)
                    if j < KC:
                        V.tensor_tensor(dq[:, j, :], x, m, A.add).then_inc(S["roped"], 1)
                    else:
                        step(V.tensor_tensor(dkz[0:64, 0, j - KC, :], x[0:64, :], m[0:64, :], A.add))
                        V.tensor_tensor(dkz[64:P, 1, j - KC, :], x[64:P, :], m[64:P, :], A.add
                                        ).then_inc(S["roped"], 1)
                dve.wait_ge(S["roped"], st["roped"] + 2 * KC)

            def da(st):
                def maximum(u, t):
                    maxima(st, u, 0.125, lambda t: (t + 1) * P, (t,))

                for hd in range(NH):
                    if hd == 0:
                        maxima(st, 0, 0.125, lambda t: (t + 1) * P)
                        dve.wait_ge(S["dp_a"], st["dp_a"])
                        step(V.tensor_tensor(lam[:, 2:3], lam[:, 1:2], lam[:, 0:1], A.subtract))
                        step(V.tensor_scalar(lam[:, 2:3], lam[:, 2:3], LAM_INIT, None, A.subtract))
                    for t in range(TT):
                        maximum(2 * hd + 1, t)
                        dve.wait_ge(S["ex"], st["ex"] + 8 * hd + t + 1)
                        step(V.reciprocal(small[:, 3, 0, t:t + 1], small[:, 2, 0, t:t + 1]))
                        p0 = causal_buf(dpa[:, hd % 2 * 2, :], t)
                        last = V.tensor_scalar(p0, p0, small[:, 3, 0, t:t + 1], None, A.mult)
                    step(last)
                    for t in range(TT):
                        dve.wait_ge(S["ex"], st["ex"] + 8 * hd + 4 + t + 1)
                        step(V.reciprocal(small[:, 3, 1, t:t + 1], small[:, 2, 1, t:t + 1]))
                        step(V.tensor_scalar(small[:, 3, 1, t:t + 1], small[:, 3, 1, t:t + 1], lam[:, 2:3], None, A.mult))
                        p0, p1 = causal_buf(dpa[:, hd % 2 * 2, :], t), causal_buf(dpa[:, 1, :], t)
                        V.scalar_tensor_tensor(out=p1, in0=p1, scalar=small[:, 3, 1, t:t + 1], in1=p0, op0=A.mult,
                                               op1=A.add).then_inc(S["pn"], 1)
                        if hd < NH - 1:
                            maximum(2 * hd + 2, t)

            def da_norm(st):
                dve.wait_ge(S["oe"], st["oe"])
                group_rstd(st, NH, LN_EPS)
                for j in range(NH):
                    dve.wait_ge(S["gbc"], st["gbc"] + j + 1)
                    V.scalar_tensor_tensor(out=dq[:, j, :], in0=dq[:, j, :], scalar=par(COL2, "subln"),
                                           in1=bank[2 + j % 2][:], op0=A.mult, op1=A.mult).then_inc(S["gused"], 1)
                    if j:
                        lower(st, j - 1, dq[:, j - 1, :])
                lower(st, NH - 1, dq[:, NH - 1, :])

            def xa_project(st):
                dve.wait_ge(S["msplit"], st["msplit"] + 1)
                V.tensor_tensor(ml[:], xm[:], mh[:], A.subtract).then_inc(S["msplit"], 1)
                copy_pairs(st["prod"], 4, xq)
                copy_pairs(st["prod"] + 4, 4, xk, MEM)
                for half in range(2):
                    copy_tiles(st["prod"] + 8 + 4 * half, 4 * (1 - half), MT, xv[:, :, 512 * half:512 * half + 512], T)

            def xa_rest(st):
                copy_pairs(st["prod"], 4, xq)
                copy_tiles(st["prod"] + 4, 4, MT, xv[:, :, T:2 * T], T)

            def xa(st):
                def out_head(hd):
                    dve.wait_ge(S["pv"], st["pv"] + hd + 1)
                    for c in range(2):
                        V.tensor_copy(xq[:, 2 * hd + c, :], bank[6 + c][:]).then_inc(S["oe"], 1)
                for u in range(4):
                    maxima(st, u, 1.0 / 16, lambda t: MEM)
                    dve.wait_ge(S["ex"], st["ex"] + 4 * u + 4)
                    rw = small[:, 3, u % 2, :]
                    step(V.reciprocal(rw, small[:, 2, u % 2, :]))
                    for t in range(TT):
                        b = xpa[:, u % 2, t, :]
                        V.tensor_scalar(b, b, rw[:, t:t + 1], None, A.mult).then_inc(S["pn"], 1)
                    if u >= 2:
                        out_head(u - 2)
                out_head(2)
                out_head(3)

            def pool_mix(st):
                clear_sums(True)
                for c in range(KC):
                    g = c // 2
                    src, x = h[:, c, :], h[:, c, :]
                    for k in range(g + 1):
                        s = 2 ** k
                        dst = tb[:, k % 2, :]
                        step(V.tensor_tensor(dst[:, s:T], src[:, s:T], src[:, 0:T - s], A.add))
                        step(V.tensor_copy(dst[:, 0:s], src[:, 0:s]))
                        src = dst
                    step(V.scalar_tensor_tensor(out=pooled[:, c, :], in0=src, scalar=1.0 / 2 ** (g + 1), in1=x,
                                                op0=A.mult, op1=A.subtract))
                    step(V.tensor_tensor(sg[:, 0, 0:16], src[:, 0:16], par(COL2, "cnt", 16 * g, 16), A.mult))
                    V.tensor_tensor(pooled[:, c, 0:16], sg[:, 0, 0:16], x[:, 0:16], A.subtract).then_inc(S["pl"], 1)
                dve.wait_ge(S["pl"], st["pl"] + KC)
                for g in range(4):
                    dve.wait_ge(S["plp"], st["plp"] + g + 1)
                    for o in range(2):
                        c = 2 * g + o
                        ins = V.tensor_scalar(tb[:, o, :], bank[(4 + 2 * g + o) % 8][:], par(COL2, "pool_b", c),
                                              par(COL2, "pool_s", c), A.add, A.mult)
                        if o:
                            ins.then_inc(S["plt"], 1)
                            dve.wait_ge(S["plt"], st["plt"] + g + 1)
                        else:
                            step(ins)
                    for o in range(2):
                        c = 2 * g + o
                        V.scalar_tensor_tensor(out=h[:, c, :], in0=h[:, c, :], scalar=ALPHA, in1=tb[:, o, :],
                                               op0=A.mult, op1=A.add).then_inc(S["r"], 1)
                        dve.wait_ge(S["r"], st["r"] + c + 1)
                        if g < 3:
                            step(V.tensor_tensor(s1[:], s1[:], h[:, c, :], A.add))
                    for o in range(2):
                        add_squares(st, 2 * g + o, S["sq"], st["sq"] + 2 * g + o + 1)

            dve.wait_ge(loaded, 16 * 4)
            V.tensor_copy(causal_b[:], tb[:, 0, 0:P]).then_inc(consts_made, 1)
            V.tensor_copy(ident_b[:], ident).then_inc(consts_made, 1)
            V.tensor_tensor(lbt[:, 2, :], par(COL1, "lb", 4, 4), par(COL1, "lb", 0, 4), A.subtract
                            ).then_inc(consts_made, 1)
            does = dict(sumsq=sumsq, rms=norm, ln=norm, split=split, project=project, compress=compress, hgrn=hgrn,
                        nsa_prep=nsa_prep, nsa=nsa, w_out=w_out, pg=pg, ffn_in=ffn_in,
                        ffn_out=ffn_out, da_prep=da_prep, da_project=da_project, da_rope=da_rope, da=da,
                        da_norm=da_norm, xa_project=xa_project, xa=xa, pool=pool_mix, xa_rest=xa_rest)
            for st in stages:
                if st["kind"] in does:
                    does[st["kind"]](st)


def shape_constants():
    eye = np.eye(P, dtype=np.float32)
    group = np.arange(P) // 64
    e64, e128 = np.zeros((P, 32), np.float32), np.zeros((P, 32), np.float32)
    e64[:, 14], e64[:, 15] = (group == 0) / 64, (group == 1) / 64
    e128[:, 14:16] = 1 / 128
    block = (group[:, None] == group[None, :]).astype(np.float32) / 64

    def rotation(half, width):
        r = np.zeros((P, P), np.float32)
        for m in range(P):
            d = m % 64
            if d < half:
                r[m + half, m] = -1
            elif d < width:
                r[m - half, m] = 1
        return r
    consts = np.concatenate([np.full((P, P), 1 / D, np.float32), eye, block, e64, e128, rotation(8, 16)], 1)
    inv = np.float32(500000.0) ** (-np.arange(0, 16, 2, dtype=np.float32) / np.float32(16))
    ang = np.arange(T, dtype=np.float32)[None, :] * inv[:, None].astype(np.float32)
    rope = np.zeros((P, 2, T), np.float32)
    rope[:, 0] = 1
    for m in range(P):
        if m % 64 < 16:
            rope[m, 0], rope[m, 1] = np.cos(ang[m % 8]), np.sin(ang[m % 8])
    s, t = np.arange(P)[:, None], np.arange(P)[None, :]
    masks = [s == t] + [(s // (2 * m) == t // (2 * m)) & (s % (2 * m) < m) & (t % (2 * m) >= m)
                        for m in (1, 2, 4, 8, 16, 32, 64)]
    masks = np.stack(masks, 1).astype(np.int32)
    tok = np.arange(TT)[None, :, None] * P + np.arange(P)[:, None, None]
    seen = (np.arange(32)[None, None, :] * 16 + 31 <= tok)
    cmp_tab = np.stack([seen.astype(np.float32), np.where(seen, 0, NEG).astype(np.float32)], 1)
    spread = np.zeros((16, 8, P), np.float32)
    for j in range(8):
        spread[2 * j, j, 0:64] = 1
        spread[2 * j + 1, j, 64:P] = 1
    causal = np.where(t <= s, 0, NEG).astype(np.float32)
    inv2 = (1.0 / (np.float32(10000.0) ** (np.arange(0, 64, 2, dtype=np.float32) / np.float32(64)))).astype(np.float32)
    cnt = np.stack([1.0 / np.minimum(np.arange(16) + 1, 2 ** (g + 1)) for g in range(4)]).astype(np.float32)
    return dict(consts=consts, rope=rope, masks=masks, cmp_tab=cmp_tab, spread=spread.reshape(16, 8 * P),
                causal=causal, rot2=rotation(32, 64), inv=inv2[np.arange(P) % 32][:, None],
                cnt=np.tile(cnt.reshape(1, 64), (P, 1)))


def weight_slabs(w_in, w_out, w_pg, ffn_w_in, ffn_w_out, da_w_qkv, da_w_o, xa_wq, xa_wkv, xa_wo):
    slabs = []

    def chunk(w, c0):
        slabs.append(w[:, c0:c0 + P].reshape(KC, P, P).transpose(1, 0, 2).reshape(P, D))

    def tokens(w):
        for q in range(4):
            slabs.append(w[256 * q:256 * q + 256].reshape(2, P, 512).transpose(1, 0, 2).reshape(P, D))

    def ffn(l, i):
        for f in range(NF):
            chunk(ffn_w_in[l, i], f * P)
            chunk(ffn_w_in[l, i], NF * P + f * P)
        for f in range(NF):
            slabs.append(ffn_w_out[l, i, f * P:(f + 1) * P])

    for l in range(DEPTH):
        w = w_in[l]
        tokens(w[:, 1024:1536])
        tokens(np.concatenate([w[:, 3456:3584], w[:, 3712:3840], w[:, 3840:3864],
                               np.zeros((D, 512 - VG), w.dtype)], 1))
        starts = [0, 512, 1536, 2048, 2560, 3864]
        for s in starts:
            for c in range(4):
                chunk(w, s + c * P)
        for s in (3072, 3200, 3328, 3584):
            chunk(w, s)
        for c in range(KC):
            chunk(w_out[l], c * P)
        for c in range(KC):
            chunk(w_pg[l], c * P)
    for l in range(DEPTH):
        ffn(l, 0)
        if l == 0:
            for c in range(2 * KC):
                chunk(da_w_qkv[0], c * P)
            for half in range(2):
                tokens(da_w_qkv[0][:, 2 * D + 512 * half:2 * D + 512 * half + 512])
            for c in range(KC):
                chunk(da_w_o[0], c * P)
        def queries():
            for c in range(KC):
                chunk(xa_wq[l], c * P)

        def memory(half=None):
            if half is None:
                for c in range(KC):
                    chunk(xa_wkv[l], c * P)
            else:
                tokens(xa_wkv[l][:, D + 512 * half:D + 512 * half + 512])
        if l == 0:
            queries()
            memory()
            memory(0)
            memory(1)
        else:
            memory()
            memory(0)
            queries()
            memory(1)
        for c in range(KC):
            chunk(xa_wo[l], c * P)
        ffn(l, 1)
    return np.ascontiguousarray(np.stack(slabs))


def by_chunk(v):
    return np.ascontiguousarray(v.reshape(-1, P).T)


def kernel(x, p, norm_g, w_in, hgrn_lb, hgrn_onorm_g, nsa_qnorm_g, nsa_knorm_g, cmp_pe, cmp_w1, cmp_w2,
           w_out, ple_norm_g, w_pg, w_pp, mem_2, positions_2, ffn_w_in_2, ffn_w_out_2, ln_g_2, ln_b_2,
           da_w_qkv_2, da_w_o_2, da_lam_q_2, da_lam_k_2, da_subln_g_2, pool_w_2, pool_b_2, pool_scale_2,
           ret_w_qkvg_2, ret_w_o_2, xa_wq_2, xa_wkv_2, xa_wo_2):
    import concourse.bacc as bacc
    from concourse.bass_utils import run_bass_kernel_spmd

    (x, p, norm_g, w_in, hgrn_lb, hgrn_onorm_g, nsa_qnorm_g, nsa_knorm_g, cmp_pe, cmp_w1, cmp_w2, w_out, ple_norm_g,
     w_pg, w_pp, mem_2, positions_2, ffn_w_in_2, ffn_w_out_2, ln_g_2, ln_b_2, da_w_qkv_2, da_w_o_2, da_lam_q_2,
     da_lam_k_2, da_subln_g_2, pool_w_2, pool_b_2, pool_scale_2, xa_wq_2, xa_wkv_2, xa_wo_2) = (
        np.asarray(a) for a in (
            x, p, norm_g, w_in, hgrn_lb, hgrn_onorm_g, nsa_qnorm_g, nsa_knorm_g, cmp_pe, cmp_w1, cmp_w2, w_out,
            ple_norm_g, w_pg, w_pp, mem_2, positions_2, ffn_w_in_2, ffn_w_out_2, ln_g_2, ln_b_2, da_w_qkv_2, da_w_o_2,
            da_lam_q_2, da_lam_k_2, da_subln_g_2, pool_w_2, pool_b_2, pool_scale_2, xa_wq_2, xa_wkv_2, xa_wo_2))
    const = shape_constants()

    def twice(v):
        return np.concatenate([v.T, v.T], 0)

    def padded(v):
        return np.concatenate([v.T, np.zeros((64, v.shape[0]), v.dtype)], 0)
    prm1 = np.concatenate([
        by_chunk(norm_g), by_chunk(ple_norm_g), by_chunk(hgrn_onorm_g), twice(nsa_qnorm_g),
        twice(nsa_knorm_g.reshape(-1, 64)), by_chunk(hgrn_lb), by_chunk(cmp_pe),
        cmp_w2[:, 0].transpose(1, 0, 2).reshape(P, -1), cmp_w2[:, 1].transpose(1, 0, 2).reshape(P, -1)], 1)
    prm2 = np.concatenate([
        by_chunk(ln_g_2), by_chunk(ln_b_2), by_chunk(da_subln_g_2), by_chunk(pool_b_2), by_chunk(pool_scale_2),
        padded(da_lam_q_2[0]), padded(da_lam_k_2[0]), const["inv"], const["cnt"]], 1)
    arrays = dict(
        x_t=x[0].T,
        slabs=weight_slabs(w_in, w_out, w_pg, ffn_w_in_2, ffn_w_out_2, da_w_qkv_2, da_w_o_2, xa_wq_2, xa_wkv_2,
                           xa_wo_2),
        prm1=prm1, prm2=prm2, consts=const["consts"], rot2=const["rot2"], rope=const["rope"],
        masks=const["masks"], cmp_tab=const["cmp_tab"], spread=const["spread"], causal=const["causal"],
        w1=cmp_w1.reshape(DEPTH, 2, 16, P, P).transpose(0, 1, 3, 2, 4),
        pp_w=w_pp.reshape(DEPTH, 2, P, KC, P).transpose(0, 2, 3, 1, 4).reshape(DEPTH, P, 16, P),
        p_t=p[:, 0].reshape(DEPTH, T, 2, P).transpose(0, 3, 2, 1),
        pool_w=pool_w_2[0].reshape(4, 2, P, 2, P).transpose(2, 0, 3, 1, 4).reshape(P, 16, P),
        mem_t=mem_2[0].reshape(MEM, KC, P).transpose(2, 1, 0),
        positions=positions_2)
    arrays = {"in_" + k: np.ascontiguousarray(v) for k, v in arrays.items()}
    nc = bacc.Bacc("TRN2", target_bir_lowering=False, num_devices=1)
    args = {k[3:]: nc.dram_tensor(k, a.shape, mybir.dt.from_np(a.dtype), kind="ExternalInput").ap()
            for k, a in arrays.items()}
    out = nc.dram_tensor("out", (D, T), mybir.dt.float32, kind="ExternalOutput").ap()
    program(nc, out=out, **args)
    r = run_bass_kernel_spmd(nc, [arrays], core_ids=[0])
    return np.ascontiguousarray(r.results[0]["out"].T)[None]
```
